# Optimizing a Trainium2 kernel written in Bass

```python
import math
import jax
import jax.numpy as jnp
from jax import lax
import numpy as np

D_MODEL = 1024
BATCH = 1
SEQ = 1024
DEPTH = 1
DEC_BATCH = 8
DEC_SEQ = 1
PAST_LEN = 2048
PAGE_SIZE = 128

NSA_HEADS = 8
NSA_KV_HEADS = 2
NSA_GROUP = NSA_HEADS // NSA_KV_HEADS
HEAD_DIM = 64
ROPE_DIM = HEAD_DIM // 4
ROPE_THETA = 500000.0
CMP_BLOCK = 32
CMP_STRIDE = 16
SEL_BLOCK = 64
SEL_TOPN = 16
WINDOW = 512
Q_BLOCK = 128
FORCE_BONUS = 1000.0
N_NSA_ROWS = 4
DN_HEADS = 4
DN_HEAD_DIM = 128
DN_WIDTH = DN_HEADS * DN_HEAD_DIM
DN_CONV = 4
DN_CHUNK = 64
N_GROUPS = 4
EXPERTS_PER_GROUP = 8
N_EXPERTS = N_GROUPS * EXPERTS_PER_GROUP
TOP_K = 2
D_EXPERT = 512
MOE_BLOCK = 128
EPS = 1e-6

NSA_Q_COLS = NSA_HEADS * HEAD_DIM
NSA_KV_COLS = NSA_KV_HEADS * HEAD_DIM
SPLIT_SIZES = (NSA_Q_COLS,) + (NSA_KV_COLS,) * 6 + (NSA_HEADS * 3, 3 * DN_WIDTH, DN_HEADS, DN_HEADS, DN_WIDTH, D_MODEL, D_MODEL)
IN_COLS = sum(SPLIT_SIZES)

kernel_name = 'hybrid_nsa_gdn_hmoe_step'

def rmsnorm(x, g):
    xf = x.astype(jnp.float32)
    xf = xf * lax.rsqrt(jnp.mean(xf * xf, axis=-1, keepdims=True) + EPS)
    return xf.astype(x.dtype) * g

def l2norm(x):
    xf = x.astype(jnp.float32)
    return xf * lax.rsqrt(jnp.sum(xf * xf, axis=-1, keepdims=True) + EPS)

def rope_partial(x, pos):
    half = ROPE_DIM // 2
    inv_freq = ROPE_THETA ** (-jnp.arange(half, dtype=jnp.float32) / half)
    ang = pos.astype(jnp.float32)[:, None] * inv_freq[None, :]
    cos = jnp.cos(ang)[:, None, :].astype(x.dtype)
    sin = jnp.sin(ang)[:, None, :].astype(x.dtype)
    x1, x2, rest = x[..., :half], x[..., half:ROPE_DIM], x[..., ROPE_DIM:]
    return jnp.concatenate([x1 * cos - x2 * sin, x2 * cos + x1 * sin, rest], axis=-1)

def masked_softmax(s, mask):
    s = jnp.where(mask, s.astype(jnp.float32), jnp.finfo(jnp.float32).min)
    return jnp.where(mask, jax.nn.softmax(s, axis=-1), 0.0)

def split_projection(h, w_in):
    offs = np.cumsum(SPLIT_SIZES)[:-1].tolist()
    return jnp.split(h @ w_in, offs, axis=-1)

def nsa_rows(q_raw, kc_raw, vc_raw, ks_raw, vs_raw, kw_raw, vw_raw, gate_raw, pos, q_norm, k_norm):
    B, T, _ = q_raw.shape
    kv_shape = (B, T, NSA_KV_HEADS, HEAD_DIM)
    q = rope_partial(rmsnorm(q_raw.reshape(B, T, NSA_HEADS, HEAD_DIM), q_norm), pos) * (HEAD_DIM ** -0.5)
    q = q.reshape(B, T, NSA_KV_HEADS, NSA_GROUP, HEAD_DIM).transpose(0, 2, 3, 1, 4)
    gates = jax.nn.sigmoid(gate_raw).reshape(B, T, NSA_KV_HEADS, NSA_GROUP, 3).transpose(0, 2, 3, 1, 4)
    ks = rope_partial(rmsnorm(ks_raw.reshape(kv_shape), k_norm[0]), pos)
    kw = rope_partial(rmsnorm(kw_raw.reshape(kv_shape), k_norm[1]), pos)
    rows = jnp.stack([kc_raw.reshape(kv_shape), vc_raw.reshape(kv_shape), ks, vs_raw.reshape(kv_shape)], axis=2)
    win = jnp.stack([kw, vw_raw.reshape(kv_shape)], axis=2)
    return q, gates, rows, win

def compress_blocks(k_raw, v_raw, cmp_pos, w_cmp, k_gain):
    L = k_raw.shape[1]
    n_cmp = (L - CMP_BLOCK) // CMP_STRIDE + 1
    starts = jnp.arange(n_cmp) * CMP_STRIDE
    idx = starts[:, None] + jnp.arange(CMP_BLOCK)[None, :]
    kb = k_raw[:, idx] + cmp_pos[0][None, None, :, None, :]
    vb = v_raw[:, idx] + cmp_pos[1][None, None, :, None, :]
    kc = jnp.einsum('bnlgd,lde->bnge', kb, w_cmp[0])
    vc = jnp.einsum('bnlgd,lde->bnge', vb, w_cmp[1])
    pos_c = starts + CMP_BLOCK - 1
    kc = rope_partial(rmsnorm(kc, k_gain), pos_c)
    return kc.transpose(0, 2, 1, 3), vc.transpose(0, 2, 1, 3), pos_c

def to_sel_blocks(rows):
    B, L, G, dk = rows.shape
    n_sel = -(-L // SEL_BLOCK)
    rows = jnp.pad(rows, ((0, 0), (0, n_sel * SEL_BLOCK - L), (0, 0), (0, 0)))
    return rows.reshape(B, n_sel, SEL_BLOCK, G, dk).transpose(0, 3, 1, 2, 4)

def cmp_sel_overlap(n_cmp, n_sel):
    cs = jnp.arange(n_cmp) * CMP_STRIDE
    ss = jnp.arange(n_sel) * SEL_BLOCK
    ov = (cs[:, None] <= ss[None, :] + SEL_BLOCK - 1) & (cs[:, None] + CMP_BLOCK - 1 >= ss[None, :])
    return ov.astype(jnp.float32)

def nsa_core(q, pos_q, gates, kc, vc, pos_c, ks_blk, vs_blk, kw, vw, pos_w, ovl):
    B, G, R, Tq, dk = q.shape
    p_c = masked_softmax(jnp.einsum('bgrqd,bgnd->bgrqn', q, kc), pos_c[None, :] <= pos_q[:, None])
    o_c = jnp.einsum('bgrqn,bgnd->bgrqd', p_c.astype(vc.dtype), vc)
    n_sel = ks_blk.shape[2]
    imp = jnp.einsum('bgrqn,ns->bgqs', p_c, ovl)
    blk = jnp.arange(n_sel)[None, :]
    cur = (pos_q // SEL_BLOCK)[:, None]
    readable = blk * SEL_BLOCK <= pos_q[:, None]
    forced = (blk == 0) | (blk == cur) | (blk == cur - 1)
    score = jnp.where(readable, imp + FORCE_BONUS * forced.astype(jnp.float32), -jnp.inf)
    top_s, top_i = lax.top_k(score, min(SEL_TOPN, n_sel))
    b_ix = jnp.arange(B)[:, None, None, None]
    g_ix = jnp.arange(G)[None, :, None, None]
    k_sel = ks_blk[b_ix, g_ix, top_i].reshape(B, G, Tq, -1, dk)
    v_sel = vs_blk[b_ix, g_ix, top_i].reshape(B, G, Tq, -1, dk)
    pos_s = top_i[..., None] * SEL_BLOCK + jnp.arange(SEL_BLOCK)
    m_s = jnp.isfinite(top_s)[..., None] & (pos_s <= pos_q[None, None, :, None, None])
    p_s = masked_softmax(jnp.einsum('bgrqd,bgqkd->bgrqk', q, k_sel), m_s.reshape(B, G, 1, Tq, -1))
    o_s = jnp.einsum('bgrqk,bgqkd->bgrqd', p_s.astype(v_sel.dtype), v_sel)
    dpos = pos_q[:, None] - pos_w[None, :]
    m_w = (dpos >= 0) & (dpos < WINDOW) & (pos_w[None, :] >= 0)
    p_w = masked_softmax(jnp.einsum('bgrqd,bgkd->bgrqk', q, kw), m_w)
    o_w = jnp.einsum('bgrqk,bgkd->bgrqd', p_w.astype(vw.dtype), vw)
    return gates[..., 0:1] * o_c + gates[..., 1:2] * o_s + gates[..., 2:3] * o_w

def nsa_prompt(q, gates, rows, win, cmp_pos, w_cmp, k_norm):
    B, G, R, T, dk = q.shape
    kc, vc, pos_c = compress_blocks(rows[:, :, 0], rows[:, :, 1], cmp_pos, w_cmp, k_norm[2])
    ks_blk = to_sel_blocks(rows[:, :, 2])
    vs_blk = to_sel_blocks(rows[:, :, 3])
    ovl = cmp_sel_overlap(kc.shape[2], ks_blk.shape[2])
    win_pad = jnp.pad(win, ((0, 0), (WINDOW, 0), (0, 0), (0, 0), (0, 0))).transpose(0, 2, 3, 1, 4)

    def block(i):
        s = i * Q_BLOCK
        pos_q = s + jnp.arange(Q_BLOCK)
        qb = lax.dynamic_slice_in_dim(q, s, Q_BLOCK, axis=3)
        gb = lax.dynamic_slice_in_dim(gates, s, Q_BLOCK, axis=3)
        wb = lax.dynamic_slice_in_dim(win_pad, s, WINDOW + Q_BLOCK, axis=3)
        pos_w = s - WINDOW + jnp.arange(WINDOW + Q_BLOCK)
        return nsa_core(qb, pos_q, gb, kc, vc, pos_c, ks_blk, vs_blk, wb[:, 0], wb[:, 1], pos_w, ovl)

    o = lax.map(block, jnp.arange(T // Q_BLOCK))
    return o.transpose(1, 0, 4, 2, 3, 5).reshape(B, T, G * R * dk)

def nsa_sample(q, gates, rows_new, win_new, cache_pool, page_table, win_buf, cmp_pos, w_cmp, k_norm):
    B, G, R, Tn, dk = q.shape
    past_len = page_table.shape[1] * cache_pool.shape[1]
    past = cache_pool[page_table].reshape(B, past_len, N_NSA_ROWS, G, dk)
    rows = jnp.concatenate([past, rows_new], axis=1)
    kc, vc, pos_c = compress_blocks(rows[:, :, 0], rows[:, :, 1], cmp_pos, w_cmp, k_norm[2])
    ks_blk = to_sel_blocks(rows[:, :, 2])
    vs_blk = to_sel_blocks(rows[:, :, 3])
    ovl = cmp_sel_overlap(kc.shape[2], ks_blk.shape[2])
    win_rows = win_buf.shape[1]
    win_all = jnp.concatenate([win_buf, win_new], axis=1)
    wt = win_all.transpose(0, 2, 3, 1, 4)
    pos_w = past_len - win_rows + jnp.arange(win_rows + Tn)
    pos_q = past_len + jnp.arange(Tn)
    o = nsa_core(q, pos_q, gates, kc, vc, pos_c, ks_blk, vs_blk, wt[:, 0], wt[:, 1], pos_w, ovl)
    return o.transpose(0, 3, 1, 2, 4).reshape(B, Tn, G * R * dk), win_all[:, -win_rows:]

def gated_delta_rule(q, k, v, g, beta, S0):
    B, T, H, dk = k.shape
    dv = v.shape[-1]
    C = min(DN_CHUNK, T)
    n = -(-T // C)
    pad = n * C - T

    def chunks(a):
        a = jnp.pad(a, ((0, 0), (0, pad)) + ((0, 0),) * (a.ndim - 2))
        return jnp.moveaxis(a.reshape((B, n, C) + a.shape[2:]), 3, 1)

    q, k, v, g, beta = (chunks(a) for a in (q, k, v, g, beta))
    Gc = jnp.cumsum(g, axis=-1)
    i = jnp.arange(C)
    incl = i[:, None] >= i[None, :]
    strict = i[:, None] > i[None, :]
    diff = Gc[..., :, None] - Gc[..., None, :]
    dmask = jnp.where(incl, jnp.exp(jnp.where(incl, diff, 0.0)), 0.0)
    kb = k * beta[..., None]
    A = jnp.where(strict, jnp.einsum('bhncd,bhnsd->bhncs', kb, k) * dmask, 0.0) + jnp.eye(C, dtype=k.dtype)
    u = lax.linalg.triangular_solve(A, v * beta[..., None], left_side=True, lower=True, unit_diagonal=True)
    w = lax.linalg.triangular_solve(A, kb * jnp.exp(Gc)[..., None], left_side=True, lower=True, unit_diagonal=True)
    qk = jnp.einsum('bhncd,bhnsd->bhncs', q, k) * dmask
    qg = q * jnp.exp(Gc)[..., None]
    g_last = Gc[..., -1]
    kd = k * jnp.exp(g_last[..., None] - Gc)[..., None]

    def step(S, xs):
        u_c, w_c, qg_c, qk_c, kd_c, gl_c = xs
        v_new = u_c - jnp.einsum('bhcd,bhde->bhce', w_c, S)
        o_c = jnp.einsum('bhcd,bhde->bhce', qg_c, S) + jnp.einsum('bhcs,bhse->bhce', qk_c, v_new)
        S = S * jnp.exp(gl_c)[..., None, None] + jnp.einsum('bhcd,bhce->bhde', kd_c, v_new)
        return S, o_c

    xs = tuple(jnp.moveaxis(a, 2, 0) for a in (u, w, qg, qk, kd, g_last))
    S, o = lax.scan(step, S0, xs)
    o = jnp.moveaxis(o, 0, 2).reshape(B, H, n * C, dv)[:, :, :T]
    return o.transpose(0, 2, 1, 3), S

def deltanet(qkv_raw, a_raw, b_raw, z_raw, conv_buf, S0, conv_w, A_log, dt_bias, dn_norm):
    B, T, _ = qkv_raw.shape
    xpad = jnp.concatenate([conv_buf.astype(qkv_raw.dtype), qkv_raw], axis=1)
    conv = xpad[:, 0:T] * conv_w[0]
    for j in range(1, DN_CONV):
        conv = conv + xpad[:, j:j + T] * conv_w[j]
    new_buf = xpad[:, T:]
    q, k, v = jnp.split(jax.nn.silu(conv), 3, axis=-1)
    shp = (B, T, DN_HEADS, DN_HEAD_DIM)
    q = l2norm(q.reshape(shp)) * (DN_HEAD_DIM ** -0.5)
    k = l2norm(k.reshape(shp))
    v = v.reshape(shp).astype(jnp.float32)
    beta = jax.nn.sigmoid(b_raw.astype(jnp.float32))
    g = -jnp.exp(A_log.astype(jnp.float32)) * jax.nn.softplus(a_raw.astype(jnp.float32) + dt_bias.astype(jnp.float32))
    o, S = gated_delta_rule(q, k, v, g, beta, S0.astype(jnp.float32))
    o = rmsnorm(o.astype(qkv_raw.dtype), dn_norm) * jax.nn.silu(z_raw.reshape(shp))
    return o.reshape(B, T, DN_WIDTH), new_buf, S.astype(S0.dtype)

def hier_moe(h, w_rg, b_rg, w_re, b_re, w_gate, w_up, w_down):
    M, D = h.shape
    p_grp = jax.nn.softmax((h @ w_rg).astype(jnp.float32) + b_rg.astype(jnp.float32), axis=-1)
    grp = jnp.argmax(p_grp, axis=-1)
    p_top = jnp.take_along_axis(p_grp, grp[:, None], axis=-1)
    logit_e = ((h @ w_re).astype(jnp.float32) + b_re.astype(jnp.float32)).reshape(M, N_GROUPS, EXPERTS_PER_GROUP)
    logit_in = jnp.take_along_axis(logit_e, grp[:, None, None], axis=1)[:, 0]
    top_v, top_i = lax.top_k(logit_in, TOP_K)
    weights = (p_top * jax.nn.softmax(top_v, axis=-1)).astype(h.dtype)
    expert = grp[:, None] * EXPERTS_PER_GROUP + top_i
    n_assign = M * TOP_K
    flat_e = expert.reshape(n_assign)
    order = jnp.argsort(flat_e)
    s_e = flat_e[order]
    s_tok = order // TOP_K
    s_w = weights.reshape(n_assign)[order]
    counts = jnp.zeros((N_EXPERTS,), jnp.int32).at[flat_e].add(1)
    padded = (counts + MOE_BLOCK - 1) // MOE_BLOCK * MOE_BLOCK
    pad_end = jnp.cumsum(padded)
    pad_start = pad_end - padded
    start = jnp.cumsum(counts) - counts
    dest = pad_start[s_e] + jnp.arange(n_assign) - start[s_e]
    n_blocks = (n_assign + N_EXPERTS * (MOE_BLOCK - 1) + MOE_BLOCK - 1) // MOE_BLOCK
    rows = jnp.zeros((n_blocks * MOE_BLOCK, D), h.dtype).at[dest].set(h[s_tok])
    blk_expert = jnp.minimum(jnp.searchsorted(pad_end, jnp.arange(n_blocks) * MOE_BLOCK, side='right'), N_EXPERTS - 1)

    def expert_block(args):
        xb, e = args
        return (jax.nn.silu(xb @ w_gate[e]) * (xb @ w_up[e])) @ w_down[e]

    out = lax.map(expert_block, (rows.reshape(n_blocks, MOE_BLOCK, D), blk_expert)).reshape(-1, D)
    return jnp.zeros((M, D), h.dtype).at[s_tok].add(out[dest] * s_w[:, None])

def merge_and_ffn(x, o_a, o_b, gate_a, gate_b, w_proj_a, w_proj_b, w_out, norm_ffn, w_rg, b_rg, w_re, b_re, w_gate, w_up, w_down):
    mixed = jax.nn.sigmoid(gate_a) * (o_a @ w_proj_a) + jax.nn.sigmoid(gate_b) * (o_b @ w_proj_b)
    x = x + mixed @ w_out
    B, T, D = x.shape
    y = hier_moe(rmsnorm(x, norm_ffn).reshape(B * T, D), w_rg, b_rg, w_re, b_re, w_gate, w_up, w_down)
    return x + y.reshape(B, T, D)

def setup_inputs(seed: int = 0) -> dict:
    key = jax.random.key(seed)
    ks = jax.random.split(key, 32)
    f32 = jnp.float32
    n_pages = PAST_LEN // PAGE_SIZE
    n_used = DEC_BATCH * n_pages
    n_pool = n_used + max(1, n_used // 4)
    win_rows = min(WINDOW, PAST_LEN)

    def nrm(k, shape, scale=1.0):
        return jax.random.normal(k, shape, f32) * scale

    page_table = jax.random.permutation(ks[3], n_pool)[:n_used].reshape(DEC_BATCH, n_pages).astype(jnp.int32)
    dt = jnp.exp(jax.random.uniform(ks[15], (DEPTH, DN_HEADS), f32, math.log(1e-3), math.log(1e-1)))
    return {
        'x_prompt': nrm(ks[0], (BATCH, SEQ, D_MODEL)),
        'x_sample': nrm(ks[1], (DEC_BATCH, DEC_SEQ, D_MODEL)),
        'cache_nsa': nrm(ks[2], (DEPTH, n_pool, PAGE_SIZE, N_NSA_ROWS, NSA_KV_HEADS, HEAD_DIM)),
        'page_table': page_table,
        'state_win': nrm(ks[4], (DEPTH, DEC_BATCH, win_rows, 2, NSA_KV_HEADS, HEAD_DIM)),
        'state_dn_conv': nrm(ks[5], (DEPTH, DEC_BATCH, DN_CONV - 1, 3 * DN_WIDTH)),
        'state_dn_S': nrm(ks[6], (DEPTH, DEC_BATCH, DN_HEADS, DN_HEAD_DIM, DN_HEAD_DIM), 0.1),
        'norm_mix': 1.0 + nrm(ks[7], (DEPTH, D_MODEL), 0.05),
        'w_in': nrm(ks[8], (DEPTH, D_MODEL, IN_COLS), D_MODEL ** -0.5),
        'q_norm': 1.0 + nrm(ks[9], (DEPTH, HEAD_DIM), 0.05),
        'k_norm': 1.0 + nrm(ks[10], (DEPTH, 3, HEAD_DIM), 0.05),
        'cmp_pos': nrm(ks[11], (DEPTH, 2, CMP_BLOCK, HEAD_DIM), 0.5),
        'w_cmp': nrm(ks[12], (DEPTH, 2, CMP_BLOCK, HEAD_DIM, HEAD_DIM), (CMP_BLOCK * HEAD_DIM) ** -0.5),
        'dn_conv_w': nrm(ks[13], (DEPTH, DN_CONV, 3 * DN_WIDTH), DN_CONV ** -0.5),
        'dn_A_log': jnp.log(jax.random.uniform(ks[14], (DEPTH, DN_HEADS), f32, 1.0, 16.0)),
        'dn_dt_bias': dt + jnp.log(-jnp.expm1(-dt)),
        'dn_norm': 1.0 + nrm(ks[16], (DEPTH, DN_HEAD_DIM), 0.05),
        'w_proj_a': nrm(ks[17], (DEPTH, NSA_Q_COLS, D_MODEL), NSA_Q_COLS ** -0.5),
        'w_proj_b': nrm(ks[18], (DEPTH, DN_WIDTH, D_MODEL), DN_WIDTH ** -0.5),
        'w_out': nrm(ks[19], (DEPTH, D_MODEL, D_MODEL), D_MODEL ** -0.5),
        'norm_ffn': 1.0 + nrm(ks[20], (DEPTH, D_MODEL), 0.05),
        'w_router_g': nrm(ks[21], (DEPTH, D_MODEL, N_GROUPS), D_MODEL ** -0.5),
        'b_router_g': nrm(ks[22], (DEPTH, N_GROUPS), 0.01),
        'w_router_e': nrm(ks[23], (DEPTH, D_MODEL, N_EXPERTS), D_MODEL ** -0.5),
        'b_router_e': nrm(ks[24], (DEPTH, N_EXPERTS), 0.01),
        'w_gate': nrm(ks[25], (DEPTH, N_EXPERTS, D_MODEL, D_EXPERT), D_MODEL ** -0.5),
        'w_up': nrm(ks[26], (DEPTH, N_EXPERTS, D_MODEL, D_EXPERT), D_MODEL ** -0.5),
        'w_down': nrm(ks[27], (DEPTH, N_EXPERTS, D_EXPERT, D_MODEL), D_EXPERT ** -0.5),
    }

def reference(x_prompt, x_sample, cache_nsa, page_table, state_win, state_dn_conv, state_dn_S,
              norm_mix, w_in, q_norm, k_norm, cmp_pos, w_cmp, dn_conv_w, dn_A_log, dn_dt_bias, dn_norm,
              w_proj_a, w_proj_b, w_out, norm_ffn, w_router_g, b_router_g, w_router_e, b_router_e,
              w_gate, w_up, w_down):
    B, T, _ = x_prompt.shape
    Bd, Tn, _ = x_sample.shape
    past_len = page_table.shape[1] * cache_nsa.shape[2]
    win_rows = state_win.shape[2]
    pos_p = jnp.arange(T)
    pos_d = past_len + jnp.arange(Tn)
    xp, xd = x_prompt, x_sample
    kv_p, kv_d, win_p, win_d, conv_p, conv_d, S_p, S_d = [], [], [], [], [], [], [], []
    for l in range(DEPTH):
        ffn_w = (norm_ffn[l], w_router_g[l], b_router_g[l], w_router_e[l], b_router_e[l], w_gate[l], w_up[l], w_down[l])
        dn_w = (dn_conv_w[l], dn_A_log[l], dn_dt_bias[l], dn_norm[l])
        (q_r, kc_r, vc_r, ks_r, vs_r, kw_r, vw_r, ng_r, dn_qkv, dn_a, dn_b, dn_z, mg_a, mg_b) = split_projection(rmsnorm(xp, norm_mix[l]), w_in[l])
        q, gts, rows, win = nsa_rows(q_r, kc_r, vc_r, ks_r, vs_r, kw_r, vw_r, ng_r, pos_p, q_norm[l], k_norm[l])
        o_a = nsa_prompt(q, gts, rows, win, cmp_pos[l], w_cmp[l], k_norm[l])
        o_b, cbuf, S = deltanet(dn_qkv, dn_a, dn_b, dn_z,
                                jnp.zeros((B, DN_CONV - 1, 3 * DN_WIDTH), xp.dtype),
                                jnp.zeros((B, DN_HEADS, DN_HEAD_DIM, DN_HEAD_DIM), state_dn_S.dtype), *dn_w)
        kv_p.append(rows)
        win_p.append(jnp.pad(win, ((0, 0), (max(0, win_rows - T), 0), (0, 0), (0, 0), (0, 0)))[:, -win_rows:])
        conv_p.append(cbuf)
        S_p.append(S)
        xp = merge_and_ffn(xp, o_a, o_b, mg_a, mg_b, w_proj_a[l], w_proj_b[l], w_out[l], *ffn_w)
        (q_r, kc_r, vc_r, ks_r, vs_r, kw_r, vw_r, ng_r, dn_qkv, dn_a, dn_b, dn_z, mg_a, mg_b) = split_projection(rmsnorm(xd, norm_mix[l]), w_in[l])
        q, gts, rows, win = nsa_rows(q_r, kc_r, vc_r, ks_r, vs_r, kw_r, vw_r, ng_r, pos_d, q_norm[l], k_norm[l])
        o_a, new_win = nsa_sample(q, gts, rows, win, cache_nsa[l], page_table, state_win[l], cmp_pos[l], w_cmp[l], k_norm[l])
        o_b, cbuf, S = deltanet(dn_qkv, dn_a, dn_b, dn_z, state_dn_conv[l], state_dn_S[l], *dn_w)
        kv_d.append(rows)
        win_d.append(new_win)
        conv_d.append(cbuf)
        S_d.append(S)
        xd = merge_and_ffn(xd, o_a, o_b, mg_a, mg_b, w_proj_a[l], w_proj_b[l], w_out[l], *ffn_w)
    return (xp, xd, jnp.stack(kv_p), jnp.stack(kv_d), jnp.stack(win_p), jnp.stack(win_d),
            jnp.stack(conv_p), jnp.stack(conv_d), jnp.stack(S_p), jnp.stack(S_d))


_drawn_inputs = setup_inputs


def setup_inputs(seed=0):
    import zlib

    import numpy as np

    out = dict(_drawn_inputs(seed))
    spreads = {}
    factors = {'q_norm': 4.52, 'b_router_g': 3.137, 'b_router_e': 3.063}
    for name, (base, spread) in spreads.items():
        noise = np.random.default_rng([zlib.crc32(name.encode()), seed]).standard_normal(out[name].shape)
        drawn = base * np.exp(spread * noise) if base else spread * noise
        out[name] = jnp.asarray(drawn.astype(out[name].dtype))
    for name, factor in factors.items():
        out[name] = (out[name] * factor).astype(out[name].dtype)
    return out
```

```python
from contextlib import ExitStack

import numpy as np

import concourse.bass as bass
from concourse import mybir

F32 = mybir.dt.float32
I32 = mybir.dt.int32
ALU = mybir.AluOpType
ACT = mybir.ActivationFunctionType
AX = mybir.AxisListType

P = 128
D = 1024
KD = D // P
TP = 1024
TS = 8
TT = TP + TS
NT = TP // P
PAST = 2048
PAGE = 128
NPAGE = PAST // PAGE
WIN = 512
NH, NKV, HD = 8, 2, 64
ROT = 8
DH, DD = 4, 128
DW = DH * DD
NE, NG, EPG = 32, 4, 8
FE = 512
EPS = 1e-6
BIG = 1e30
NCP = 63
NCS = 127
NSEL = 33
MAXBLK = 48
MINBLK = -(-2 * TT // P)

Q0, KC0, VC0, KS0, VS0, KW0, VW0, NG0 = 0, 512, 640, 768, 896, 1024, 1152, 1280
QKV0, AB0, Z0, MA0, MB0 = 1304, 2840, 2848, 3360, 4384
RAB, RZ, RW = 1304, 1312, 1824


def constants():
    cols, where, at = [], {}, 0

    def put(name, a):
        nonlocal at
        full = np.zeros((P, int(np.prod(a.shape[1:]))), np.float32)
        full[:a.shape[0]] = a.reshape(a.shape[0], -1)
        cols.append(full)
        where[name] = (at, full.shape[1])
        at += full.shape[1]

    i = np.arange(P)
    put("ident", np.eye(P))
    put("ones", np.ones((P, P)))
    put("tri", (i[:, None] <= i[None, :]) * 1.0)
    put("strictT", (i[:, None] < i[None, :]) * 1.0)
    put("upper", np.where(i[None, :] >= i[:, None], BIG, 0.0))
    put("lower", np.where(i[None, :] < i[:, None], -BIG, 0.0))
    for s in (1, 2, 4, 8, 16, 32, 64):
        m = (i[:, None] // (2 * s) == i[None, :] // (2 * s)) & (i[:, None] // s % 2 == 1) & (i[None, :] // s % 2 == 0)
        put(f"level{s}", m * 1.0)
    inv = (np.float32(500000.0) ** (-np.arange(ROT, dtype=np.float32) / np.float32(ROT))).astype(np.float32)

    def angles(pos):
        return (pos.astype(np.float32)[..., None] * inv).astype(np.float32)

    pos = np.concatenate([np.arange(TP).reshape(NT, P), np.full((1, P), PAST)]).T
    put("cos", np.cos(angles(pos)))
    put("sin", np.sin(angles(pos)))
    put("ccos", np.cos(angles(16 * i + 31)))
    put("csin", np.sin(angles(16 * i + 31)))
    put("causal", np.where(i[None, :] > i[:, None], -BIG, 0.0))
    put("edge", np.where(i[None, :] <= i[:, None], -BIG, 0.0))
    n = np.arange(64)
    put("cmpmask", np.where(16 * n[None, None, :] + 31 > np.arange(TP).reshape(NT, P).T[:, :, None], -BIG, 0.0))
    put("cmpvalid", (i[:, None] >= 31) * 1.0)
    n, s = np.arange(NCS), np.arange(NSEL)
    put("ovl", ((16 * n[:, None] <= 64 * s + 63) & (16 * n[:, None] + 31 >= 64 * s)) * 1.0)
    put("bonus", np.tile(np.where((s == 0) | (s == 32) | (s == 31), 1000.0, 0.0), (64, 1)))
    h = np.arange(64)
    put("group", (h[:, None] // 4 == h[None, :] // 4) * 1.0)
    put("seq", (h[:, None] // 8 == np.arange(8)[None, :]) * 1.0)
    put("mhalf", np.full((P, 16), -0.5))
    put("eid", np.tile(np.arange(NE, dtype=np.float32), (P, 1)))
    put("blk", np.tile(128.0 * np.arange(NT + 1), (P, 1)))
    put("blkid", np.tile(1.0 * np.arange(MAXBLK), (P, 1)))
    put("tokvalid", (i[:, None] < TS) * 1.0)
    tok = np.arange(9 * P).reshape(9, P).T
    put("tok", np.stack([np.stack([tok, k * TT + tok], -1) for k in range(2)], 2))
    return np.concatenate(cols, axis=1).astype(np.float32), where


CONST, WHERE = constants()


class Layout:

    def __init__(self, nc):
        self.nc = nc
        self.n = 0
        self.signals = Signals(nc)

    def at(self, name, offset, shape, dt=F32):
        self.n += 1
        return self.nc.alloc_sbuf_tensor_at(f"{name}_{self.n}", shape, dt, offset=offset)


class Signals:

    def __init__(self, nc):
        self.nc, self.made = nc, []

    def named(self, prefix):
        def sem(name):
            self.made.append(self.nc.alloc_semaphore(prefix + name))
            return self.made[-1]
        return sem

    def renew(self):
        self.nc.clear_and_free_semaphores(self.made)
        self.nc.all_engine_barrier()
        self.made = []


class Region:

    def __init__(self, L, start, end):
        self.L, self.start, self.end = L, start, end

    def __call__(self, name, shape, dt=F32):
        size = int(np.prod(shape[1:])) * (2 if dt == mybir.dt.bfloat16 else 4)
        r = self.L.at(name, self.start, shape, dt)
        self.start += (size + 31) // 32 * 32
        assert self.start <= self.end, (name, self.start, self.end)
        return r


BASE = 16512
A_HT = BASE
A_CONST = A_HT + KD * TT * 4
A_OB = A_CONST + ((CONST.shape[1] * 4 + 31) // 32) * 32
A_R = A_OB + DH * TT * 4
A_RS = A_R + NT * RW * 4
A_DN = A_RS + RW * 4
A_OA = A_DN + 12 * TT * 4
A_FREE = A_OA + DH * TT * 4
A_QT = A_DN
A_KT = A_QT + 4 * TT * 4
A_MID = A_KT + 4 * TT * 4
A_END = 229344
A_SMALL = A_END - 4096


def block_norm(nc, L, PS, C, x_p, x_s, gain, hT):
    ctx = ExitStack()
    with ctx:
        sem = L.signals.named("")
        x_loaded = [sem(f"n_x_loaded{i}") for i in range(3)]
        gain_loaded, squares_done, rs_ready, xn_ready, tp_done, ht_done, dve_step = map(
            sem, ("n_gain_loaded", "n_squares_done", "n_rs_ready", "n_xn_ready", "n_tp_done", "n_ht_done", "n_dve_step"))
        x = L.at("x", A_R, [P, 3, D])
        junk = L.at("junk", A_R + 12288, [P, D])
        xn = L.at("xn", A_R + 16384, [P, 2, D])
        ss = L.at("ss", A_R + 24576, [P, 16])
        rs = L.at("rs", A_R + 24576 + 64, [P, 16])
        g = L.at("gain", A_R + 24576 + 128, [P, KD])
        rows = [P] * NT + [TS]
        block = ctx.enter_context(nc.Block())

        @block.sync
        def _(sp):
            sp.dma_start(g[:, :], gain.rearrange("(k p) -> p k", p=P), allow_slow_non_contiguous=True).then_inc(gain_loaded, 16)
            for t, n in enumerate(rows):
                if t >= 3:
                    sp.wait_ge(xn_ready, t - 2)
                src = x_p[0, t * P:(t + 1) * P, :] if t < NT else x_s[:, 0, :]
                sp.dma_start(x[0:n, t % 3, :], src).then_inc(x_loaded[t % 3], 16)

        @block.scalar
        def _(act):
            for t, n in enumerate(rows):
                act.wait_ge(x_loaded[t % 3], 16 * (t // 3 + 1))
                if t >= 1:
                    act.wait_ge(squares_done, t)
                nc.scalar.activation(junk[0:n, :], x[0:n, t % 3, :], ACT.Square, accum_out=ss[0:n, t:t + 1]).then_inc(squares_done, 1)

        @block.gpsimd
        def _(pool):
            for t, n in enumerate(rows):
                pool.wait_ge(squares_done, t + 1)
                pool.tensor_scalar(ss[0:n, t:t + 1], ss[0:n, t:t + 1], 1.0 / D, EPS, ALU.mult, ALU.add).then_inc(dve_step, 1)
                pool.wait_ge(dve_step, t + 1)
                pool.tensor_tensor(rs[0:n, t:t + 1], ss[0:n, t:t + 1], C["mhalf"][0:n, 0:1], ALU.pow).then_inc(rs_ready, 1)

        @block.vector
        def _(dve):
            dve.wait_ge(gain_loaded, 16)

            def emit(t, n):
                dve.wait_ge(tp_done, t + 1)
                for j in range(2):
                    ins = nc.vector.tensor_tensor(
                        hT[:, 4 * j:4 * j + 4, t * P:t * P + n],
                        PS[2 * (t % 2) + j][:, :].rearrange("p (k n) -> p k n", k=4)[:, :, 0:n],
                        g[:, 4 * j:4 * j + 4].unsqueeze(2).to_broadcast([P, 4, n]), ALU.mult)
                ins.then_inc(ht_done, 1)

            for t, n in enumerate(rows):
                dve.wait_ge(rs_ready, t + 1)
                if t >= 2:
                    dve.wait_ge(tp_done, t - 1)
                nc.vector.tensor_scalar(xn[0:n, t % 2, :], x[0:n, t % 3, :], rs[0:n, t:t + 1], None, ALU.mult).then_inc(xn_ready, 1)
                if t >= 1:
                    emit(t - 1, rows[t - 1])
            emit(NT, TS)

        @block.tensor
        def _(pe):
            for t, n in enumerate(rows):
                pe.wait_ge(xn_ready, t + 1)
                if t >= 2:
                    pe.wait_ge(ht_done, t - 1)
                for k in range(KD):
                    ins = nc.tensor.transpose(PS[2 * (t % 2) + k // 4][:, (k % 4) * P:(k % 4) * P + n],
                                              xn[0:n, t % 2, k * P:(k + 1) * P], C["ident"][0:n, 0:n])
                ins.then_inc(tp_done, 1)


def block_project(nc, L, PS, C, w_in, hT, R, Rs, dnT):
    ctx = ExitStack()
    with ctx:
        sem = L.signals.named("")
        w_loaded0, w_loaded1, mm_done, act_copied, dve_copied = map(
            sem, ("p_w_loaded0", "p_w_loaded1", "p_mm_done", "p_act_copied", "p_dve_copied"))
        w_loaded = (w_loaded0, w_loaded1)
        w = [L.at("w0", A_OB, [P, KD, 512]), L.at("w1", A_OA, [P, KD, 512])]
        wv = w_in.rearrange("(k p) n -> p k n", p=P)
        loads = [([(0, 512)], 0), ([(512, 1024)], 512), ([(1024, QKV0), (AB0, Z0)], 1024), ([(Z0, MA0)], RZ)]
        loads += [([(QKV0 + 512 * j, QKV0 + 512 * j + 512)], None) for j in range(3)]
        units = []
        for c, (pieces, at) in enumerate(loads):
            width = sum(b - a for a, b in pieces)
            if at is not None:
                for t in range(NT + 1):
                    n = P if t < NT else TS
                    dst = R[:, t, at:at + width] if t < NT else Rs[0:TS, at:at + width]
                    if c == 0:
                        dst = dst.rearrange("p (j g d) -> p g j d", g=NKV, d=HD)
                    units.append((c, n, width, None, t, dst))
            else:
                for m in range(4):
                    for t0, n in ((0, 512), (512, 512), (TP, TS)):
                        units.append((c, P, n, m, t0, dnT[:, 4 * (c - 4) + m, t0:t0 + n]))
        last_of = {c: max(i for i, u in enumerate(units) if u[0] == c) for c in range(len(loads))}
        counts, done = [], [0, 0]
        for c, (pieces, _) in enumerate(loads):
            done[c % 2] += 16 * len(pieces)
            counts.append(done[c % 2])

        def source(i, c, rows, n):
            s = PS[i % 8][0:rows, 0:n]
            return s.rearrange("p (g j d) -> p g j d", g=NKV, d=HD) if c == 0 else s

        block = ctx.enter_context(nc.Block())

        @block.sync
        def _(sp):
            for c, (pieces, _) in enumerate(loads):
                if c >= 2:
                    sp.wait_ge(mm_done, last_of[c - 2] + 1)
                o = 0
                for a, b in pieces:
                    sp.dma_start(w[c % 2][:, :, o:o + b - a], wv[:, :, a:b]).then_inc(w_loaded[c % 2], 16)
                    o += b - a

        @block.tensor
        def _(pe):
            seen = -1
            for i, (c, m_rows, n, m, t, _) in enumerate(units):
                if c != seen:
                    pe.wait_ge(w_loaded[c % 2], counts[c])
                    seen = c
                if i >= 8:
                    pe.wait_ge((act_copied, dve_copied)[i % 2], (i - 8) // 2 + 1)
                for k in range(KD):
                    if m is None:
                        lhsT, rhs = hT[:, k, t * P:t * P + m_rows], w[c % 2][:, k, 0:n]
                    else:
                        lhsT, rhs = w[c % 2][:, k, m * P:(m + 1) * P], hT[:, k, t:t + n]
                    ins = nc.tensor.matmul(PS[i % 8][0:m_rows, 0:n], lhsT, rhs, start=(k == 0), stop=(k == KD - 1))
                ins.then_inc(mm_done, 1)

        @block.scalar
        def _(act):
            for i, (c, rows, n, m, t, dst) in enumerate(units):
                if i % 2 == 0:
                    act.wait_ge(mm_done, i + 1)
                    nc.scalar.copy(dst, source(i, c, rows, n)).then_inc(act_copied, 1)

        @block.vector
        def _(dve):
            for i, (c, rows, n, m, t, dst) in enumerate(units):
                if i % 2 == 1:
                    dve.wait_ge(mm_done, i + 1)
                    nc.vector.tensor_copy(dst, source(i, c, rows, n)).then_inc(dve_copied, 1)


class Steps:

    def __init__(self, engine, semaphore):
        self.engine, self.semaphore, self.n = engine, semaphore, 0

    def __call__(self, ins):
        self.n += 1
        ins.then_inc(self.semaphore, 1)
        self.engine.wait_ge(self.semaphore, self.n)


def block_conv(nc, L, PS, C, state_conv, conv_w, dnT, convT, out_conv_p, out_conv_s):
    NC = 12
    NR = 4 + 3 * TS
    ctx = ExitStack()
    with ctx:
        sem = L.signals.named("")
        rows_loaded, rows_tp, rows_copied, tail_tp, tail_copied, stored, conv_done, silu_done, sq_done, sum_done, sum_copied, root_done, diag_done, bcast_done, unit_done, dve_step = map(
            sem, ("c_rows_loaded", "c_rows_tp", "c_rows_copied", "c_tail_tp", "c_tail_copied", "c_stored", "c_conv_done",
                  "c_silu_done", "c_sq_done", "c_sum_done", "c_sum_copied", "c_root_done", "c_diag_done", "c_bcast_done", "c_unit_done", "c_dve_step"))
        rows = L.at("conv_rows", A_OB, [NR, NC * P])
        tail = L.at("conv_tail", A_OB + 6144, [3 + TS, NC * P])
        samp = L.at("conv_samp", A_OB + 12288, [P, 2, NC, TS])
        acc = L.at("conv_acc", A_OA, [P, 2, TT])
        rn = L.at("conv_rn", A_OA + 2 * TT * 4, [P, 72])
        diag = L.at("conv_diag", A_OA + 2 * TT * 4 + 288, [P, 2, 4, P])
        w = convT
        units = [(c, j, t0, n) for c in range(8) for j, (t0, n) in enumerate(((0, 512), (512, 512), (TP, TS)))]
        block = ctx.enter_context(nc.Block())

        @block.sync
        def _(sp):
            sp.dma_start(rows[0:4, :], conv_w).then_inc(rows_loaded, 16)
            sp.dma_start(rows[4:NR, :], state_conv.rearrange("b j c -> (b j) c")).then_inc(rows_loaded, 16)
            sp.wait_ge(tail_copied, 3)
            sp.dma_start(out_conv_p, tail[0:3, :]).then_inc(stored, 16)
            sp.dma_start(out_conv_s[:, 2, :], tail[3:3 + TS, :]).then_inc(stored, 16)
            sp.dma_start(out_conv_s[:, 0:2, :], state_conv[:, 1:3, :]).then_inc(stored, 16)
            sp.wait_ge(stored, 48)

        @block.tensor
        def _(pe):
            pe.wait_ge(rows_loaded, 32)
            for c in range(NC):
                ins = nc.tensor.transpose(PS[0][:, c * NR:(c + 1) * NR], rows[0:NR, c * P:(c + 1) * P], C["ident"][0:NR, 0:NR])
            ins.then_inc(rows_tp, 1)
            for c in range(NC):
                ins = nc.tensor.transpose(PS[1 + c // 4][0:3 + TS, (c % 4) * P:(c % 4 + 1) * P], dnT[:, c, TP - 3:TT], C["ident"][:, :])
            ins.then_inc(tail_tp, 1)
            for c in range(8):
                pe.wait_ge(sq_done, c + 1)
                for t in range(NT + 1):
                    n = P if t < NT else TS
                    ins = nc.tensor.matmul(PS[4][0:n, 8 * t + c:8 * t + c + 1], acc[:, c % 2, t * P:t * P + n], C["ones"][:, 0:1], start=True, stop=True)
                ins.then_inc(sum_done, 1)
            for u, (c, j, t0, n) in enumerate(units):
                m = min(n, P)
                pe.wait_ge(diag_done, u + 1)
                if u >= 2:
                    pe.wait_ge(unit_done, u - 1)
                nc.tensor.matmul(PS[5 + u % 2][:, 0:n], C["ones"][0:m, :],
                                 diag[0:m, u % 2].rearrange("p t n -> p (t n)")[:, 0:n], start=True, stop=True).then_inc(bcast_done, 1)

        @block.vector
        def _(dve):
            step = Steps(dve, dve_step)
            dve.wait_ge(rows_tp, 1)
            nc.vector.tensor_copy(w[:, :, :], PS[0][:, 0:NC * NR].rearrange("p (c r) -> p c r", r=NR)).then_inc(rows_copied, 1)
            dve.wait_ge(rows_copied, 1)
            dve.wait_ge(tail_tp, 1)
            for b in range(3):
                nc.vector.tensor_copy(tail[:, 512 * b:512 * b + 512], PS[1 + b][0:3 + TS, :]).then_inc(tail_copied, 1)
            st = w[:, :, 4:NR].rearrange("p c (b j) -> p c b j", j=3)
            tap = lambda j: w[:, :, j:j + 1].to_broadcast([P, NC, TS])
            step(nc.vector.tensor_tensor(samp[:, 0], dnT[:, :, TP:TT], tap(3), ALU.mult))
            for j in range(3):
                step(nc.vector.tensor_tensor(samp[:, 1], st[:, :, :, j], tap(j), ALU.mult))
                step(nc.vector.tensor_tensor(samp[:, 0], samp[:, 0], samp[:, 1], ALU.add))
            for c in range(NC):
                if c >= 2:
                    dve.wait_ge(silu_done, c - 1)
                    if c - 2 < 8:
                        dve.wait_ge(sum_done, c - 1)
                a, x = acc[:, c % 2, :], dnT[:, c, :]
                nc.vector.tensor_copy(a[:, TP:TT], samp[:, 0, c, :])
                step(nc.vector.tensor_scalar(a[:, 0:TP], x[:, 0:TP], w[:, c, 3:4], None, ALU.mult))
                for j in (2, 1, 0):
                    d = 3 - j
                    ins = nc.vector.scalar_tensor_tensor(a[:, d:TP], x[:, 0:TP - d], w[:, c, j:j + 1], a[:, d:TP], ALU.mult, ALU.add)
                    if j:
                        step(ins)
                    else:
                        ins.then_inc(conv_done, 1)
            dve.wait_ge(sum_done, 8)
            nc.vector.tensor_scalar(rn[:, 0:64], PS[4][:, 0:64], EPS, None, ALU.add).then_inc(sum_copied, 1)
            nc.vector.tensor_scalar(rn[0:TS, 64:72], PS[4][0:TS, 64:72], EPS, None, ALU.add).then_inc(sum_copied, 1)
            dve.wait_ge(silu_done, 12)
            for u, (c, j, t0, n) in enumerate(units):
                dve.wait_ge(bcast_done, u + 1)
                nc.vector.scalar_tensor_tensor(dnT[:, c, t0:t0 + n], PS[5 + u % 2][:, 0:n], DD ** -0.5 if c < 4 else 1.0,
                                               dnT[:, c, t0:t0 + n], ALU.mult, ALU.mult).then_inc(unit_done, 1)

        @block.gpsimd
        def _(pool):
            for c in range(8):
                pool.wait_ge(silu_done, c + 1)
                nc.gpsimd.tensor_tensor(acc[:, c % 2, :], dnT[:, c, :], dnT[:, c, :], ALU.mult).then_inc(sq_done, 1)
            pool.wait_ge(sum_copied, 2)
            nc.gpsimd.tensor_tensor(rn[:, 0:64], rn[:, 0:64], C["mhalf"][:, 0:1].to_broadcast([P, 64]), ALU.pow).then_inc(root_done, 1)
            nc.gpsimd.tensor_tensor(rn[0:TS, 64:72], rn[0:TS, 64:72], C["mhalf"][0:TS, 0:8], ALU.pow).then_inc(root_done, 1)
            pool.wait_ge(root_done, 2)
            for u, (c, j, t0, n) in enumerate(units):
                if u >= 2:
                    pool.wait_ge(bcast_done, u - 1)
                if j < 2:
                    ins = nc.gpsimd.tensor_tensor(diag[:, u % 2], C["ident"].unsqueeze(1).to_broadcast([P, 4, P]),
                                                  rn[:, 32 * j + c:32 * j + 32:8].unsqueeze(2).to_broadcast([P, 4, P]), ALU.mult)
                else:
                    ins = nc.gpsimd.tensor_tensor(diag[0:TS, u % 2, 0, 0:TS], C["ident"][0:TS, 0:TS],
                                                  rn[0:TS, 64 + c:65 + c].to_broadcast([TS, TS]), ALU.mult)
                ins.then_inc(diag_done, 1)

        @block.scalar
        def _(act):
            act.wait_ge(tail_tp, 1)
            for c in range(NC):
                act.wait_ge(conv_done, c + 1)
                nc.scalar.activation(dnT[:, c, :], acc[:, c % 2, :], ACT.Silu).then_inc(silu_done, 1)


def block_decays(nc, L, PS, C, A_log, dt_bias, R, Rs, ab_p, ab_s):
    ctx = ExitStack()
    with ctx:
        sem = L.signals.named("")
        loaded, dve_step, act_step = map(sem, ("d_loaded", "d_dve_step", "d_act_step"))
        par = L.at("decay_par", A_FREE, [P, 8])
        y = L.at("decay_y", A_FREE + 32, [P, NT, 4])
        z = L.at("decay_z", A_FREE + 160, [P, NT, 4])
        block = ctx.enter_context(nc.Block())
        cases = ((P, NT, R[:, :, RAB:RAB + 4], R[:, :, RAB + 4:RZ], ab_p), (TS, 1, Rs[:, RAB:RAB + 4].unsqueeze(1), Rs[:, RAB + 4:RZ].unsqueeze(1), ab_s))

        @block.sync
        def _(sp):
            sp.dma_start(par[:, 0:4], A_log.unsqueeze(0).to_broadcast([P, 4])).then_inc(loaded, 16)
            sp.dma_start(par[:, 4:8], dt_bias.unsqueeze(0).to_broadcast([P, 4])).then_inc(loaded, 16)

        @block.vector
        def _(dve):
            step = Steps(dve, dve_step)
            dve.wait_ge(loaded, 32)
            for i, (n, t, a, b, out) in enumerate(cases):
                yy, zz = y[0:n, 0:t], z[0:n, 0:t]
                step(nc.vector.tensor_tensor(yy, a, par[0:n, 4:8].unsqueeze(1).to_broadcast([n, t, 4]), ALU.add))
                step(nc.vector.tensor_scalar(zz, yy, -1.0, None, ALU.mult))
                step(nc.vector.tensor_tensor(zz, zz, yy, ALU.min))
                dve.wait_ge(act_step, 2 * i + 3)
                step(nc.vector.scalar_tensor_tensor(yy, yy, 0.0, zz, ALU.max, ALU.add))
                step(nc.vector.tensor_tensor(yy, yy, par[0:n, 0:4].unsqueeze(1).to_broadcast([n, t, 4]), ALU.mult))
                step(nc.vector.tensor_scalar(out[0:n, :, 0:4], yy, -1.0, None, ALU.mult))

        @block.scalar
        def _(act):
            step = Steps(act, act_step)
            act.wait_ge(loaded, 32)
            step(nc.scalar.activation(par[:, 0:4], par[:, 0:4], ACT.Exp))
            for i, (n, t, a, b, out) in enumerate(cases):
                zz = z[0:n, 0:t]
                act.wait_ge(dve_step, 6 * i + 3)
                step(nc.scalar.activation(zz, zz, ACT.Exp))
                step(nc.scalar.activation(zz, zz, ACT.Ln, bias=1.0))
            for n, t, a, b, out in cases:
                nc.scalar.activation(out[0:n, :, 4:8], b, ACT.Sigmoid)


def block_delta(nc, L, PS, C, dnT, ab, S_out):
    ctx = ExitStack()
    with ctx:
        sem = L.signals.named("g_")
        gates_done, rows_tp, grow_done, gcol_done, kk_done, qk_done = map(sem, ("gates", "rows_tp", "grow", "gcol", "kk", "qk"))
        w_done, w_copied, z_done, tu_done, mask_done = map(sem, ("w", "w_copied", "z", "tu", "mask"))
        first_tp, u_ready, wT_done, wT_copied, vnew_done, vnew_copied, o_done, qs_scaled, s_done, s_ready = map(
            sem, ("first_tp", "u_ready", "wT", "wT_copied", "vnew", "vnew_copied", "o", "qs_scaled", "s", "s_ready"))
        pre, d_in, d_exp, a_ready, qkd_ready, kv_ready, o_ready, chunk_done, dve_step, col_done, s_stored, small = map(
            sem, ("pre", "d_in", "d_exp", "a_ready", "qkd_ready", "kv_ready", "o_ready", "chunk", "dve_step", "col", "s_stored", "small"))
        t = Region(L, A_OA, A_END - 512)
        H4 = [P, DH, P]
        tg, D1, D2, A, Tm, Um, Wb, wT, QKD = (t(n, H4) for n in ("tg", "D1", "D2", "A", "T", "U", "W", "wT", "QKD"))
        kd, vb, kbg, vnew, S, o = (t(n, H4) for n in ("kd", "vb", "kbg", "vnew", "S", "o"))
        B = [t("B0", H4), t("B1", H4)]
        sm = t("small", [P, 12, 4])
        gcol, ngcol, egc, egl, kds, nbg = (sm[:, i, :] for i in range(6))
        v4 = lambda ps: ps[:, :].rearrange("p (h n) -> p h n", h=DH)
        heads = range(DH)
        LV = (2, 4, 8, 16, 32, 64)
        NL = len(LV)
        block = ctx.enter_context(nc.Block())
        bc = lambda m: m.unsqueeze(1).to_broadcast(H4)
        col = lambda m: m.unsqueeze(2).to_broadcast(H4)

        @block.tensor
        def _(pe):
            for c in range(NT):
                tok = slice(c * P, (c + 1) * P)
                if c:
                    pe.wait_ge(chunk_done, c)
                for h in heads:
                    nc.tensor.transpose(PS[0][:, h * P:(h + 1) * P], dnT[:, 4 + h, tok], C["ident"])
                for h in heads:
                    ins = nc.tensor.transpose(PS[1][:, h * P:(h + 1) * P], dnT[:, 8 + h, tok], C["ident"])
                ins.then_inc(rows_tp, 1)
                pe.wait_ge(gates_done, c + 1)
                nc.tensor.matmul(PS[2][:, :], C["ones"], tg[:, :, :].rearrange("p h n -> p (h n)"), start=True, stop=True)
                nc.tensor.matmul(PS[3][:, 0:4], C["tri"], ab[:, c, 0:4], start=True, stop=True).then_inc(grow_done, 1)
                for h in heads:
                    ins = nc.tensor.matmul(PS[4][:, h * P:(h + 1) * P], dnT[:, 4 + h, tok], dnT[:, 4 + h, tok], start=True, stop=True)
                ins.then_inc(kk_done, 1)
                for h in heads:
                    ins = nc.tensor.matmul(PS[5][:, h * P:(h + 1) * P], dnT[:, 4 + h, tok], dnT[:, h, tok], start=True, stop=True)
                ins.then_inc(qk_done, 1)
                pe.wait_ge(mask_done, (NL + 1) * c + 1)
                for h in heads:
                    ins = nc.tensor.transpose(PS[6][:, h * P:(h + 1) * P], B[0][:, h, :], C["ident"])
                ins.then_inc(first_tp, 1)
                for l in range(NL):
                    pe.wait_ge(mask_done, (NL + 1) * c + l + 2)
                    pe.wait_ge(tu_done, (NL + 1) * c + l + 1)
                    for h in heads:
                        ins = nc.tensor.matmul(PS[7][:, h * P:(h + 1) * P], B[(l + 1) % 2][:, h, :], Um[:, h, :], start=True, stop=True)
                    ins.then_inc(w_done, 1)
                    pe.wait_ge(w_copied, NL * c + l + 1)
                    if l == NL - 1:
                        pe.wait_ge(kv_ready, c + 1)
                    else:
                        for h in heads:
                            nc.tensor.matmul(PS[4][:, h * P:(h + 1) * P], Wb[:, h, :], Tm[:, h, :], start=True, stop=True)
                    for h in heads:
                        ins = nc.tensor.matmul(PS[6][:, h * P:(h + 1) * P], Tm[:, h, :], Wb[:, h, :], start=True, stop=True)
                    ins.then_inc(z_done, 1)
                pe.wait_ge(tu_done, (NL + 1) * (c + 1))
                for h in heads:
                    ins = nc.tensor.matmul(PS[4][:, h * P:(h + 1) * P], kbg[:, h, :], Um[:, h, :], start=True, stop=True)
                ins.then_inc(wT_done, 1)
                pe.wait_ge(wT_copied, c + 1)
                pe.wait_ge(s_ready, c + 1)
                for h in heads:
                    nc.tensor.matmul(PS[0][:, h * P:(h + 1) * P], Um[:, h, :], vb[:, h, :], start=True, stop=False)
                    ins = nc.tensor.matmul(PS[0][:, h * P:(h + 1) * P], wT[:, h, :], S[:, h, :], start=False, stop=True)
                ins.then_inc(vnew_done, 1)
                for h in heads:
                    ins = nc.tensor.matmul(PS[1][:, h * P:(h + 1) * P], dnT[:, h, tok], S[:, h, :], start=True, stop=True)
                ins.then_inc(o_done, 1)
                pe.wait_ge(vnew_copied, c + 1)
                pe.wait_ge(qkd_ready, c + 1)
                for h in heads:
                    nc.tensor.matmul(PS[2][:, h * P:(h + 1) * P], QKD[:, h, :], vnew[:, h, :], start=True, stop=True)
                for h in heads:
                    ins = nc.tensor.matmul(PS[5][:, h * P:(h + 1) * P], kd[:, h, :], vnew[:, h, :], start=True, stop=True)
                ins.then_inc(s_done, 1)

        @block.gpsimd
        def _(pool):
            nc.gpsimd.memset(S[:, :, :], 0.0).then_inc(s_ready, 1)
            for c in range(NT):
                if c:
                    pool.wait_ge(chunk_done, c)
                nc.gpsimd.tensor_tensor(tg[:, :, :], bc(C["tri"]), col(ab[:, c, 0:4]), ALU.mult).then_inc(gates_done, 1)
                pool.wait_ge(a_ready, c + 1)
                for l, s in enumerate((1,) + LV):
                    if l >= 3:
                        pool.wait_ge(w_done, NL * c + l - 2)
                    nc.gpsimd.tensor_tensor(B[l % 2][:, :, :], bc(C[f"level{s}"]), A[:, :, :], ALU.mult).then_inc(mask_done, 1)
                    if l == 0:
                        pool.wait_ge(mask_done, (NL + 1) * c + 1)
                        nc.gpsimd.tensor_tensor(Tm[:, :, :], bc(C["ident"]), B[0][:, :, :], ALU.subtract).then_inc(pre, 1)
                    if l == 1:
                        pool.wait_ge(first_tp, c + 1)
                        pool.wait_ge(pre, c + 1)

        @block.vector
        def _(dve):
            step = Steps(dve, dve_step)
            for c in range(NT):
                dve.wait_ge(grow_done, c + 1)
                step(nc.vector.tensor_copy(gcol, PS[3][:, 0:4]))
                step(nc.vector.tensor_scalar(ngcol, PS[3][:, 0:4], -1.0, None, ALU.mult))
                last = v4(PS[2])[:, :, P - 1]
                nc.vector.tensor_copy(egl, last)
                nc.vector.tensor_tensor(kds, last, gcol, ALU.subtract).then_inc(small, 1)
                nc.vector.tensor_tensor(D1[:, :, :], v4(PS[2]), bc(C["upper"]), ALU.add).then_inc(d_in, 1)
                nc.vector.tensor_tensor(D2[:, :, :], v4(PS[2]), bc(C["lower"]), ALU.add).then_inc(d_in, 1)
                dve.wait_ge(col_done, c + 1)
                dve.wait_ge(rows_tp, c + 1)
                step(nc.vector.scalar_tensor_tensor(nbg, egc, -1.0, ab[:, c, 4:8], ALU.mult, ALU.mult))
                dve.wait_ge(d_exp, 2 * c + 1)
                dve.wait_ge(kk_done, c + 1)
                step(nc.vector.tensor_tensor(D1[:, :, :], v4(PS[4]), D1[:, :, :], ALU.mult))
                nc.vector.tensor_tensor(A[:, :, :], D1[:, :, :], col(ab[:, c, 4:8]), ALU.mult).then_inc(a_ready, 1)
                nc.vector.tensor_tensor(kbg[:, :, :], v4(PS[0]), col(nbg), ALU.mult)
                nc.vector.tensor_tensor(vb[:, :, :], v4(PS[1]), col(ab[:, c, 4:8]), ALU.mult)
                nc.vector.tensor_tensor(kd[:, :, :], v4(PS[0]), col(kds), ALU.mult).then_inc(kv_ready, 1)
                dve.wait_ge(d_exp, 2 * c + 2)
                dve.wait_ge(qk_done, c + 1)
                nc.vector.tensor_tensor(QKD[:, :, :], v4(PS[5]), D2[:, :, :], ALU.mult).then_inc(qkd_ready, 1)
                dve.wait_ge(first_tp, c + 1)
                dve.wait_ge(pre, c + 1)
                nc.vector.scalar_tensor_tensor(Um[:, :, :], v4(PS[6]), -1.0, bc(C["ident"]), ALU.mult, ALU.add).then_inc(tu_done, 1)
                for l in range(NL):
                    dve.wait_ge(z_done, NL * c + l + 1)
                    if l == 0:
                        dve.wait_ge(tu_done, (NL + 1) * c + 1)
                    if l < NL - 1:
                        step(nc.vector.tensor_tensor(Tm[:, :, :], Tm[:, :, :], v4(PS[4]), ALU.subtract))
                    ins = nc.vector.tensor_tensor(Um[:, :, :], Um[:, :, :], v4(PS[6]), ALU.subtract)
                    ins.then_inc(tu_done, 1)
                    dve.wait_ge(tu_done, (NL + 1) * c + l + 2)
                dve.wait_ge(qs_scaled, c + 1)
                dve.wait_ge(s_done, c + 1)
                ov = dnT[:, 8:12, c * P:(c + 1) * P]
                nc.vector.tensor_tensor(ov, o[:, :, :], v4(PS[2]), ALU.add).then_inc(o_ready, 1)
                step(nc.vector.tensor_tensor(S[:, :, :], S[:, :, :], col(egl), ALU.mult))
                nc.vector.tensor_tensor(S[:, :, :], S[:, :, :], v4(PS[5]), ALU.add).then_inc(s_ready, 1)
                dve.wait_ge(s_ready, c + 2)
                dve.wait_ge(o_ready, c + 1)
                nc.vector.tensor_copy(sm[:, 11, :], gcol).then_inc(chunk_done, 1)

        @block.scalar
        def _(act):
            for c in range(NT):
                act.wait_ge(small, c + 1)
                nc.scalar.activation(egc, gcol, ACT.Exp)
                nc.scalar.activation(kds, kds, ACT.Exp)
                nc.scalar.activation(egl, egl, ACT.Exp).then_inc(col_done, 1)
                for i, (Dm, bias, scale) in enumerate(((D1, gcol, -1.0), (D2, ngcol, 1.0))):
                    act.wait_ge(d_in, 2 * c + i + 1)
                    for h in heads:
                        ins = nc.scalar.activation(Dm[:, h, :], Dm[:, h, :], ACT.Exp, bias=bias[:, h:h + 1], scale=scale)
                    ins.then_inc(d_exp, 1)
                for l in range(NL):
                    act.wait_ge(w_done, NL * c + l + 1)
                    nc.scalar.copy(Wb[:, :, :], v4(PS[7])).then_inc(w_copied, 1)
                act.wait_ge(wT_done, c + 1)
                nc.scalar.copy(wT[:, :, :], v4(PS[4])).then_inc(wT_copied, 1)
                act.wait_ge(vnew_done, c + 1)
                nc.scalar.copy(vnew[:, :, :], v4(PS[0])).then_inc(vnew_copied, 1)
                act.wait_ge(o_done, c + 1)
                act.wait_ge(col_done, c + 1)
                for h in heads:
                    ins = nc.scalar.mul(o[:, h, :], v4(PS[1])[:, h, :], egc[:, h:h + 1])
                ins.then_inc(qs_scaled, 1)

        @block.sync
        def _(sp):
            sp.wait_ge(s_ready, NT + 1)
            sp.dma_start(S_out.rearrange("h d e -> d h e"), S[:, :, :]).then_inc(s_stored, 16)
            sp.wait_ge(s_stored, 16)


def block_delta_sample(nc, L, PS, C, state_S, dnT, ab_s, Os, S_out):
    ctx = ExitStack()
    with ctx:
        sem = L.signals.named("e_")
        S_loaded = [sem("S_loaded0"), sem("S_loaded1")]
        S_stored = [sem("S_stored0"), sem("S_stored1")]
        diag_done, row_done, row_ready, kS_done, v_ready, vdiag_done, vb_done, S_ready, o_done, o_copied, otp_done, dve_step = map(
            sem, ("diag", "row", "row_ready", "kS", "v_ready", "vdiag", "vb", "S_ready", "o", "o_copied", "otp", "dve_step"))
        t = Region(L, A_OA, A_FREE + 14336)
        S0 = t("S0", [P, 2, DH, P])
        S1 = t("S1", [P, 2, DH, P])
        diag = t("diag", [P, DH, P])
        T1 = t("T1", [P, DH, P])
        rdiag = t("rdiag", [TS, 2, DH, TS])
        row = t("row", [P, 2, DH, TS])
        bg = t("bg", [P, DH, TS])
        bv = t("bv", [P, DH, TS])
        kx = t("kx", [P, DH])
        vn = t("vn", [P, DH])
        oT = t("oT", [P, DH, TS])
        q, k, v = (dnT[:, 4 * i:4 * i + 4, TP:TT] for i in range(3))
        block = ctx.enter_context(nc.Block())

        @block.sync
        def _(sp):
            for b in range(TS):
                if b >= 2:
                    sp.wait_ge(S_ready, b - 1)
                sp.dma_start(S0[:, b % 2], state_S[b].rearrange("h d e -> d h e")).then_inc(S_loaded[b % 2], 16)
                if b >= 1:
                    sp.wait_ge(S_ready, b)
                    sp.dma_start(S_out[b - 1].rearrange("h d e -> d h e"), S1[:, (b - 1) % 2]).then_inc(S_stored[(b - 1) % 2], 16)
            sp.wait_ge(S_ready, TS)
            sp.dma_start(S_out[TS - 1].rearrange("h d e -> d h e"), S1[:, (TS - 1) % 2]).then_inc(S_stored[(TS - 1) % 2], 16)
            for s in S_stored:
                sp.wait_ge(s, 16 * (TS // 2))

        @block.gpsimd
        def _(pool):
            for i in range(2):
                nc.gpsimd.tensor_tensor(rdiag[:, i], C["ident"][0:TS, 0:TS].unsqueeze(1).to_broadcast([TS, DH, TS]),
                                        ab_s[0:TS, 0, 4 * i:4 * i + 4].unsqueeze(2).to_broadcast([TS, DH, TS]), ALU.mult).then_inc(diag_done, 1)
            for b in range(TS):
                pool.wait_ge(v_ready, b + 1)
                if b:
                    pool.wait_ge(vb_done, b)
                nc.gpsimd.tensor_tensor(diag[:, :, :], C["ident"].unsqueeze(1).to_broadcast([P, DH, P]),
                                        vn[:, :].unsqueeze(2).to_broadcast([P, DH, P]), ALU.mult).then_inc(vdiag_done, 1)

        @block.tensor
        def _(pe):
            pe.wait_ge(diag_done, 2)
            nc.tensor.matmul(PS[3][:, 0:64], C["ones"][0:TS, :], rdiag[:, :, :, :].rearrange("p i h b -> p (i h b)"), start=True, stop=True).then_inc(row_done, 1)
            for b in range(TS):
                pe.wait_ge(S_loaded[b % 2], 16 * (b // 2 + 1))
                if b:
                    pe.wait_ge(v_ready, b)
                for h in range(DH):
                    ins = nc.tensor.matmul(PS[0][:, h:h + 1], S0[:, b % 2, h, :], k[:, h, b:b + 1], start=True, stop=True)
                ins.then_inc(kS_done, 1)
                pe.wait_ge(vdiag_done, b + 1)
                if b:
                    pe.wait_ge(S_ready, b)
                nc.tensor.matmul(PS[1][:, :], C["ones"], diag[:, :, :].rearrange("p h n -> p (h n)"), start=True, stop=True).then_inc(vb_done, 1)
                pe.wait_ge(S_ready, b + 1)
                for h in range(DH):
                    ins = nc.tensor.matmul(PS[2][:, h * TS + b:h * TS + b + 1], S1[:, b % 2, h, :], q[:, h, b:b + 1], start=True, stop=True)
                ins.then_inc(o_done, 1)
            pe.wait_ge(o_copied, 1)
            for h in range(DH):
                ins = nc.tensor.transpose(PS[4][0:TS, h * P:(h + 1) * P], oT[:, h, :], C["ident"])
            ins.then_inc(otp_done, 1)

        @block.scalar
        def _(act):
            act.wait_ge(row_done, 1)
            nc.scalar.activation(row[:, 0], PS[3][:, 0:32].rearrange("p (h b) -> p h b", h=DH), ACT.Exp).then_inc(row_ready, 1)
            nc.scalar.copy(row[:, 1], PS[3][:, 32:64].rearrange("p (h b) -> p h b", h=DH)).then_inc(row_ready, 1)

        @block.vector
        def _(dve):
            step = Steps(dve, dve_step)
            dve.wait_ge(row_ready, 2)
            nc.vector.tensor_tensor(bg[:, :, :], row[:, 0], row[:, 1], ALU.mult)
            step(nc.vector.tensor_tensor(bv[:, :, :], v, row[:, 1], ALU.mult))
            for b in range(TS):
                dve.wait_ge(kS_done, b + 1)
                step(nc.vector.tensor_tensor(kx[:, :], PS[0][:, 0:DH], bg[:, :, b], ALU.mult))
                if b:
                    dve.wait_ge(vdiag_done, b)
                nc.vector.tensor_tensor(vn[:, :], bv[:, :, b], kx[:, :], ALU.subtract).then_inc(v_ready, 1)
                if b >= 2:
                    dve.wait_ge(S_stored[b % 2], 16 * (b // 2))
                    dve.wait_ge(o_done, b - 1)
                nc.vector.tensor_tensor(S1[:, b % 2], S0[:, b % 2], row[:, 0, :, b].unsqueeze(2).to_broadcast([P, DH, P]), ALU.mult)
                dve.wait_ge(vb_done, b + 1)
                step(nc.vector.tensor_tensor(T1[:, :, :], PS[1][:, :].rearrange("p (h n) -> p h n", h=DH), k[:, :, b].unsqueeze(2).to_broadcast([P, DH, P]), ALU.mult))
                nc.vector.tensor_tensor(S1[:, b % 2], S1[:, b % 2], T1[:, :, :], ALU.add).then_inc(S_ready, 1)
            dve.wait_ge(o_done, TS)
            nc.vector.tensor_copy(oT[:, :, :], PS[2][:, 0:32].rearrange("p (h b) -> p h b", h=DH)).then_inc(o_copied, 1)
            dve.wait_ge(otp_done, 1)
            nc.vector.tensor_copy(Os[:, :], PS[4][0:TS, :])


def block_delta_gate(nc, L, PS, C, dnT, Os, R, Rs, dn_norm, obT):
    ctx = ExitStack()
    with ctx:
        sem = L.signals.named("h_")
        loaded, silu_done, zg_done, sq_done, ss_done, mean_done, r_done, y_done, tp_done, copied, dve_step = map(
            sem, ("loaded", "silu", "zg", "sq", "ss", "mean", "r", "y", "tp", "copied", "dve_step"))
        sq = L.at("h_sq", A_OA, [P, 2, DH, P])
        y = L.at("h_y", A_OA + 4096, [P, 2, DH, P])
        gain = L.at("h_gain", A_OA + 8192, [P, P])
        ss = L.at("h_ss", A_OA + 8704, [P, NT + 1, DH])
        mean = L.at("h_mean", A_OA + 8704 + 160, [P, NT + 1, DH])
        r = L.at("h_r", A_OA + 8704 + 320, [P, NT + 1, DH])
        tiles = [(c, P, dnT[:, 8:12, c * P:(c + 1) * P], R[:, c, RZ:RW].rearrange("p (h n) -> p h n", h=DH)) for c in range(NT)]
        tiles.append((NT, TS, Os[:, :].rearrange("p (h n) -> p h n", h=DH), Rs[:, RZ:RW].rearrange("p (h n) -> p h n", h=DH)))
        block = ctx.enter_context(nc.Block())

        @block.sync
        def _(sp):
            sp.dma_start(gain[:, :], dn_norm.unsqueeze(0).to_broadcast([P, P])).then_inc(loaded, 16)

        @block.scalar
        def _(act):
            for c, n, o, z in tiles:
                nc.scalar.activation(z, z, ACT.Silu).then_inc(silu_done, 1)
            for c, n, o, z in tiles:
                act.wait_ge(tp_done, c + 1)
                nc.scalar.copy(obT[:, :, c * P:c * P + n], PS[c % 2][:, :].rearrange("p (h n) -> p h n", h=DH)[:, :, 0:n]).then_inc(copied, 1)

        @block.gpsimd
        def _(pool):
            for c, n, o, z in tiles:
                if c >= 2:
                    pool.wait_ge(ss_done, c - 1)
                nc.gpsimd.tensor_tensor(sq[0:n, c % 2], o, o, ALU.mult).then_inc(sq_done, 1)
            pool.wait_ge(mean_done, 2)
            for i, (n, a, b) in enumerate(((P, 0, NT), (TS, NT, NT + 1))):
                nc.gpsimd.tensor_tensor(r[0:n, a:b, :], mean[0:n, a:b, :], C["mhalf"][0:n, 0:1].unsqueeze(2).to_broadcast([n, b - a, DH]), ALU.pow).then_inc(r_done, 1)
            pool.wait_ge(loaded, 16)
            for c, n, o, z in tiles:
                pool.wait_ge(silu_done, c + 1)
                nc.gpsimd.tensor_tensor(z, z, gain[0:n, :].unsqueeze(1).to_broadcast([n, DH, P]), ALU.mult).then_inc(zg_done, 1)

        @block.vector
        def _(dve):
            step = Steps(dve, dve_step)
            for c, n, o, z in tiles:
                dve.wait_ge(sq_done, c + 1)
                nc.vector.tensor_reduce(ss[0:n, c, :], sq[0:n, c % 2], AX.X, ALU.add).then_inc(ss_done, 1)
            dve.wait_ge(ss_done, NT + 1)
            for n, a, b in ((P, 0, NT), (TS, NT, NT + 1)):
                nc.vector.tensor_scalar(mean[0:n, a:b, :], ss[0:n, a:b, :], 1.0 / DD, EPS, ALU.mult, ALU.add).then_inc(mean_done, 1)
            dve.wait_ge(r_done, 2)
            for c, n, o, z in tiles:
                if c >= 2:
                    dve.wait_ge(tp_done, c - 1)
                step(nc.vector.tensor_tensor(y[0:n, c % 2], o, r[0:n, c, :].unsqueeze(2).to_broadcast([n, DH, P]), ALU.mult))
                dve.wait_ge(zg_done, c + 1)
                nc.vector.tensor_tensor(y[0:n, c % 2], y[0:n, c % 2], z, ALU.mult).then_inc(y_done, 1)

        @block.tensor
        def _(pe):
            for c, n, o, z in tiles:
                pe.wait_ge(y_done, c + 1)
                if c >= 2:
                    pe.wait_ge(copied, c - 1)
                for h in range(DH):
                    ins = nc.tensor.transpose(PS[c % 2][:, h * P:h * P + n], y[0:n, c % 2, h, :], C["ident"][0:n, 0:n])
                ins.then_inc(tp_done, 1)


GROUPS = ((Q0, 8, 0), (KS0, 2, 8), (KW0, 2, 10))


def block_qk(nc, L, PS, C, q_norm, k_norm, state_win, R, Rs, gates_p, gates_s, qT, kT, kv_p, kv_s, win_p, win_s):
    ctx = ExitStack()
    with ctx:
        sem = L.signals.named("q_")
        loaded, sq_done, ss_done, mean_done, r_done, gain_ready, x_done, xg_done, rope_done, tp_done, act_copied, dve_copied, stored, passed, dve_step = map(
            sem, ("loaded", "sq", "ss", "mean", "r", "gain", "x", "xg", "rope", "tp", "act_copied", "dve_copied", "stored", "passed", "dve_step"))
        T = Region(L, A_MID, A_OA)
        gain = T("q_gain", [P, 3, HD])
        ss, mean, r = (T("q_" + n, [P, NT + 1, 12]) for n in ("ss", "mean", "r"))
        sq = T("q_sq", [P, 2, 12, HD])
        T = Region(L, A_FREE, A_SMALL)
        rot = [T(f"q_rot{i}", [P, NT, 8, ROT]) for i in range(4)]
        cases = [(c, P, R[:, c, :]) for c in range(NT)] + [(NT, TS, Rs[:, :])]
        spans = ((P, 0, NT), (TS, NT, NT + 1))
        heads = lambda x, at, n: x[:, at:at + n * HD].rearrange("p (h d) -> p h d", d=HD)
        block = ctx.enter_context(nc.Block())

        @block.sync
        def _(sp):
            sp.dma_start(gain[:, 0, :], q_norm.unsqueeze(0).to_broadcast([P, HD])).then_inc(loaded, 16)
            sp.dma_start(gain[:, 1, :], k_norm[0].unsqueeze(0).to_broadcast([P, HD])).then_inc(loaded, 16)
            sp.dma_start(gain[:, 2, :], k_norm[1].unsqueeze(0).to_broadcast([P, HD])).then_inc(loaded, 16)
            sp.dma_start(win_s[:, 0:WIN - 1], state_win[:, 1:WIN]).then_inc(passed, 16)
            sp.wait_ge(rope_done, 6)
            sp.dma_start(kv_p.rearrange("(t p) c -> p t c", p=P), R[:, :, KC0:KW0]).then_inc(stored, 16)
            sp.dma_start(kv_s, Rs[:, KC0:KW0]).then_inc(stored, 16)
            sp.dma_start(win_p.rearrange("(t p) c -> p t c", p=P), R[:, NT - WIN // P:NT, KW0:NG0]).then_inc(stored, 16)
            sp.dma_start(win_s[:, WIN - 1], Rs[:, KW0:NG0]).then_inc(stored, 16)
            sp.wait_ge(stored, 64)
            sp.wait_ge(passed, 16)

        @block.gpsimd
        def _(pool):
            for c, n, x in cases:
                if c >= 2:
                    pool.wait_ge(ss_done, c - 1)
                for at, h, slot in GROUPS:
                    ins = nc.gpsimd.tensor_tensor(sq[0:n, c % 2, slot:slot + h, :], heads(x, at, h), heads(x, at, h), ALU.mult)
                ins.then_inc(sq_done, 1)
            pool.wait_ge(mean_done, 2)
            for n, a, b in spans:
                nc.gpsimd.tensor_tensor(r[0:n, a:b, :], mean[0:n, a:b, :], C["mhalf"][0:n, 0:1].unsqueeze(2).to_broadcast([n, b - a, 12]), ALU.pow).then_inc(r_done, 1)
            pool.wait_ge(gain_ready, 1)
            for c, n, x in cases:
                pool.wait_ge(x_done, c + 1)
                for i, (at, h, slot) in enumerate(GROUPS):
                    ins = nc.gpsimd.tensor_tensor(heads(x, at, h), heads(x, at, h), gain[0:n, i:i + 1, :].to_broadcast([n, h, HD]), ALU.mult)
                ins.then_inc(xg_done, 1)

        @block.vector
        def _(dve):
            step = Steps(dve, dve_step)
            dve.wait_ge(loaded, 48)
            nc.vector.tensor_scalar(gain[:, 0, :], gain[:, 0, :], HD ** -0.5, None, ALU.mult).then_inc(gain_ready, 1)
            for c, n, x in cases:
                dve.wait_ge(sq_done, c + 1)
                nc.vector.tensor_reduce(ss[0:n, c, :], sq[0:n, c % 2], AX.X, ALU.add).then_inc(ss_done, 1)
            dve.wait_ge(ss_done, NT + 1)
            for n, a, b in spans:
                nc.vector.tensor_scalar(mean[0:n, a:b, :], ss[0:n, a:b, :], 1.0 / HD, EPS, ALU.mult, ALU.add).then_inc(mean_done, 1)
            dve.wait_ge(r_done, 2)
            for c, n, x in cases:
                for at, h, slot in GROUPS:
                    ins = nc.vector.tensor_tensor(heads(x, at, h), heads(x, at, h), r[0:n, c, slot:slot + h].unsqueeze(2).to_broadcast([n, h, HD]), ALU.mult)
                ins.then_inc(x_done, 1)
            dve.wait_ge(xg_done, NT + 1)
            for i, (at, h, slot) in enumerate(GROUPS):
                for n, t0, t1, x in ((P, 0, NT, R[:, :, at:at + h * HD]), (TS, NT, NT + 1, Rs[:, at:at + h * HD].unsqueeze(1))):
                    x = x.rearrange("p t (h d) -> p t h d", d=HD)
                    nt = t1 - t0
                    cos, sin = (C[k][0:n, ROT * t0:ROT * t1].rearrange("p (t d) -> p t d", d=ROT).unsqueeze(2).to_broadcast([n, nt, h, ROT]) for k in ("cos", "sin"))
                    a, b = x[:, :, :, 0:ROT], x[:, :, :, ROT:2 * ROT]
                    ra, rb, rc, rd = (t[0:n, 0:nt, 0:h, :] for t in rot)
                    nc.vector.tensor_tensor(ra, a, cos, ALU.mult)
                    nc.vector.tensor_tensor(rb, b, sin, ALU.mult)
                    nc.vector.tensor_tensor(rc, b, cos, ALU.mult)
                    step(nc.vector.tensor_tensor(rd, a, sin, ALU.mult))
                    nc.vector.tensor_tensor(a, ra, rb, ALU.subtract)
                    ins = nc.vector.tensor_tensor(b, rc, rd, ALU.add)
                    ins.then_inc(rope_done, 1)
                    dve.wait_ge(rope_done, 2 * i + (1 if t0 == 0 else 2))
            for c, n, x in cases:
                dve.wait_ge(tp_done, 2 * c + 2)
                nc.vector.tensor_copy(kT[:, :, c * P:c * P + n], PS[2 * (c % 2) + 1][:, :].rearrange("p (j n) -> p j n", j=4)[:, :, 0:n]).then_inc(dve_copied, 1)

        @block.tensor
        def _(pe):
            pe.wait_ge(rope_done, 6)
            for c, n, x in cases:
                if c >= 2:
                    pe.wait_ge(act_copied, c - 1)
                for j in range(4):
                    pair = x[:, j * P:(j + 1) * P]
                    ins = nc.tensor.transpose(PS[2 * (c % 2)][:, j * P:j * P + n], pair, C["ident"][0:n, 0:n])
                ins.then_inc(tp_done, 1)
                if c >= 2:
                    pe.wait_ge(dve_copied, c - 1)
                for j, at in enumerate((KS0, KW0, KC0, VC0)):
                    ins = nc.tensor.transpose(PS[2 * (c % 2) + 1][:, j * P:j * P + n], x[:, at:at + P], C["ident"][0:n, 0:n])
                ins.then_inc(tp_done, 1)

        @block.scalar
        def _(act):
            nc.scalar.activation(gates_p[:, :, :], R[:, :, NG0:RAB], ACT.Sigmoid)
            nc.scalar.activation(gates_s[:, :], Rs[:, NG0:RAB], ACT.Sigmoid)
            for c, n, x in cases:
                act.wait_ge(tp_done, 2 * c + 1)
                nc.scalar.copy(qT[:, :, c * P:c * P + n], PS[2 * (c % 2)][:, :].rearrange("p (j n) -> p j n", j=4)[:, :, 0:n]).then_inc(act_copied, 1)


def load_cmp_weights(nc, engine, i, w_cmp, wbd, zeroed, loaded):
    engine.wait_ge(zeroed, 1)
    for g in range(2):
        engine.dma_start(wbd[64 * g:64 * g + 64, :, 64 * g:64 * g + 64], w_cmp[i].rearrange("l d e -> d l e")).then_inc(loaded, 16)


def block_compress_prompt(nc, L, PS, C, cmp_pos, w_cmp, kT, cpos, kv_cmp):
    ctx = ExitStack()
    with ctx:
        sem = L.signals.named("m_")
        pos_loaded, pos_tp, pos_copied, zeroed0, zeroed1, w_loaded0, w_loaded1, mm_done, c_done, c_copied = map(
            sem, ("pos_loaded", "pos_tp", "pos_copied", "zeroed0", "zeroed1", "w_loaded0", "w_loaded1", "mm", "c", "c_copied"))
        wbd = [L.at("m_wk", A_MID, [P, 32, P]), L.at("m_wv", A_OA, [P, 32, P])]
        T = Region(L, A_FREE, A_SMALL)
        pos = T("m_pos", [64, P])
        posT = T("m_posT", [P, 64])
        block = ctx.enter_context(nc.Block())

        @block.gpsimd
        def _(pool):
            nc.gpsimd.memset(wbd[0][:, :, :], 0.0).then_inc(zeroed0, 1)

        @block.sync
        def _(sp):
            for g in range(2):
                sp.dma_start(pos[:, 64 * g:64 * g + 64], cmp_pos.rearrange("i l d -> (i l) d")).then_inc(pos_loaded, 16)
            load_cmp_weights(nc, sp, 0, w_cmp, wbd[0], zeroed0, w_loaded0)
            load_cmp_weights(nc, sp, 1, w_cmp, wbd[1], zeroed1, w_loaded1)

        @block.tensor
        def _(pe):
            pe.wait_ge(pos_loaded, 32)
            nc.tensor.transpose(PS[0][:, 0:64], pos[:, :], C["ident"][0:64, 0:64]).then_inc(pos_tp, 1)
            pe.wait_ge(pos_copied, 1)
            for i in range(2):
                pe.wait_ge((w_loaded0, w_loaded1)[i], 32)
                for l in range(32):
                    nc.tensor.matmul(PS[1 + i][:, 0:P], posT[:, 32 * i + l:32 * i + l + 1].to_broadcast([P, P]), wbd[i][:, l, :], start=(l == 0), stop=(l == 31))
                for l in range(32):
                    ins = nc.tensor.matmul(PS[3 + i][0:NCP, 0:P], kT[:, 2 + i, l:l + 16 * (NCP - 1) + 1:16], wbd[i][:, l, :], start=(l == 0), stop=(l == 31))
                ins.then_inc(mm_done, 1)

        @block.vector
        def _(dve):
            nc.vector.memset(wbd[1][:, :, :], 0.0).then_inc(zeroed1, 1)
            dve.wait_ge(pos_tp, 1)
            nc.vector.tensor_copy(posT[:, :], PS[0][:, 0:64]).then_inc(pos_copied, 1)
            for i in range(2):
                dve.wait_ge(mm_done, i + 1)
                nc.vector.tensor_copy(cpos[:, i, :], PS[1 + i][:, 0:P]).then_inc(c_copied, 1)
                dve.wait_ge(c_copied, i + 1)
                nc.vector.tensor_tensor(kv_cmp[0:NCP, i, :], PS[3 + i][0:NCP, 0:P], cpos[0:NCP, i, :], ALU.add)


def block_cmp_norm(nc, L, PS, C, k_gain, n, B, kc, kcT, base, end, bank=0):
    ctx = ExitStack()
    with ctx:
        sem = L.signals.named(f"r{B}_")
        loaded, mean_done, r_done, k_ready, tp_done, copied, dve_step = map(sem, ("loaded", "mean", "r", "k_ready", "tp", "copied", "dve_step"))
        T = Region(L, base, end)
        gain = T("r_gain", [P, HD])
        sq = T("r_sq", [P, 2 * B, HD])
        mean, r = T("r_mean", [P, 2 * B]), T("r_r", [P, 2 * B])
        rot = [T(f"r_rot{i}", [P, 2 * B, ROT]) for i in range(4)]
        x = kc.rearrange("p b (g d) -> p (b g) d", d=HD)
        block = ctx.enter_context(nc.Block())

        @block.sync
        def _(sp):
            sp.dma_start(gain[:, :], k_gain.unsqueeze(0).to_broadcast([P, HD])).then_inc(loaded, 16)

        @block.gpsimd
        def _(pool):
            pool.wait_ge(mean_done, 1)
            nc.gpsimd.tensor_tensor(r[0:n, :], mean[0:n, :], C["mhalf"][0:n, 0:1].to_broadcast([n, 2 * B]), ALU.pow).then_inc(r_done, 1)

        @block.vector
        def _(dve):
            step = Steps(dve, dve_step)
            step(nc.vector.tensor_tensor(sq[0:n], x, x, ALU.mult))
            step(nc.vector.tensor_reduce(mean[0:n, :], sq[0:n], AX.X, ALU.add))
            nc.vector.tensor_scalar(mean[0:n, :], mean[0:n, :], 1.0 / HD, EPS, ALU.mult, ALU.add).then_inc(mean_done, 1)
            dve.wait_ge(r_done, 1)
            dve.wait_ge(loaded, 16)
            step(nc.vector.tensor_tensor(x, x, r[0:n, :].unsqueeze(2).to_broadcast([n, 2 * B, HD]), ALU.mult))
            step(nc.vector.tensor_tensor(x, x, gain[0:n, :].unsqueeze(1).to_broadcast([n, 2 * B, HD]), ALU.mult))
            cos, sin = (C[k][0:n, :].unsqueeze(1).to_broadcast([n, 2 * B, ROT]) for k in ("ccos", "csin"))
            a, b = x[:, :, 0:ROT], x[:, :, ROT:2 * ROT]
            ra, rb, rc, rd = (t[0:n] for t in rot)
            nc.vector.tensor_tensor(ra, a, cos, ALU.mult)
            nc.vector.tensor_tensor(rb, b, sin, ALU.mult)
            nc.vector.tensor_tensor(rc, b, cos, ALU.mult)
            step(nc.vector.tensor_tensor(rd, a, sin, ALU.mult))
            nc.vector.tensor_tensor(a, ra, rb, ALU.subtract)
            nc.vector.tensor_tensor(b, rc, rd, ALU.add).then_inc(k_ready, 1)
            for s in range(B):
                dve.wait_ge(tp_done, s + 1)
                nc.vector.tensor_copy(kcT[:, s, 0:n], PS[bank + s % 2][:, 0:n]).then_inc(copied, 1)

        @block.tensor
        def _(pe):
            pe.wait_ge(k_ready, 1)
            for s in range(B):
                if s >= 2:
                    pe.wait_ge(copied, s - 1)
                nc.tensor.transpose(PS[bank + s % 2][:, 0:n], kc[:, s, :], C["ident"][0:n, 0:n]).then_inc(tp_done, 1)


def block_attend_prompt(nc, L, PS, C, qT, kT, kcT, kv_cmp, R, gates, oaT):
    NWT = WIN // P
    SEL, WINB, CMP, PW = 0, TP, TP + (NWT + 1) * P, TP + (NWT + 1) * P + 64
    ctx = ExitStack()
    with ctx:
        sem = L.signals.named("a_")
        s_done, max_done, exp_done, scale_ready, scaled, tp_done, act_pt, dve_pt, pv_done, o_copied, dve_step = map(
            sem, ("s", "max", "exp", "scale", "scaled", "tp", "act_pt", "dve_pt", "pv", "o_copied", "dve_step"))
        T = Region(L, A_MID - 2 * TT * 4, A_OA)
        Pb = [T(f"a_P{i}", [P, PW]) for i in range(2)]
        small = T("a_small", [P, 2, 16])
        T = Region(L, A_FREE, A_SMALL)
        PT = [T(f"a_PT{i}", [P, 14 * P]) for i in range(2)]
        SLOT = (1, 2, 0)
        units = [(i, g, j) for i in range(NT) for g in range(2) for j in range(4)]

        def parts(i):
            lo = max(0, i - NWT)
            return lo, ((SEL, (i + 1) * P), (WINB, (i + 1 - lo) * P), (CMP, NCP))

        def blocks(i):
            lo, _ = parts(i)
            return ([(SEL + k * P, P, 0, k) for k in range(i + 1)] + [(WINB + (k - lo) * P, P, 1, k) for k in range(lo, i + 1)]
                    + [(CMP, NCP, 2, 0)])

        def quads(i):
            b = blocks(i)
            return [b[k:k + 4] for k in range(0, len(b), 4)]

        S = PS[8]
        sview = {0: lambda n: S[:, 0:n], 1: lambda n: S[:, 1024:1024 + n], 2: lambda n: S[:, 1024 + 640:1024 + 640 + n]}
        first_quad = []
        n = 0
        for i, g, j in units:
            first_quad.append(n)
            n += len(quads(i))
        block = ctx.enter_context(nc.Block())

        @block.tensor
        def _(pe):
            def scores(u):
                i, g, j = units[u]
                if u:
                    pe.wait_ge(exp_done, u)
                rows = slice(64 * g, 64 * g + 64)
                q = qT[rows, j, i * P:(i + 1) * P]
                lo, _ = parts(i)
                for branch, first, last in ((0, 0, i), (1, lo, i)):
                    width = (last + 1 - first) * P
                    for c0 in range(0, width, 512):
                        w = min(512, width - c0)
                        out = sview[branch](width)[:, c0:c0 + w]
                        masks = []
                        if c0 + w == width:
                            masks.append((w - P, "causal"))
                        if branch == 1 and i - first == NWT and c0 == 0:
                            masks.append((0, "edge"))
                        nc.tensor.matmul(out, q, kT[rows, branch, first * P + c0:first * P + c0 + w], start=True, stop=not masks)
                        for m, (at, name) in enumerate(masks):
                            nc.tensor.matmul(out[:, at:at + P], C["ident"], C[name], start=False, stop=(m == len(masks) - 1))
                nc.tensor.matmul(sview[2](NCP), q, kcT[rows, 0, 0:NCP], start=True, stop=False)
                nc.tensor.matmul(sview[2](NCP), C["ident"], C["cmpmask"][:, 64 * i:64 * i + NCP], start=False, stop=True).then_inc(s_done, 1)

            def values(u):
                i, g, j = units[u]
                pe.wait_ge(scaled, u + 1)
                f = first_quad[u]
                for n, quad in enumerate(quads(i)):
                    if f + n >= 2:
                        m = f + n - 2
                        pe.wait_ge((act_pt, dve_pt)[m % 2], m // 2 + 1)
                    for k, (at, keys, _, _) in enumerate(quad):
                        ins = nc.tensor.transpose(PS[4 + (f + n) % 2][0:keys, k * P:(k + 1) * P], Pb[u % 2][:, at:at + keys], C["ident"])
                    ins.then_inc(tp_done, 1)
                out = PS[6 + (u // 4) % 2]
                if j == 0 and u >= 8:
                    pe.wait_ge(o_copied, u // 4 - 1)
                b = blocks(i)
                for n, quad in enumerate(quads(i)):
                    pe.wait_ge((act_pt, dve_pt)[(f + n) % 2], (f + n) // 2 + 1)
                    for k, (at, keys, branch, kt) in enumerate(quad):
                        v = kv_cmp[0:NCP, 1, :] if branch == 2 else R[:, kt, (VS0, VW0)[branch]:(VS0, VW0)[branch] + P]
                        x = 4 * n + k
                        ins = nc.tensor.matmul(out[:, j * P:(j + 1) * P], v, PT[u % 2][0:keys, x * P:(x + 1) * P], start=(x == 0), stop=(x == len(b) - 1))
                ins.then_inc(pv_done, 1)

            scores(0)
            for u in range(len(units)):
                if u + 1 < len(units):
                    scores(u + 1)
                values(u)

        def copy_quad(engine, u, n, quad, done):
            engine.wait_ge(tp_done, first_quad[u] + n + 1)
            if n <= 1 and u >= 2:
                engine.wait_ge(pv_done, u - 1)
            src = PS[4 + (first_quad[u] + n) % 2]
            full = len([b for b in quad if b[1] == P])
            ins = None
            pieces = []
            if full:
                pieces.append((P, 0, full))
            if full < len(quad):
                pieces.append((NCP, full, full + 1))
            for rows, a, b in pieces:
                dst, s = PT[u % 2][0:rows, (4 * n + a) * P:(4 * n + b) * P], src[0:rows, a * P:b * P]
                ins = nc.scalar.copy(dst, s) if done is act_pt else nc.vector.tensor_copy(dst, s)
            ins.then_inc(done, 1)

        @block.vector
        def _(dve):
            def maxima(u):
                i, g, j = units[u]
                dve.wait_ge(s_done, u + 1)
                if u >= 2:
                    dve.wait_ge(exp_done, u - 1)
                for b, (at, n) in enumerate(parts(i)[1]):
                    ins = nc.vector.tensor_reduce(small[:, u % 2, SLOT[b]:SLOT[b] + 1], sview[b](n), AX.X, ALU.max, negate=True)
                ins.then_inc(max_done, 1)

            def factors(u):
                i, g, j = units[u]
                dve.wait_ge(exp_done, u + 1)
                s = small[:, u % 2, :]
                step(nc.vector.reciprocal(s[:, 8:11], s[:, 4:7]))
                if i == 0:
                    step(nc.vector.tensor_scalar(s[:, 8:9], s[:, 8:9], C["cmpvalid"], None, ALU.mult))
                if u >= 2:
                    dve.wait_ge(scaled, u - 1)
                nc.vector.tensor_tensor(s[:, 12:15], s[:, 8:11], gates[:, i, 3 * (4 * g + j):3 * (4 * g + j) + 3], ALU.mult).then_inc(scale_ready, 1)

            def output(u):
                i, g, j = units[u]
                dve.wait_ge(pv_done, u + 1)
                rows = slice(64 * g, 64 * g + 64)
                nc.vector.tensor_copy(oaT[rows, :, i * P:(i + 1) * P], PS[6 + (u // 4) % 2][rows, :].rearrange("p (j n) -> p j n", j=4)).then_inc(o_copied, 1)

            step = Steps(dve, dve_step)
            maxima(0)
            factors(0)
            for u in range(len(units)):
                if u + 1 < len(units):
                    maxima(u + 1)
                for n, quad in enumerate(quads(units[u][0])):
                    if (first_quad[u] + n) % 2:
                        copy_quad(dve, u, n, quad, dve_pt)
                if u + 1 < len(units):
                    factors(u + 1)
                if u % 4 == 3:
                    output(u)

        @block.scalar
        def _(act):
            def exps(u):
                i, g, j = units[u]
                act.wait_ge(max_done, u + 1)
                if u >= 2:
                    act.wait_ge(scale_ready, u - 1)
                    act.wait_ge(tp_done, first_quad[u - 1])
                s = small[:, u % 2, :]
                for b, (at, n) in enumerate(parts(i)[1]):
                    ins = nc.scalar.activation(Pb[u % 2][:, at:at + n], sview[b](n), ACT.Exp, bias=s[:, SLOT[b]:SLOT[b] + 1], accum_out=s[:, 4 + SLOT[b]:5 + SLOT[b]])
                ins.then_inc(exp_done, 1)

            exps(0)
            for u in range(len(units)):
                if u + 1 < len(units):
                    exps(u + 1)
                for n, quad in enumerate(quads(units[u][0])):
                    if (first_quad[u] + n) % 2 == 0:
                        copy_quad(act, u, n, quad, act_pt)

        @block.gpsimd
        def _(pool):
            for u, (i, g, j) in enumerate(units):
                pool.wait_ge(scale_ready, u + 1)
                for b, (at, n) in enumerate(parts(i)[1]):
                    p = Pb[u % 2][:, at:at + n]
                    ins = nc.gpsimd.tensor_scalar(p, p, small[:, u % 2, 12 + SLOT[b]:13 + SLOT[b]], None, ALU.mult)
                ins.then_inc(scaled, 1)


def block_window_keys(nc, L, PS, C, state_win, page_table, qT, kT, gates_s, qbd, snew, g64, pages, sw):
    ctx = ExitStack()
    with ctx:
        sem = L.signals.named("w_")
        zeroed, qbd_ready, loaded, other_loaded, tp_done, act_copied, dve_copied, s_done, new_done = map(
            sem, ("zeroed", "qbd", "loaded", "other_loaded", "tp", "act_copied", "dve_copied", "s", "new"))
        kw = L.at("w_k", A_R, [P, TS, WIN // P, P])
        kwT = L.at("w_kT", A_R + 16384, [P, TS, WIN])
        block = ctx.enter_context(nc.Block())

        @block.sync
        def _(sp):
            for b in range(TS):
                sp.dma_start(kw[:, b], state_win[b, :, 0:P].rearrange("(t p) c -> p t c", p=P)).then_inc(loaded, 16)
            sp.dma_start(pages[:, :], page_table.rearrange("(a b) n -> a (b n)", a=1)).then_inc(other_loaded, 16)
            sp.dma_start(g64[:, :], gates_s[:, :].rearrange("b (h i) -> b h i", i=3)).then_inc(other_loaded, 16)
            sp.wait_ge(other_loaded, 32)

        @block.gpsimd
        def _(pool):
            nc.gpsimd.memset(qbd[:, :, :], 0.0).then_inc(zeroed, 1)
            pool.wait_ge(zeroed, 1)
            for b in range(TS):
                nc.gpsimd.tensor_copy(qbd[0:64, b, 8 * b:8 * b + 4], qT[0:64, :, TP + b])
                ins = nc.gpsimd.tensor_copy(qbd[64:P, b, 8 * b + 4:8 * b + 8], qT[64:P, :, TP + b])
            ins.then_inc(qbd_ready, 1)

        @block.tensor
        def _(pe):
            pe.wait_ge(loaded, 16 * TS)
            for b in range(TS):
                if b >= 4:
                    pe.wait_ge((act_copied, dve_copied)[b % 2], (b - 4) // 2 + 1)
                for t in range(WIN // P):
                    ins = nc.tensor.transpose(PS[b % 4][:, t * P:(t + 1) * P], kw[:, b, t, :], C["ident"])
                ins.then_inc(tp_done, 1)
            pe.wait_ge(qbd_ready, 1)
            for b in range(TS):
                nc.tensor.matmul(PS[5][0:64, 0:2], qbd[:, b, :], kT[:, 0:2, TP + b], start=(b == 0), stop=(b == TS - 1))
            for b in range(TS):
                pe.wait_ge((act_copied, dve_copied)[b % 2], b // 2 + 1)
                ins = nc.tensor.matmul(PS[4][0:64, :], qbd[:, b, :], kwT[:, b, :], start=(b == 0), stop=(b == TS - 1))
            ins.then_inc(s_done, 1)

        @block.scalar
        def _(act):
            for b in range(0, TS, 2):
                act.wait_ge(tp_done, b + 1)
                nc.scalar.copy(kwT[:, b, :], PS[b % 4]).then_inc(act_copied, 1)

        @block.vector
        def _(dve):
            for b in range(1, TS, 2):
                dve.wait_ge(tp_done, b + 1)
                nc.vector.tensor_copy(kwT[:, b, :], PS[b % 4]).then_inc(dve_copied, 1)
            dve.wait_ge(s_done, 1)
            nc.vector.tensor_copy(snew[:, :], PS[5][0:64, 0:2]).then_inc(new_done, 1)
            dve.wait_ge(new_done, 1)
            nc.vector.tensor_copy(sw[:, 0:WIN], PS[4][0:64, :])
            nc.vector.tensor_copy(sw[:, WIN:WIN + 1], snew[:, 1:2])


def block_cache_keys(nc, L, PS, C, cache, pages, w_cmp, cpos, qbd, kcs, vcs):
    HP = NPAGE // 2
    ctx = ExitStack()
    with ctx:
        sem = L.signals.named("k_")
        loaded = [sem(f"loaded{i}") for i in range(3)]
        zeroed, w_loaded, tp_done, act_copied, dve_copied, cmp_done, s_done, c_copied = map(
            sem, ("zeroed", "w_loaded", "tp", "act_copied", "dve_copied", "cmp", "s", "c_copied"))
        X = Region(L, A_R, A_RS)
        wbd = [X(f"k_wbd{i}", [P, 32, P]) for i in range(2)]
        T3 = X("k_T3", [P, 3, PAST])
        stage = [L.at(f"k_stage{i}", A_DN + 12288 * i, [P, HP, 3, P]) for i in range(3)]
        steps = [(b, half) for b in range(TS) for half in range(2)]
        def copies(engine, parity, done):
            n = 0
            for s, (b, half) in enumerate(steps):
                for i in range(3):
                    for quad in range(2):
                        if n % 2 == parity:
                            engine.wait_ge(tp_done, n + 1)
                            if half == 0 and b and i == 0:
                                engine.wait_ge(s_done, b)
                            dst, src = T3[:, i, 1024 * half + 512 * quad:1024 * half + 512 * quad + 512], PS[4 + n % 2]
                            ins = nc.scalar.copy(dst, src) if parity == 0 else nc.vector.tensor_copy(dst, src)
                            ins.then_inc(done, 1)
                        n += 1
                if half and parity:
                    engine.wait_ge(cmp_done, b + 1)
                    nc.vector.tensor_tensor(kcs[0:NCS, b, :], PS[6][0:NCS, 0:P], cpos[0:NCS, 0, :], ALU.add).then_inc(c_copied, 1)
                    nc.vector.tensor_tensor(vcs[0:NCS, b, :], PS[7][0:NCS, 0:P], cpos[0:NCS, 1, :], ALU.add).then_inc(c_copied, 1)

        block = ctx.enter_context(nc.Block())

        @block.gpsimd
        def _(pool):
            for i in range(2):
                nc.gpsimd.memset(wbd[i][:, :, :], 0.0).then_inc(zeroed, 1)

        @block.scalar
        def _(act):
            act.wait_ge(zeroed, 2)
            for i in range(2):
                load_cmp_weights(nc, act, i, w_cmp, wbd[i], zeroed, w_loaded)
            copies(act, 0, act_copied)

        @block.sync
        def _(sp):
            for s, (b, half) in enumerate(steps):
                if s >= 3:
                    sp.wait_ge(tp_done, 6 * (s - 2))
                for p in range(HP):
                    page = sp.value_load(pages[0:1, NPAGE * b + HP * half + p:NPAGE * b + HP * half + p + 1], min_val=0, max_val=cache.shape[0] - 1)
                    sp.dma_start(stage[s % 3][:, p], cache[bass.ds(page, 1), :, 0:3 * P].rearrange("a t (i c) -> (a t) i c", c=P)).then_inc(loaded[s % 3], 16)

        @block.tensor
        def _(pe):
            n = 0
            for s, (b, half) in enumerate(steps):
                pe.wait_ge(loaded[s % 3], 16 * HP * (s // 3 + 1))
                for i in range(3):
                    for quad in range(2):
                        if n >= 2:
                            pe.wait_ge((act_copied, dve_copied)[n % 2], (n - 2) // 2 + 1)
                        for p in range(4):
                            ins = nc.tensor.transpose(PS[4 + n % 2][:, p * P:(p + 1) * P], stage[s % 3][:, 4 * quad + p, i, :], C["ident"])
                        ins.then_inc(tp_done, 1)
                        n += 1
                if half:
                    pe.wait_ge(act_copied, n // 2)
                    pe.wait_ge(dve_copied, n // 2)
                    if b == 0:
                        pe.wait_ge(w_loaded, 64)
                    else:
                        pe.wait_ge(c_copied, 2 * b)
                    for i in range(2):
                        for l in range(32):
                            ins = nc.tensor.matmul(PS[6 + i][0:NCS, 0:P], T3[:, i, l:l + 16 * (NCS - 1) + 1:16], wbd[i][:, l, :], start=(l == 0), stop=(l == 31))
                    ins.then_inc(cmp_done, 1)
                    for c in range(4):
                        ins = nc.tensor.matmul(PS[c][0:64, :], qbd[:, b, :], T3[:, 2, 512 * c:512 * c + 512], start=(b == 0), stop=(b == TS - 1))
                    ins.then_inc(s_done, 1)

        @block.vector
        def _(dve):
            copies(dve, 1, dve_copied)


def block_attend_sample(nc, L, PS, C, cache, pages, state_win, kcsT, vcs, qbd, snew, g64, sw, Rs, oaT):
    ctx = ExitStack()
    with ctx:
        sem = L.signals.named("b_")
        v_loaded, vw_loaded = sem("v_loaded"), sem("vw_loaded")
        c_done, grouped, g_copied, imp_done, ct_done, ct_copied, pd_done, pd_copied, pt_done, act_pt, dve_pt, o_done = map(
            sem, ("c", "grouped", "g_copied", "imp", "ct", "ct_copied", "pd", "pd_copied", "pt", "act_pt", "dve_pt", "o"))
        max_done, exp_done, p_ready, pg_ready, act_step, dve_step, pd_ready = map(
            sem, ("max", "exp", "p_ready", "pg_ready", "act_step", "dve_step", "pd_ready"))
        X = Region(L, A_R, A_RS)
        v_lo = X("b_vlo", [P, 4, NPAGE, P])
        ss = X("b_ss", [64, PAST + 1])
        PT = X("b_PT", [P, NPAGE, 64])
        wT = X("b_wT", [P, WIN // P, 64])
        pc, pcg, pgT, pcT = X("b_pc", [64, P]), X("b_pcg", [64, P]), X("b_pgT", [P, 64]), X("b_pcT", [P, 64])
        score, top, msk = X("b_score", [64, 3, 40]), X("b_top", [64, 2, 8]), X("b_msk", [64, 40])
        st, pdd, pd = X("b_st", [64, 16]), X("b_pdd", [64, 2, 64]), X("b_pd", [TS, 2, 64])
        v_hi = L.at("b_vhi", A_DN, [P, 4, NPAGE, P])
        vw_lo = L.at("b_vwlo", A_DN + 32768, [P, TS - 1, WIN // P, P])
        vw_hi = X("b_vwhi", [P, 1, WIN // P, P])
        NW = WIN // P
        block = ctx.enter_context(nc.Block())

        @block.sync
        def _(sp):
            for b in range(TS):
                dst = vw_lo[:, b] if b < TS - 1 else vw_hi[:, 0]
                sp.dma_start(dst, state_win[b, :, P:2 * P].rearrange("(t p) c -> p t c", p=P)).then_inc(vw_loaded, 16)
                v = v_lo[:, b] if b < 4 else v_hi[:, b - 4]
                for p in range(NPAGE):
                    page = sp.value_load(pages[0:1, NPAGE * b + p:NPAGE * b + p + 1], min_val=0, max_val=cache.shape[0] - 1)
                    sp.dma_start(v[:, p, :], cache[bass.ds(page, 1), :, 3 * P:4 * P].rearrange("a t c -> (a t) c")).then_inc(v_loaded, 16)

        @block.tensor
        def _(pe):
            for b in range(TS):
                ins = nc.tensor.matmul(PS[6][0:64, 0:NCS], qbd[:, b, :], kcsT[:, b, 0:NCS], start=(b == 0), stop=(b == TS - 1))
            ins.then_inc(c_done, 1)
            pe.wait_ge(p_ready, 1)
            nc.tensor.matmul(PS[5][0:NCS, 0:64], pc[:, 0:NCS], C["group"][0:64, :], start=True, stop=True).then_inc(grouped, 1)
            pe.wait_ge(pg_ready, 1)
            nc.tensor.transpose(PS[7][0:NCS, 0:64], pcg[:, 0:NCS], C["ident"][0:64, 0:64]).then_inc(ct_done, 1)
            pe.wait_ge(g_copied, 1)
            nc.tensor.matmul(PS[6][0:64, 0:NSEL], pgT[0:NCS, :], C["ovl"][0:NCS, :], start=True, stop=True).then_inc(imp_done, 1)
            pe.wait_ge(pd_ready, 2)
            for h in range(2):
                for t in range(8):
                    k = 8 * h + t
                    ins = nc.tensor.transpose(PS[4 + h][:, t * 64:(t + 1) * 64], ss[:, k * P:(k + 1) * P], C["ident"][0:64, 0:64])
                ins.then_inc(pt_done, 1)
            for t in range(NW):
                ins = nc.tensor.transpose(PS[0][:, t * 64:(t + 1) * 64], sw[:, t * P:(t + 1) * P], C["ident"][0:64, 0:64])
            ins.then_inc(pt_done, 1)
            nc.tensor.matmul(PS[6][0:TS, 0:P], C["seq"][0:64, :], pdd[:, :, :].rearrange("r i c -> r (i c)"), start=True, stop=True).then_inc(pd_done, 1)
            pe.wait_ge(pd_copied, 1)
            pe.wait_ge(ct_copied, 1)
            out = PS[7][:, 0:64]
            nc.tensor.matmul(out, Rs[:, VS0:VS0 + P], pd[:, 0, :], start=True, stop=False)
            nc.tensor.matmul(out, Rs[:, VW0:VW0 + P], pd[:, 1, :], start=False, stop=False)
            pe.wait_ge(act_pt, 1)
            pe.wait_ge(dve_pt, 2)
            pe.wait_ge(vw_loaded, 16 * TS)
            pe.wait_ge(v_loaded, 16 * TS * NPAGE)
            for b in range(TS):
                cols = slice(8 * b, 8 * b + 8)
                o = out[:, cols]
                v = v_lo[:, b] if b < 4 else v_hi[:, b - 4]
                w = vw_lo[:, b] if b < TS - 1 else vw_hi[:, 0]
                for t in range(NPAGE):
                    nc.tensor.matmul(o, v[:, t, :], PT[:, t, cols], start=False, stop=False)
                for t in range(NW):
                    nc.tensor.matmul(o, w[:, t, :], wT[:, t, cols], start=False, stop=False)
                ins = nc.tensor.matmul(o, vcs[0:NCS, b, :], pcT[0:NCS, cols], start=False, stop=(b == TS - 1))
            ins.then_inc(o_done, 1)

        @block.scalar
        def _(act):
            act.wait_ge(max_done, 1)
            nc.scalar.activation(pc[:, 0:NCS], PS[6][0:64, 0:NCS], ACT.Exp, bias=st[:, 0:1], accum_out=st[:, 1:2]).then_inc(exp_done, 1)
            act.wait_ge(grouped, 1)
            nc.scalar.copy(pgT[0:NCS, :], PS[5][0:NCS, 0:64]).then_inc(g_copied, 1)
            act.wait_ge(ct_done, 1)
            nc.scalar.copy(pcT[0:NCS, :], PS[7][0:NCS, 0:64]).then_inc(ct_copied, 1)
            act.wait_ge(max_done, 2)
            nc.scalar.activation(sw[:, 1:WIN + 1], sw[:, 1:WIN + 1], ACT.Exp, bias=st[:, 4:5], accum_out=st[:, 6:7]).then_inc(exp_done, 1)
            act.wait_ge(max_done, 3)
            nc.scalar.activation(ss[:, :], ss[:, :], ACT.Exp, bias=st[:, 3:4], accum_out=st[:, 5:6]).then_inc(exp_done, 1)
            act.wait_ge(pt_done, 1)
            nc.scalar.copy(PT[:, 0:8, :], PS[4][:, :].rearrange("p (t r) -> p t r", r=64)).then_inc(act_pt, 1)

        @block.vector
        def _(dve):
            step = Steps(dve, dve_step)
            dve.wait_ge(c_done, 1)
            nc.vector.tensor_reduce(st[:, 0:1], PS[6][0:64, 0:NCS], AX.X, ALU.max, negate=True).then_inc(max_done, 1)
            nc.vector.tensor_reduce(st[:, 4:5], sw[:, 1:WIN + 1], AX.X, ALU.max, negate=True).then_inc(max_done, 1)
            dve.wait_ge(exp_done, 1)
            step(nc.vector.reciprocal(st[:, 2:3], st[:, 1:2]))
            nc.vector.tensor_scalar(pc[:, 0:NCS], pc[:, 0:NCS], st[:, 2:3], None, ALU.mult).then_inc(p_ready, 1)
            dve.wait_ge(p_ready, 1)
            nc.vector.tensor_scalar(pcg[:, 0:NCS], pc[:, 0:NCS], g64[:, 0:1], None, ALU.mult).then_inc(pg_ready, 1)
            dve.wait_ge(imp_done, 1)
            step(nc.vector.tensor_tensor(score[:, 0, 0:NSEL], PS[6][0:64, 0:NSEL], C["bonus"][0:64, :], ALU.add))
            for r in range(2):
                step(nc.vector.max(top[:, r, :], score[:, r, 0:NSEL]))
                step(nc.vector.match_replace(score[:, r + 1, 0:NSEL], top[:, r, :], score[:, r, 0:NSEL], -BIG))
            step(nc.vector.tensor_scalar(msk[:, 0:NSEL], score[:, 2, 0:NSEL], -BIG, None, ALU.is_equal))
            step(nc.vector.tensor_scalar(msk[:, 0:NSEL], msk[:, 0:NSEL], -1.0, BIG, ALU.add, ALU.mult))
            nc.vector.tensor_tensor(ss[:, 0:PAST].rearrange("r (s k) -> r s k", k=64), PS[8][0:64, 0:PAST].rearrange("r (s k) -> r s k", k=64),
                                    msk[:, 0:NSEL - 1].unsqueeze(2).to_broadcast([64, NSEL - 1, 64]), ALU.add)
            step(nc.vector.tensor_tensor(ss[:, PAST:PAST + 1], snew[:, 0:1], msk[:, NSEL - 1:NSEL], ALU.add))
            nc.vector.tensor_reduce(st[:, 3:4], ss[:, :], AX.X, ALU.max, negate=True).then_inc(max_done, 1)
            dve.wait_ge(exp_done, 3)
            step(nc.vector.reciprocal(st[:, 8:10], st[:, 5:7]))
            step(nc.vector.tensor_tensor(st[:, 10:12], st[:, 8:10], g64[:, 1:3], ALU.mult))
            nc.vector.memset(sw[:, 0:1], 0.0)
            step(nc.vector.tensor_scalar(ss[:, :], ss[:, :], st[:, 10:11], None, ALU.mult))
            step(nc.vector.tensor_scalar(sw[:, 1:WIN + 1], sw[:, 1:WIN + 1], st[:, 11:12], None, ALU.mult))
            nc.vector.tensor_scalar(pdd[:, 0, :], C["ident"][0:64, 0:64], ss[:, PAST:PAST + 1], None, ALU.mult).then_inc(pd_ready, 1)
            nc.vector.tensor_scalar(pdd[:, 1, :], C["ident"][0:64, 0:64], sw[:, WIN:WIN + 1], None, ALU.mult).then_inc(pd_ready, 1)
            dve.wait_ge(pt_done, 2)
            nc.vector.tensor_copy(PT[:, 8:16, :], PS[5][:, :].rearrange("p (t r) -> p t r", r=64)).then_inc(dve_pt, 1)
            dve.wait_ge(pt_done, 3)
            nc.vector.tensor_copy(wT[:, :, :], PS[0][:, 0:64 * NW].rearrange("p (t r) -> p t r", r=64)).then_inc(dve_pt, 1)
            dve.wait_ge(pd_done, 1)
            nc.vector.tensor_copy(pd[:, :, :], PS[6][0:TS, 0:P].rearrange("b (i r) -> b i r", r=64)).then_inc(pd_copied, 1)
            dve.wait_ge(o_done, 1)
            o = PS[7][:, 0:64].rearrange("p (b h) -> p h b", h=NH)
            for g in range(2):
                nc.vector.tensor_copy(oaT[64 * g:64 * g + 64, :, TP:TT], o[64 * g:64 * g + 64, 4 * g:4 * g + 4, :])


def block_merge(nc, L, PS, C, w_in, w_a, w_b, hT, oaT, obT, mixed):
    ctx = ExitStack()
    with ctx:
        sem = L.signals.named("x_")
        wab_loaded, mm_done, sig_done, t_done, m_done = map(sem, ("wab_loaded", "mm", "sig", "t", "m"))
        g_loaded = [sem(f"g_loaded{i}") for i in range(3)]
        wa = L.at("x_wa", A_R, [P, 4, D])
        wb = L.at("x_wb", A_R + 16384, [P, 4, D])
        T = Region(L, A_R + 32768, A_R + 41856)
        sg = [T(f"x_sig{i}", [P, 2, 512]) for i in range(2)]
        wg = [L.at(f"x_wg{i}", A_DN + 16384 * i, [P, KD, 2, 256]) for i in range(3)]
        wv = w_in.rearrange("(k p) n -> p k n", p=P)
        chunks = ((0, 512), (512, 512), (TP, TS))
        units = [(m, t0, n) for m in range(KD) for t0, n in chunks]
        block = ctx.enter_context(nc.Block())

        @block.sync
        def _(sp):
            for g in range(2):
                sp.dma_start(wa[64 * g:64 * g + 64, :, :], w_a[256 * g:256 * g + 256].rearrange("(j d) n -> d j n", d=HD)).then_inc(wab_loaded, 16)
            for q in range(4):
                if q == 1:
                    sp.dma_start(wb[:, :, :], w_b.rearrange("(j p) n -> p j n", p=P)).then_inc(wab_loaded, 16)
                if q >= 3:
                    sp.wait_ge(mm_done, 6 * (q - 2))
                for i, at in enumerate((MA0, MB0)):
                    sp.dma_start(wg[q % 3][:, :, i, :], wv[:, :, at + 256 * q:at + 256 * q + 256]).then_inc(g_loaded[q % 3], 16)

        @block.tensor
        def _(pe):
            for u, (m, t0, n) in enumerate(units):
                q, c = m // 2, 128 * (m % 2)
                if m % 2 == 0 and t0 == 0:
                    pe.wait_ge(g_loaded[q % 3], 32 * (q // 3 + 1))
                b = 4 * (u % 2)
                if u >= 2:
                    pe.wait_ge(t_done, 2 * (u - 1))
                for i in range(2):
                    for k in range(KD):
                        ins = nc.tensor.matmul(PS[b + i][:, 0:n], wg[q % 3][:, k, i, c:c + P], hT[:, k, t0:t0 + n], start=(k == 0), stop=(k == KD - 1))
                if u == 0:
                    pe.wait_ge(wab_loaded, 48)
                for i, (w, o) in enumerate(((wa, oaT), (wb, obT))):
                    for k in range(4):
                        ins = nc.tensor.matmul(PS[b + 2 + i][:, 0:n], w[:, k, m * P:(m + 1) * P], o[:, k, t0:t0 + n], start=(k == 0), stop=(k == 3))
                ins.then_inc(mm_done, 1)

        @block.scalar
        def _(act):
            for u, (m, t0, n) in enumerate(units):
                act.wait_ge(mm_done, u + 1)
                if u >= 2:
                    act.wait_ge(m_done, u - 1)
                for i in range(2):
                    nc.scalar.activation(sg[u % 2][:, i, 0:n], PS[4 * (u % 2) + i][:, 0:n], ACT.Sigmoid).then_inc(sig_done, 1)

        @block.vector
        def _(dve):
            for u, (m, t0, n) in enumerate(units):
                for i in range(2):
                    dve.wait_ge(sig_done, 2 * u + i + 1)
                    nc.vector.tensor_tensor(sg[u % 2][:, i, 0:n], sg[u % 2][:, i, 0:n], PS[4 * (u % 2) + 2 + i][:, 0:n], ALU.mult).then_inc(t_done, 1)

        @block.gpsimd
        def _(pool):
            for u, (m, t0, n) in enumerate(units):
                pool.wait_ge(t_done, 2 * u + 2)
                nc.gpsimd.tensor_tensor(mixed[m][:, t0:t0 + n], sg[u % 2][:, 0, 0:n], sg[u % 2][:, 1, 0:n], ALU.add).then_inc(m_done, 1)


def block_out(nc, L, PS, C, x_p, x_s, w_out, norm_ffn, w_rg, w_re, b_rg, b_re, mixed, x1, h2_rows, logits):
    ctx = ExitStack()
    with ctx:
        sem = L.signals.named("o_")
        w_loaded, small_loaded, zeroed, zero_stored, mm_done, x1_done, sq_done, mean_done, r_done, xn_done, h2_done, tp_done, h2T_done, lg_done, lg_copied, bias_done = map(
            sem, ("w_loaded", "small", "zeroed", "zero_stored", "mm", "x1", "sq", "mean", "r", "xn", "h2", "tp", "h2T", "lg", "lg_copied", "bias"))
        x_loaded = [sem("x_loaded0"), sem("x_loaded1")]
        h2_stored = [sem("h2_stored0"), sem("h2_stored1")]
        wo = L.at("o_w", A_HT, [P, KD, D])
        Y = Region(L, A_DN, A_OA)
        x = Y("o_x", [P, 2, D])
        junk = Y("o_junk", [P, D])
        h2 = Y("o_h2", [P, 2, D])
        h2T = Y("o_h2T", [P, 2, KD, P])
        gain = Y("o_gain", [P, D])
        wr = Y("o_wr", [P, KD, NG + NE])
        bias = Y("o_bias", [P, NG + NE])
        zrow = Y("o_zero", [1, D])
        ss, mean, r = Y("o_ss", [P, 16]), Y("o_mean", [P, 16]), Y("o_r", [P, 16])
        tiles = [(t, P) for t in range(NT)] + [(NT, TS)]
        block = ctx.enter_context(nc.Block())

        def store(sp, t):
            n = tiles[t][1]
            sp.wait_ge(h2_done, t + 1)
            sp.dma_start(h2_rows[t * P:t * P + n, :], h2[0:n, t % 2, :]).then_inc(h2_stored[t % 2], 16)

        @block.sync
        def _(sp):
            for t, n in tiles:
                if t >= 2:
                    sp.wait_ge(x1_done, t - 1)
                src = x_p[0, t * P:(t + 1) * P, :] if t < NT else x_s[:, 0, :]
                sp.dma_start(x[0:n, t % 2, :], src).then_inc(x_loaded[t % 2], 16)
                if t == 0:
                    sp.dma_start(wo[:, :, :], w_out.rearrange("(k p) n -> p k n", p=P)).then_inc(w_loaded, 16)
                    sp.dma_start(gain[:, :], norm_ffn.unsqueeze(0).to_broadcast([P, D])).then_inc(small_loaded, 16)
                    sp.dma_start(wr[:, :, 0:NG], w_rg.rearrange("(k p) n -> p k n", p=P)).then_inc(small_loaded, 16)
                    sp.dma_start(wr[:, :, NG:NG + NE], w_re.rearrange("(k p) n -> p k n", p=P)).then_inc(small_loaded, 16)
                    sp.dma_start(bias[:, 0:NG], b_rg.unsqueeze(0).to_broadcast([P, NG])).then_inc(small_loaded, 16)
                    sp.dma_start(bias[:, NG:NG + NE], b_re.unsqueeze(0).to_broadcast([P, NE])).then_inc(small_loaded, 16)
                if t >= 1:
                    store(sp, t - 1)
            store(sp, NT)
            sp.wait_ge(h2_stored[0], 16 * 5)
            sp.wait_ge(h2_stored[1], 16 * 4)
            sp.wait_ge(zeroed, 1)
            sp.dma_start(h2_rows[TT:TT + 1, :], zrow[:, :]).then_inc(zero_stored, 16)
            sp.wait_ge(zero_stored, 16)

        @block.tensor
        def _(pe):
            def project(t, n):
                if t >= 2:
                    pe.wait_ge(x1_done, t - 1)
                for half in range(2):
                    for k in range(KD):
                        ins = nc.tensor.matmul(PS[2 * (t % 2) + half][0:n, :], mixed[k][:, t * P:t * P + n], wo[:, k, 512 * half:512 * half + 512], start=(k == 0), stop=(k == KD - 1))
                ins.then_inc(mm_done, 1)

            pe.wait_ge(w_loaded, 16)
            project(0, P)
            for t, n in tiles:
                if t + 1 < len(tiles):
                    project(*tiles[t + 1])
                pe.wait_ge(h2_done, t + 1)
                if t >= 1:
                    pe.wait_ge(h2T_done, t)
                for k in range(KD):
                    ins = nc.tensor.transpose(PS[4 + k // 4][:, (k % 4) * P:(k % 4) * P + n], h2[0:n, t % 2, k * P:(k + 1) * P], C["ident"][0:n, 0:n])
                ins.then_inc(tp_done, 1)
                pe.wait_ge(h2T_done, t + 1)
                if t == 0:
                    pe.wait_ge(small_loaded, 80)
                if t >= 2:
                    pe.wait_ge(lg_copied, t - 1)
                for k in range(KD):
                    ins = nc.tensor.matmul(PS[6 + t % 2][0:n, 0:NG + NE], h2T[:, t % 2, k, 0:n], wr[:, k, :], start=(k == 0), stop=(k == KD - 1))
                ins.then_inc(lg_done, 1)

        @block.vector
        def _(dve):
            nc.vector.memset(zrow[:, :], 0.0).then_inc(zeroed, 1)
            nc.vector.memset(logits[:, NT, :], 0.0).then_inc(zeroed, 1)
            dve.wait_ge(zeroed, 2)

            def copy_logits(t, n):
                dve.wait_ge(lg_done, t + 1)
                nc.vector.tensor_tensor(logits[0:n, t, :], PS[6 + t % 2][0:n, 0:NG + NE], bias[0:n, :], ALU.add).then_inc(lg_copied, 1)

            dve.wait_ge(small_loaded, 80)
            for t, n in tiles:
                dve.wait_ge(mm_done, t + 1)
                dve.wait_ge(x_loaded[t % 2], 16 * (t // 2 + 1))
                for half in range(2):
                    s = slice(512 * half, 512 * half + 512)
                    ins = nc.vector.tensor_tensor(x1[0:n, t, s], PS[2 * (t % 2) + half][0:n, :], x[0:n, t % 2, s], ALU.add)
                ins.then_inc(x1_done, 1)
                dve.wait_ge(r_done, t + 1)
                if t >= 2:
                    dve.wait_ge(h2_stored[t % 2], 16 * (t // 2))
                    dve.wait_ge(tp_done, t - 1)
                nc.vector.tensor_scalar(h2[0:n, t % 2, :], x1[0:n, t, :], r[0:n, t:t + 1], None, ALU.mult).then_inc(xn_done, 1)
                if t >= 1:
                    copy_logits(*tiles[t - 1])
            copy_logits(*tiles[NT])

        @block.scalar
        def _(act):
            for t, n in tiles:
                act.wait_ge(x1_done, t + 1)
                if t >= 1:
                    act.wait_ge(sq_done, t)
                nc.scalar.activation(junk[0:n, :], x1[0:n, t, :], ACT.Square, accum_out=ss[0:n, t:t + 1]).then_inc(sq_done, 1)
                act.wait_ge(tp_done, t + 1)
                if t >= 2:
                    act.wait_ge(lg_done, t - 1)
                for half in range(2):
                    ins = nc.scalar.copy(h2T[:, t % 2, 4 * half:4 * half + 4, 0:n], PS[4 + half][:, :].rearrange("p (k n) -> p k n", k=4)[:, :, 0:n])
                ins.then_inc(h2T_done, 1)

        @block.gpsimd
        def _(pool):
            pool.wait_ge(small_loaded, 80)
            for t, n in tiles:
                pool.wait_ge(sq_done, t + 1)
                nc.gpsimd.tensor_scalar(mean[0:n, t:t + 1], ss[0:n, t:t + 1], 1.0 / D, EPS, ALU.mult, ALU.add).then_inc(mean_done, 1)
                pool.wait_ge(mean_done, t + 1)
                nc.gpsimd.tensor_tensor(r[0:n, t:t + 1], mean[0:n, t:t + 1], C["mhalf"][0:n, 0:1], ALU.pow).then_inc(r_done, 1)
                pool.wait_ge(xn_done, t + 1)
                nc.gpsimd.tensor_tensor(h2[0:n, t % 2, :], h2[0:n, t % 2, :], gain[0:n, :], ALU.mult).then_inc(h2_done, 1)


def block_route(nc, L, PS, C, logits, slot, weight, blocks, table):
    NT1 = NT + 1
    TILES = [(t, P) for t in range(NT)] + [(NT, TS)]
    ctx = ExitStack()
    with ctx:
        sem = L.signals.named("t_")
        step_sem, exp_in, exp_done, a_ready, rank_done, filled, fill_ready, slot_ready, scattered = map(
            sem, ("step", "exp_in", "exp", "a_ready", "rank", "filled", "fill_ready", "slot_ready", "scattered"))
        Y = Region(L, A_DN, A_OA)
        g, e = logits[:, :, 0:NG], logits[:, :, NG:NG + NE]
        N = lambda name, n: Y("t_" + name, [P, NT1, n])
        mx, gi, den = N("mx", 1), N("gi", 1), N("den", 1)
        ga, gb = N("ga", NG), N("gb", NG)
        le, tmp, tmp2 = N("le", NE), N("tmp", NE), N("tmp2", NE)
        oh = [N("oh1", NE), N("oh2", NE)]
        m1, m2, ei = N("m1", 1), N("m2", 1), N("ei", 1)
        A = N("A", NE)
        ex, w1 = N("ex", 1), N("w1", 1)
        count, nb, end, end2, start = (Y("t_" + s, [P, NE]) for s in ("count", "nb", "end", "end2", "start"))
        cmpb = Y("t_cmp", [P, NE, NT1])
        eb = Y("t_eb", [P, MAXBLK, NE])
        ebs = Y("t_ebs", [P, MAXBLK])
        slotf = Y("t_slotf", [P, NT1, 2])
        fill = Y("t_fill", [P, MAXBLK + 1, 2], I32)
        tok = Y("t_tok", [P, NT1, 2, 2], I32)
        b3 = lambda x, n: x.to_broadcast([P, NT1, n])
        block = ctx.enter_context(nc.Block())

        @block.vector
        def _(dve):
            step = Steps(dve, step_sem)
            V = nc.vector
            ids = C["eid"].unsqueeze(1)

            def first_max(x, n, idx, onehot, scratch, m):
                step(V.tensor_reduce(m[:, :, 0], x, AX.X, ALU.max))
                step(V.tensor_tensor(scratch, x, b3(m[:, :, :], n), ALU.not_equal))
                step(V.scalar_tensor_tensor(scratch, scratch, 100.0, ids[:, :, 0:n].to_broadcast([P, NT1, n]), ALU.mult, ALU.add))
                step(V.tensor_reduce(idx[:, :, 0], scratch, AX.X, ALU.min))
                step(V.tensor_tensor(onehot, ids[:, :, 0:n].to_broadcast([P, NT1, n]), b3(idx[:, :, :], n), ALU.is_equal))

            V.memset(fill[:, :, 0], TT).then_inc(fill_ready, 1)
            V.memset(fill[:, :, 1], 2 * TT).then_inc(fill_ready, 1)
            V.tensor_copy(tok[:, :, :, :], C["tok"].rearrange("p (t k c) -> p t k c", k=2, c=2)).then_inc(fill_ready, 1)
            first_max(g, NG, gi, gb[:, :, :], ga[:, :, :], mx)
            V.tensor_tensor(ga[:, :, :], g, b3(mx[:, :, :], NG), ALU.subtract).then_inc(exp_in, 1)
            step(V.tensor_scalar(gb[:, :, :], gb[:, :, :], -1.0, BIG, ALU.add, ALU.mult))
            for t in range(NT1):
                ins = V.tensor_tensor(le[:, t, :].rearrange("p (g e) -> p g e", g=NG), e[:, t, :].rearrange("p (g e) -> p g e", g=NG),
                                      gb[:, t, :].unsqueeze(2).to_broadcast([P, NG, EPG]), ALU.add)
                if t == NT1 - 1:
                    step(ins)
            first_max(le[:, :, :], NE, ei, oh[0][:, :, :], tmp[:, :, :], m1)
            step(V.scalar_tensor_tensor(tmp2[:, :, :], oh[0][:, :, :], -3.0 * BIG, le[:, :, :], ALU.mult, ALU.add))
            first_max(tmp2[:, :, :], NE, ei, oh[1][:, :, :], tmp[:, :, :], m2)
            V.tensor_tensor(ex[:, :, :], m2[:, :, :], m1[:, :, :], ALU.subtract).then_inc(exp_in, 1)
            step(V.tensor_tensor(A[:, :, :], oh[0][:, :, :], oh[1][:, :, :], ALU.add))
            V.tensor_tensor(A[:, NT, :], A[:, NT, :], C["tokvalid"].to_broadcast([P, NE]), ALU.mult).then_inc(a_ready, 1)
            dve.wait_ge(exp_done, 2)
            step(V.tensor_reduce(den[:, :, 0], ga[:, :, :], AX.X, ALU.add))
            step(V.tensor_scalar(w1[:, :, :], ex[:, :, :], 1.0, None, ALU.add))
            step(V.tensor_tensor(w1[:, :, :], w1[:, :, :], den[:, :, :], ALU.mult))
            step(V.reciprocal(weight[:, :, 0], w1[:, :, 0]))
            step(V.tensor_tensor(weight[:, :, 1], weight[:, :, 0], ex[:, :, 0], ALU.mult))
            dve.wait_ge(rank_done, 1)
            step(V.tensor_copy(count[:, :], PS[1][:, 0:NE]))
            step(V.tensor_tensor(cmpb[:, :, :], count[:, :].unsqueeze(2).to_broadcast([P, NE, NT1]), C["blk"][:, 0:NT1].unsqueeze(1).to_broadcast([P, NE, NT1]), ALU.is_gt))
            step(V.tensor_reduce(nb[:, :], cmpb[:, :, :], AX.X, ALU.add))
            cur, nxt = nb, end
            for s in (1, 2, 4, 8, 16):
                V.tensor_copy(nxt[:, 0:s], cur[:, 0:s])
                step(V.tensor_tensor(nxt[:, s:NE], cur[:, s:NE], cur[:, 0:NE - s], ALU.add))
                cur, nxt = nxt, (end2 if nxt is end else end)
            step(V.tensor_tensor(start[:, :], cur[:, :], nb[:, :], ALU.subtract))
            step(V.tensor_scalar(start[:, :], start[:, :], float(P), None, ALU.mult))
            step(V.tensor_tensor(tmp[:, :, :], PS[0][:, 0:NT1 * NE].rearrange("p (t e) -> p t e", e=NE), start[:, :].unsqueeze(1).to_broadcast([P, NT1, NE]), ALU.add))
            for k in range(2):
                step(V.tensor_tensor(tmp2[:, :, :], tmp[:, :, :], oh[k][:, :, :], ALU.mult))
                step(V.tensor_reduce(slotf[:, :, k], tmp2[:, :, :], AX.X, ALU.add))
            V.tensor_copy(slot[:, :, :], slotf[:, :, :]).then_inc(slot_ready, 1)
            step(V.tensor_tensor(eb[:, :, :], cur[:, :].unsqueeze(1).to_broadcast([P, MAXBLK, NE]), C["blkid"].unsqueeze(2).to_broadcast([P, MAXBLK, NE]), ALU.is_le))
            step(V.tensor_reduce(ebs[:, :], eb[:, :, :], AX.X, ALU.add))
            step(V.tensor_scalar(ebs[:, :], ebs[:, :], float(NE - 1), None, ALU.min))
            V.tensor_copy(blocks[0:1, 0:MAXBLK], ebs[0:1, :])
            V.tensor_copy(blocks[0:1, MAXBLK:MAXBLK + 1], cur[0:1, NE - 1:NE])

        @block.scalar
        def _(act):
            act.wait_ge(exp_in, 1)
            nc.scalar.activation(ga[:, :, :], ga[:, :, :], ACT.Exp).then_inc(exp_done, 1)
            act.wait_ge(exp_in, 2)
            nc.scalar.activation(ex[:, :, :], ex[:, :, :], ACT.Exp).then_inc(exp_done, 1)

        @block.tensor
        def _(pe):
            pe.wait_ge(a_ready, 1)
            for t in range(NT1):
                for s in range(t):
                    nc.tensor.matmul(PS[0][:, NE * t:NE * (t + 1)], C["ones"], A[:, s, :], start=(s == 0), stop=False)
                nc.tensor.matmul(PS[0][:, NE * t:NE * (t + 1)], C["strictT"], A[:, t, :], start=(t == 0), stop=True)
            for t in range(NT1):
                ins = nc.tensor.matmul(PS[1][:, 0:NE], C["ones"], A[:, t, :], start=(t == 0), stop=(t == NT1 - 1))
            ins.then_inc(rank_done, 1)

        @block.gpsimd
        def _(pool):
            pool.wait_ge(fill_ready, 3)
            pool.dma_start(table.rearrange("(p b) c -> p b c", p=P), fill[:, :, :]).then_inc(filled, 16)
            pool.wait_ge(filled, 16)
            pool.wait_ge(slot_ready, 1)
            for t, n in TILES:
                for k in range(2):
                    pool.indirect_dma_start(out=table, out_offset=bass.IndirectOffsetOnAxis(ap=slot[0:n, t, k:k + 1], axis=0),
                                            in_=tok[0:n, t, k, :], in_offset=None).then_inc(scattered, 16)
            pool.wait_ge(scattered, 16 * 2 * NT1)


def block_experts(nc, L, PS, C, w_gate, w_up, w_down, h2_rows, table, blocks, expert_out):
    ctx = ExitStack()
    with ctx:
        sem = L.signals.named("f_")
        slots_loaded = sem("slots")
        (gu_loaded, d_loaded, x_loaded, stored, gidx_ready, sidx_ready, tp_done, xT_act, xT_dve, gu_done, silu_done, a_done, atp_done,
         aT_done, down_done, out_act, out_dve, out_free) = ([sem(n + str(i)) for i in range(2)] for n in (
             "gu_loaded", "d_loaded", "x_loaded", "stored", "gidx", "sidx", "tp", "xT_act", "xT_dve", "gu", "silu", "a", "atp",
             "aT", "down", "out_act", "out_dve", "out_free"))
        W = [L.at(f"f_W{i}", A_R + 36864 + 49152 * i, [P, 3 * 4096]) for i in range(2)]
        wg, wu = ([w[:, o:o + 4096].rearrange("p (k n) -> p k n", k=KD) for w in W] for o in (0, 4096))
        wd = [w[:, 8192:12288].rearrange("p (k n) -> p k n", k=4) for w in W]
        T = Region(L, A_HT, A_CONST)
        x = [T(f"f_x{i}", [P, D]) for i in range(2)]
        xT = [T(f"f_xT{i}", [P, KD, P]) for i in range(2)]
        sg, a = T("f_sg", [P, FE]), T("f_a", [P, FE])
        aT = T("f_aT", [P, 4, P])
        out = [T(f"f_out{i}", [P, D]) for i in range(2)]
        tokens = L.at("f_tokens", A_R + 36864 + 98304, [P, MAXBLK + 1, 2], I32)
        gidx, sidx = (L.at(f"f_idx{i}", A_R + 36864 + 98304 + 416 + 32 * i, [P, 2, 2], I32) for i in range(2))
        wgv, wuv = (w.rearrange("e (k p) n -> e p k n", p=P) for w in (w_gate, w_up))
        wdv = w_down.rearrange("e (k p) n -> e p k n", p=P)
        block = ctx.enter_context(nc.Block())

        def each_block(engine, body):
            n = engine.value_load(blocks[0:1, MAXBLK:MAXBLK + 1], min_val=MINBLK, max_val=MAXBLK)
            with engine.Fori(0, MAXBLK // 2) as i:
                for par in range(2):
                    with engine.If(2 * i + par < n):
                        body(i, par)
            return n

        @block.sync
        def _(sp):
            for pair in (gu_done, down_done, tp_done, out_act, out_dve, out_free):
                for s in pair:
                    sp.sem_inc(s, 1)

            def body(i, par):
                e = sp.value_load(blocks[0:1, bass.ds(2 * i + par, 1)], min_val=0, max_val=NE - 1)
                sp.wait_ge(gu_done[par], i + 1)
                for dst, src in ((wg[par], wgv), (wu[par], wuv)):
                    sp.dma_start(dst, src[bass.ds(e, 1)].rearrange("a p k n -> (a p) k n")).then_inc(gu_loaded[par], 16)
                sp.wait_ge(down_done[par], i + 1)
                sp.dma_start(wd[par], wdv[bass.ds(e, 1)].rearrange("a p k n -> (a p) k n")).then_inc(d_loaded[par], 16)

            each_block(sp, body)

        @block.gpsimd
        def _(pool):
            pool.dma_start(tokens[:, :, :], table.rearrange("(b p) c -> p b c", p=P), allow_slow_non_contiguous=True).then_inc(slots_loaded, 16)
            pool.wait_ge(slots_loaded, 16)
            turn = pool.alloc_register("turn")

            def gather(count, par, b):
                nc.gpsimd.tensor_copy(gidx[:, par, :], tokens[:, bass.ds(b, 1), :].rearrange("p b c -> p (b c)")).then_inc(gidx_ready[par], 1)
                pool.wait_ge(slots_loaded, 16)
                pool.wait_ge(gidx_ready[par], count)
                pool.indirect_dma_start(out=x[par][:, :], out_offset=None, in_=h2_rows,
                                        in_offset=bass.IndirectOffsetOnAxis(ap=gidx[:, par, 0:1], axis=0)).then_inc(x_loaded[par], 16)

            gather(1, 0, 0)

            def body(i, par):
                pool.reg_mov(turn, i + par + 1)
                count = pool.snap(turn)
                pool.wait_ge(tp_done[1 - par], count)
                gather(count, 1 - par, 2 * i + par + 1)
                nc.gpsimd.tensor_copy(sidx[:, par, :], tokens[:, bass.ds(2 * i + par, 1), :].rearrange("p b c -> p (b c)")).then_inc(sidx_ready[par], 1)
                pool.wait_ge(sidx_ready[par], i + 1)
                pool.wait_ge(out_act[par], i + 2)
                pool.reg_mov(turn, i + 2)
                count = pool.snap(turn)
                pool.wait_ge(slots_loaded, 16)
                pool.wait_ge(out_dve[par], count)
                pool.indirect_dma_start(out=expert_out, out_offset=bass.IndirectOffsetOnAxis(ap=sidx[:, par, 1:2], axis=0),
                                        in_=out[par][:, :], in_offset=None).then_inc(stored[par], 16)
                pool.wait_ge(stored[par], 16 * (i + 1))
                pool.sem_inc(out_free[par], 1)

            n = each_block(pool, body)
            pool.wait_ge(x_loaded[0], n // 2 * 16 + 16)
            pool.wait_ge(x_loaded[1], (n + 1) // 2 * 16)

        @block.tensor
        def _(pe):
            def transpose_rows(par, count):
                pe.wait_ge(x_loaded[par], count)
                for k in range(KD):
                    ins = nc.tensor.transpose(PS[k // 4][:, (k % 4) * P:(k % 4 + 1) * P], x[par][:, k * P:(k + 1) * P], C["ident"])
                ins.then_inc(tp_done[par], 1)

            def body(i, par):
                pe.wait_ge(xT_act[par], i + 1)
                pe.wait_ge(xT_dve[par], i + 1)
                pe.wait_ge(gu_loaded[par], 32 * i + 32)
                for w, bank in ((wg, 2), (wu, 3)):
                    for k in range(KD):
                        ins = nc.tensor.matmul(PS[bank][:, :], xT[par][:, k, :], w[par][:, k, :], start=(k == 0), stop=(k == KD - 1))
                ins.then_inc(gu_done[par], 1)
                transpose_rows(1 - par, 16 * (i + par + 1))
                pe.wait_ge(a_done[par], i + 1)
                for k in range(4):
                    ins = nc.tensor.transpose(PS[4][:, k * P:(k + 1) * P], a[:, k * P:(k + 1) * P], C["ident"])
                ins.then_inc(atp_done[par], 1)
                pe.wait_ge(aT_done[par], i + 1)
                pe.wait_ge(d_loaded[par], 16 * i + 16)
                pe.wait_ge(out_act[1 - par], i + par + 1)
                pe.wait_ge(out_dve[1 - par], i + par + 1)
                for half in range(2):
                    for k in range(4):
                        ins = nc.tensor.matmul(PS[5 + half][:, :], aT[:, k, :], wd[par][:, k, 512 * half:512 * half + 512], start=(k == 0), stop=(k == 3))
                ins.then_inc(down_done[par], 1)

            transpose_rows(0, 16)
            each_block(pe, body)

        @block.scalar
        def _(act):
            def copy_rows(par, count):
                act.wait_ge(tp_done[par], count)
                nc.scalar.copy(xT[par][:, 0:4, :], PS[0][:, :].rearrange("p (k n) -> p k n", k=4)).then_inc(xT_act[par], 1)

            def body(i, par):
                act.wait_ge(gu_done[par], i + 2)
                nc.scalar.activation(sg[:, :], PS[2][:, :], ACT.Silu).then_inc(silu_done[par], 1)
                copy_rows(1 - par, i + par + 2)
                act.wait_ge(down_done[par], i + 2)
                act.wait_ge(out_free[par], i + 1)
                nc.scalar.copy(out[par][:, 0:512], PS[5][:, :]).then_inc(out_act[par], 1)

            copy_rows(0, 2)
            each_block(act, body)

        @block.vector
        def _(dve):
            def copy_rows(par, count):
                dve.wait_ge(tp_done[par], count)
                nc.vector.tensor_copy(xT[par][:, 4:8, :], PS[1][:, :].rearrange("p (k n) -> p k n", k=4)).then_inc(xT_dve[par], 1)

            def body(i, par):
                dve.wait_ge(silu_done[par], i + 1)
                nc.vector.tensor_tensor(a[:, :], sg[:, :], PS[3][:, :], ALU.mult).then_inc(a_done[par], 1)
                dve.wait_ge(atp_done[par], i + 1)
                nc.vector.tensor_copy(aT[:, :, :], PS[4][:, :].rearrange("p (k n) -> p k n", k=4)).then_inc(aT_done[par], 1)
                copy_rows(1 - par, i + par + 2)
                dve.wait_ge(down_done[par], i + 2)
                dve.wait_ge(out_free[par], i + 1)
                nc.vector.tensor_copy(out[par][:, 512:1024], PS[6][:, :]).then_inc(out_dve[par], 1)

            copy_rows(0, 2)
            each_block(dve, body)


def block_combine(nc, L, C, weight, x1, expert_out, y_p, y_s):
    ctx = ExitStack()
    with ctx:
        sem = L.signals.named("z_")
        got = [sem(f"got{i}") for i in range(3)]
        stored = [sem("stored0"), sem("stored1")]
        y_done, step_sem = sem("y_done"), sem("step")
        T = Region(L, A_HT, A_CONST)
        r = [T(f"z_r{i}", [P, 2, D]) for i in range(3)]
        tiles = [(t, P) for t in range(NT)] + [(NT, TS)]
        rows = expert_out[0:2 * TT].rearrange("(k t) n -> t k n", k=2)
        block = ctx.enter_context(nc.Block())

        @block.scalar
        def _(act):
            for t, n in tiles:
                if t >= 3:
                    act.wait_ge(y_done, t - 2)
                act.dma_start(r[t % 3][0:n, :, :], rows[t * P:t * P + n]).then_inc(got[t % 3], 16)

        @block.vector
        def _(dve):
            step = Steps(dve, step_sem)
            for t, n in tiles:
                dve.wait_ge(got[t % 3], 16 * (t // 3 + 1))
                x = x1[0:n, t, :]
                step(nc.vector.scalar_tensor_tensor(x, r[t % 3][0:n, 0, :], weight[0:n, t, 0:1], x, ALU.mult, ALU.add))
                nc.vector.scalar_tensor_tensor(x, r[t % 3][0:n, 1, :], weight[0:n, t, 1:2], x, ALU.mult, ALU.add).then_inc(y_done, 1)

        @block.sync
        def _(sp):
            for t, n in tiles:
                sp.wait_ge(y_done, t + 1)
                dst = y_p[0, t * P:(t + 1) * P, :] if t < NT else y_s[:, 0, :]
                sp.dma_start(dst, x1[0:n, t, :]).then_inc(stored[t % 2], 16)
            sp.wait_ge(stored[0], 16 * 5)
            sp.wait_ge(stored[1], 16 * 4)


def load_constants(nc, L, table):
    t = L.at("constants", A_CONST, [P, CONST.shape[1]])
    with nc.semaphore("constants_loaded") as loaded, nc.Block() as block:
        @block.sync
        def _(sp):
            sp.dma_start(t[:, :], table).then_inc(loaded, 16)
            sp.wait_ge(loaded, 16)
    return {name: t[:, a:a + n] for name, (a, n) in WHERE.items()}


def build(nc, I, O):
    L = Layout(nc)
    whole = nc.alloc_psum_tensor("psum", [P, 4096], F32)
    PS = [whole[:, 512 * i:512 * i + 512] for i in range(8)] + [whole[:, :]]
    C = load_constants(nc, L, I["shape_constants"])
    hT = L.at("hT", A_HT, [P, KD, TT])
    R = L.at("R", A_R, [P, NT, RW])
    Rs = L.at("Rs", A_RS, [TS, RW])
    block_norm(nc, L, PS, C, I["x_prompt"], I["x_sample"], I["norm_mix"][0], hT)
    dnT = L.at("dnT", A_DN, [P, 12, TT])
    block_project(nc, L, PS, C, I["w_in"][0], hT, R, Rs, dnT)
    obT = L.at("obT", A_OB, [P, DH, TT])
    convT = L.at("convT", A_FREE + 18432, [P, 12, 4 + 3 * TS])
    ab_p = L.at("ab_p", A_END - 512, [P, NT, 8])
    ab_s = L.at("ab_s", A_END - 256, [TS, 1, 8])
    Os = L.at("Os", A_FREE + 14336, [TS, DW])
    block_conv(nc, L, PS, C, I["state_dn_conv"][0], I["dn_conv_w"][0], dnT, convT, O["conv_prompt"][0, 0], O["conv_sample"][0])
    block_decays(nc, L, PS, C, I["dn_A_log"][0], I["dn_dt_bias"][0], R, Rs, ab_p, ab_s)
    block_delta(nc, L, PS, C, dnT, ab_p, O["S_prompt"][0, 0])
    block_delta_sample(nc, L, PS, C, I["state_dn_S"][0], dnT, ab_s, Os, O["S_sample"][0])
    block_delta_gate(nc, L, PS, C, dnT, Os, R, Rs, I["dn_norm"][0], obT)
    L.signals.renew()
    S = Region(L, A_SMALL, A_END)
    gates_p, gates_s = S("gates_p", [P, NT, 24]), S("gates_s", [TS, 24])
    cpos, kv_cmp, kcT = S("cpos", [P, 2, P]), S("kv_cmp", [64, 2, P]), S("kcT", [P, 1, 64])
    qT, kT = L.at("qT", A_QT, [P, 4, TT]), L.at("kT", A_KT, [P, 4, TT])
    oaT = L.at("oaT", A_OA, [P, 4, TT])
    rows = lambda ap: ap.rearrange("b t i g d -> b t (i g d)")
    block_qk(nc, L, PS, C, I["q_norm"][0], I["k_norm"][0], rows(I["state_win"][0]), R, Rs, gates_p, gates_s, qT, kT,
             rows(O["kv_prompt"][0])[0], rows(O["kv_sample"][0])[:, 0], rows(O["win_prompt"][0])[0], rows(O["win_sample"][0]))
    block_compress_prompt(nc, L, PS, C, I["cmp_pos"][0], I["w_cmp"][0], kT, cpos, kv_cmp)
    block_cmp_norm(nc, L, PS, C, I["k_norm"][0, 2], NCP, 1, kv_cmp[0:NCP, 0:1, :], kcT, A_FREE, A_SMALL)
    block_attend_prompt(nc, L, PS, C, qT, kT, kcT, kv_cmp, R, gates_p, oaT)
    L.signals.renew()
    Z = Region(L, A_FREE, A_SMALL)
    kcs, vcs, kcsT, qbd = Z("kcs", [P, TS, P]), Z("vcs", [P, TS, P]), Z("kcsT", [P, TS, P]), Z("qbd", [P, TS, 64])
    snew, g64 = Z("snew", [64, 2]), Z("g64", [64, 3])
    pages = Z("pages", [1, TS * NPAGE], I32)
    sw = L.at("sw", A_OA - 2080, [64, WIN + 1])
    block_window_keys(nc, L, PS, C, rows(I["state_win"][0]), I["page_table"], qT, kT, gates_s, qbd, snew, g64, pages, sw)
    cache = I["cache_nsa"][0].rearrange("n t i g d -> n t (i g d)")
    block_cache_keys(nc, L, PS, C, cache, pages, I["w_cmp"][0], cpos, qbd, kcs, vcs)
    block_cmp_norm(nc, L, PS, C, I["k_norm"][0, 2], NCS, TS, kcs[0:NCS, :, :], kcsT, A_R, A_RS, 4)
    block_attend_sample(nc, L, PS, C, cache, pages, rows(I["state_win"][0]), kcsT, vcs, qbd, snew, g64, sw, Rs, oaT)
    L.signals.renew()
    lo, hi = L.at("mixed_lo", A_R + 41856, [P, 4, TT]), L.at("mixed_hi", A_FREE, [P, 4, TT])
    mixed = [(lo, hi)[m // 4][:, m % 4, :] for m in range(KD)]
    block_merge(nc, L, PS, C, I["w_in"][0], I["w_proj_a"][0], I["w_proj_b"][0], hT, oaT, obT, mixed)
    K = Region(L, A_OB, A_R)
    logits, slot, weight, blocks = K("logits", [P, NT + 1, NG + NE]), K("slot", [P, NT + 1, 2], I32), K("weight", [P, NT + 1, 2]), K("blocks", [1, 64], I32)
    x1 = L.at("x1", A_R, [P, NT + 1, D])
    h2_rows = nc.dram_tensor("h2_rows", [TT + 1, D], F32, kind="Internal").ap()
    table = nc.dram_tensor("slot_tokens", [(MAXBLK + 1) * P, 2], I32, kind="Internal").ap()
    expert_out = nc.dram_tensor("expert_out", [2 * TT + 1, D], F32, kind="Internal").ap()
    block_out(nc, L, PS, C, I["x_prompt"], I["x_sample"], I["w_out"][0], I["norm_ffn"][0], I["w_router_g"][0], I["w_router_e"][0],
              I["b_router_g"][0], I["b_router_e"][0], mixed, x1, h2_rows, logits)
    block_route(nc, L, PS, C, logits, slot, weight, blocks, table)
    block_experts(nc, L, PS, C, I["w_gate"][0], I["w_up"][0], I["w_down"][0], h2_rows, table, blocks, expert_out)
    block_combine(nc, L, C, weight, x1, expert_out, O["y_prompt"], O["y_sample"])

_INS = ["x_prompt", "x_sample", "cache_nsa", "page_table", "state_win", "state_dn_conv", "state_dn_S",
        "norm_mix", "w_in", "q_norm", "k_norm", "cmp_pos", "w_cmp", "dn_conv_w", "dn_A_log", "dn_dt_bias", "dn_norm",
        "w_proj_a", "w_proj_b", "w_out", "norm_ffn", "w_router_g", "b_router_g", "w_router_e", "b_router_e",
        "w_gate", "w_up", "w_down"]
_OUTS = [("y_prompt", (1, TP, D)), ("y_sample", (TS, 1, D)), ("kv_prompt", (1, 1, TP, 4, NKV, HD)), ("kv_sample", (1, TS, 1, 4, NKV, HD)),
         ("win_prompt", (1, 1, WIN, 2, NKV, HD)), ("win_sample", (1, TS, WIN, 2, NKV, HD)),
         ("conv_prompt", (1, 1, 3, 3 * DW)), ("conv_sample", (1, TS, 3, 3 * DW)),
         ("S_prompt", (1, 1, DH, DD, DD)), ("S_sample", (1, TS, DH, DD, DD))]


def kernel(**inputs):
    import concourse.bacc as bacc
    from concourse.bass_utils import run_bass_kernel_spmd

    nc = bacc.Bacc("TRN2", target_bir_lowering=False, num_devices=1)
    arrays = {name: np.ascontiguousarray(inputs[name]) for name in _INS}
    arrays["shape_constants"] = CONST
    ins = {n: nc.dram_tensor(n, a.shape, mybir.dt.from_np(a.dtype), kind="ExternalInput").ap() for n, a in arrays.items()}
    outs = {n: nc.dram_tensor("out_" + n, shape, F32, kind="ExternalOutput").ap() for n, shape in _OUTS}
    build(nc, ins, outs)
    r = run_bass_kernel_spmd(nc, [arrays], core_ids=[0])
    return tuple(r.results[0]["out_" + n] for n, _ in _OUTS)
```

```python
from contextlib import ExitStack

import numpy as np

import concourse.bass as bass
from concourse import mybir

F32 = mybir.dt.float32
I32 = mybir.dt.int32
ALU = mybir.AluOpType
ACT = mybir.ActivationFunctionType
AX = mybir.AxisListType

P = 128
D = 1024
KD = D // P
TP = 1024
TS = 8
TT = TP + TS
NT = TP // P
PAST = 2048
PAGE = 128
NPAGE = PAST // PAGE
WIN = 512
NH, NKV, HD = 8, 2, 64
ROT = 8
DH, DD = 4, 128
DW = DH * DD
NE, NG, EPG = 32, 4, 8
FE = 512
EPS = 1e-6
BIG = 1e30
NCP = 63
NCS = 127
NSEL = 33
MAXBLK = 48
MINBLK = -(-2 * TT // P)

Q0, KC0, VC0, KS0, VS0, KW0, VW0, NG0 = 0, 512, 640, 768, 896, 1024, 1152, 1280
QKV0, AB0, Z0, MA0, MB0 = 1304, 2840, 2848, 3360, 4384
RAB, RZ, RW = 1304, 1312, 1824


def constants():
    cols, where, at = [], {}, 0

    def put(name, a):
        nonlocal at
        full = np.zeros((P, int(np.prod(a.shape[1:]))), np.float32)
        full[:a.shape[0]] = a.reshape(a.shape[0], -1)
        cols.append(full)
        where[name] = (at, full.shape[1])
        at += full.shape[1]

    i = np.arange(P)
    put("ident", np.eye(P))
    put("ones", np.ones((P, P)))
    put("tri", (i[:, None] <= i[None, :]) * 1.0)
    put("strictT", (i[:, None] < i[None, :]) * 1.0)
    put("upper", np.where(i[None, :] >= i[:, None], BIG, 0.0))
    put("lower", np.where(i[None, :] < i[:, None], -BIG, 0.0))
    for s in (1, 2, 4, 8, 16, 32, 64):
        m = (i[:, None] // (2 * s) == i[None, :] // (2 * s)) & (i[:, None] // s % 2 == 1) & (i[None, :] // s % 2 == 0)
        put(f"level{s}", m * 1.0)
    inv = (np.float32(500000.0) ** (-np.arange(ROT, dtype=np.float32) / np.float32(ROT))).astype(np.float32)

    def angles(pos):
        return (pos.astype(np.float32)[..., None] * inv).astype(np.float32)

    pos = np.concatenate([np.arange(TP).reshape(NT, P), np.full((1, P), PAST)]).T
    put("cos", np.cos(angles(pos)))
    put("sin", np.sin(angles(pos)))
    put("ccos", np.cos(angles(16 * i + 31)))
    put("csin", np.sin(angles(16 * i + 31)))
    put("causal", np.where(i[None, :] > i[:, None], -BIG, 0.0))
    put("edge", np.where(i[None, :] <= i[:, None], -BIG, 0.0))
    n = np.arange(64)
    put("cmpmask", np.where(16 * n[None, None, :] + 31 > np.arange(TP).reshape(NT, P).T[:, :, None], -BIG, 0.0))
    put("cmpvalid", (i[:, None] >= 31) * 1.0)
    n, s = np.arange(NCS), np.arange(NSEL)
    put("ovl", ((16 * n[:, None] <= 64 * s + 63) & (16 * n[:, None] + 31 >= 64 * s)) * 1.0)
    put("bonus", np.tile(np.where((s == 0) | (s == 32) | (s == 31), 1000.0, 0.0), (64, 1)))
    h = np.arange(64)
    put("group", (h[:, None] // 4 == h[None, :] // 4) * 1.0)
    put("seq", (h[:, None] // 8 == np.arange(8)[None, :]) * 1.0)
    put("mhalf", np.full((P, 16), -0.5))
    put("eid", np.tile(np.arange(NE, dtype=np.float32), (P, 1)))
    put("blk", np.tile(128.0 * np.arange(NT + 1), (P, 1)))
    put("blkid", np.tile(1.0 * np.arange(MAXBLK), (P, 1)))
    put("tokvalid", (i[:, None] < TS) * 1.0)
    tok = np.arange(9 * P).reshape(9, P).T
    put("tok", np.stack([np.stack([tok, k * TT + tok], -1) for k in range(2)], 2))
    return np.concatenate(cols, axis=1).astype(np.float32), where


CONST, WHERE = constants()


class Layout:

    def __init__(self, nc):
        self.nc = nc
        self.n = 0
        self.signals = Signals(nc)

    def at(self, name, offset, shape, dt=F32):
        self.n += 1
        return self.nc.alloc_sbuf_tensor_at(f"{name}_{self.n}", shape, dt, offset=offset)


class Signals:

    def __init__(self, nc):
        self.nc, self.made = nc, []

    def named(self, prefix):
        def sem(name):
            self.made.append(self.nc.alloc_semaphore(prefix + name))
            return self.made[-1]
        return sem

    def renew(self):
        self.nc.clear_and_free_semaphores(self.made)
        self.nc.all_engine_barrier()
        self.made = []


class Region:

    def __init__(self, L, start, end):
        self.L, self.start, self.end = L, start, end

    def __call__(self, name, shape, dt=F32):
        size = int(np.prod(shape[1:])) * (2 if dt == mybir.dt.bfloat16 else 4)
        r = self.L.at(name, self.start, shape, dt)
        self.start += (size + 31) // 32 * 32
        assert self.start <= self.end, (name, self.start, self.end)
        return r


BASE = 16512
A_HT = BASE
A_CONST = A_HT + KD * TT * 4
A_OB = A_CONST + ((CONST.shape[1] * 4 + 31) // 32) * 32
A_R = A_OB + DH * TT * 4
A_RS = A_R + NT * RW * 4
A_DN = A_RS + RW * 4
A_OA = A_DN + 12 * TT * 4
A_FREE = A_OA + DH * TT * 4
A_QT = A_DN
A_KT = A_QT + 4 * TT * 4
A_MID = A_KT + 4 * TT * 4
A_END = 229344
THIRDS = [(TT // 3 * i, TT // 3) for i in range(3)]
A_W = A_R + (NT + 1) * D * 4
A_SMALL = A_END - 4096


def block_norm(nc, L, PS, C, x_p, x_s, gain, hT):
    ctx = ExitStack()
    with ctx:
        sem = L.signals.named("")
        x_loaded = [sem(f"n_x_loaded{i}") for i in range(3)]
        gain_loaded, squares_done, rs_ready, xn_ready, tp_done, ht_done, dve_step = map(
            sem, ("n_gain_loaded", "n_squares_done", "n_rs_ready", "n_xn_ready", "n_tp_done", "n_ht_done", "n_dve_step"))
        x = L.at("x", A_R, [P, 3, D])
        junk = L.at("junk", A_R + 12288, [P, D])
        xn = L.at("xn", A_R + 16384, [P, 2, D])
        ss = L.at("ss", A_R + 24576, [P, 16])
        rs = L.at("rs", A_R + 24576 + 64, [P, 16])
        g = L.at("gain", A_R + 24576 + 128, [P, KD])
        rows = [P] * NT + [TS]
        block = ctx.enter_context(nc.Block())

        @block.sync
        def _(sp):
            sp.dma_start(g[:, :], gain.rearrange("(k p) -> p k", p=P), allow_slow_non_contiguous=True).then_inc(gain_loaded, 16)
            for t, n in enumerate(rows):
                if t >= 3:
                    sp.wait_ge(xn_ready, t - 2)
                src = x_p[0, t * P:(t + 1) * P, :] if t < NT else x_s[:, 0, :]
                sp.dma_start(x[0:n, t % 3, :], src).then_inc(x_loaded[t % 3], 16)

        @block.scalar
        def _(act):
            for t, n in enumerate(rows):
                act.wait_ge(x_loaded[t % 3], 16 * (t // 3 + 1))
                if t >= 1:
                    act.wait_ge(squares_done, t)
                nc.scalar.activation(junk[0:n, :], x[0:n, t % 3, :], ACT.Square, accum_out=ss[0:n, t:t + 1]).then_inc(squares_done, 1)

        @block.gpsimd
        def _(pool):
            for t, n in enumerate(rows):
                pool.wait_ge(squares_done, t + 1)
                pool.tensor_scalar(ss[0:n, t:t + 1], ss[0:n, t:t + 1], 1.0 / D, EPS, ALU.mult, ALU.add).then_inc(dve_step, 1)
                pool.wait_ge(dve_step, t + 1)
                pool.tensor_tensor(rs[0:n, t:t + 1], ss[0:n, t:t + 1], C["mhalf"][0:n, 0:1], ALU.pow).then_inc(rs_ready, 1)

        @block.vector
        def _(dve):
            dve.wait_ge(gain_loaded, 16)

            def emit(t, n):
                dve.wait_ge(tp_done, t + 1)
                for j in range(2):
                    ins = nc.vector.tensor_tensor(
                        hT[:, 4 * j:4 * j + 4, t * P:t * P + n],
                        PS[2 * (t % 2) + j][:, :].rearrange("p (k n) -> p k n", k=4)[:, :, 0:n],
                        g[:, 4 * j:4 * j + 4].unsqueeze(2).to_broadcast([P, 4, n]), ALU.mult)
                ins.then_inc(ht_done, 1)

            for t, n in enumerate(rows):
                dve.wait_ge(rs_ready, t + 1)
                if t >= 2:
                    dve.wait_ge(tp_done, t - 1)
                nc.vector.tensor_scalar(xn[0:n, t % 2, :], x[0:n, t % 3, :], rs[0:n, t:t + 1], None, ALU.mult).then_inc(xn_ready, 1)
                if t >= 1:
                    emit(t - 1, rows[t - 1])
            emit(NT, TS)

        @block.tensor
        def _(pe):
            for t, n in enumerate(rows):
                pe.wait_ge(xn_ready, t + 1)
                if t >= 2:
                    pe.wait_ge(ht_done, t - 1)
                for k in range(KD):
                    ins = nc.tensor.transpose(PS[2 * (t % 2) + k // 4][:, (k % 4) * P:(k % 4) * P + n],
                                              xn[0:n, t % 2, k * P:(k + 1) * P], C["ident"][0:n, 0:n])
                ins.then_inc(tp_done, 1)


def block_project(nc, L, PS, C, w_in, hT, R, Rs, dnT):
    ctx = ExitStack()
    with ctx:
        sem = L.signals.named("")
        w_loaded0, w_loaded1, mm_done, act_copied, dve_copied = map(
            sem, ("p_w_loaded0", "p_w_loaded1", "p_mm_done", "p_act_copied", "p_dve_copied"))
        w_loaded = (w_loaded0, w_loaded1)
        w = [L.at("w0", A_OB, [P, KD, 512]), L.at("w1", A_OA, [P, KD, 512])]
        wv = w_in.rearrange("(k p) n -> p k n", p=P)
        loads = [([(0, 512)], 0), ([(512, 1024)], 512), ([(1024, QKV0), (AB0, Z0)], 1024), ([(Z0, MA0)], RZ)]
        loads += [([(QKV0 + 512 * j, QKV0 + 512 * j + 512)], None) for j in range(3)]
        units = []
        for c, (pieces, at) in enumerate(loads):
            width = sum(b - a for a, b in pieces)
            if at is not None:
                for t in range(NT + 1):
                    n = P if t < NT else TS
                    dst = R[:, t, at:at + width] if t < NT else Rs[0:TS, at:at + width]
                    if c == 0:
                        dst = dst.rearrange("p (j g d) -> p g j d", g=NKV, d=HD)
                    units.append((c, n, width, None, t, dst))
            else:
                for m in range(4):
                    for t0, n in THIRDS:
                        units.append((c, P, n, m, t0, dnT[:, 4 * (c - 4) + m, t0:t0 + n]))
        last_of = {c: max(i for i, u in enumerate(units) if u[0] == c) for c in range(len(loads))}
        counts, done = [], [0, 0]
        for c, (pieces, _) in enumerate(loads):
            done[c % 2] += 16 * len(pieces)
            counts.append(done[c % 2])

        def source(i, c, rows, n):
            s = PS[i % 8][0:rows, 0:n]
            return s.rearrange("p (g j d) -> p g j d", g=NKV, d=HD) if c == 0 else s

        block = ctx.enter_context(nc.Block())

        @block.sync
        def _(sp):
            for c, (pieces, _) in enumerate(loads):
                if c >= 2:
                    sp.wait_ge(mm_done, last_of[c - 2] + 1)
                o = 0
                for a, b in pieces:
                    sp.dma_start(w[c % 2][:, :, o:o + b - a], wv[:, :, a:b]).then_inc(w_loaded[c % 2], 16)
                    o += b - a

        @block.tensor
        def _(pe):
            seen = -1
            for i, (c, m_rows, n, m, t, _) in enumerate(units):
                if c != seen:
                    pe.wait_ge(w_loaded[c % 2], counts[c])
                    seen = c
                if i >= 8:
                    pe.wait_ge((act_copied, dve_copied)[i % 2], (i - 8) // 2 + 1)
                for k in range(KD):
                    if m is None:
                        lhsT, rhs = hT[:, k, t * P:t * P + m_rows], w[c % 2][:, k, 0:n]
                    else:
                        lhsT, rhs = w[c % 2][:, k, m * P:(m + 1) * P], hT[:, k, t:t + n]
                    ins = nc.tensor.matmul(PS[i % 8][0:m_rows, 0:n], lhsT, rhs, start=(k == 0), stop=(k == KD - 1))
                ins.then_inc(mm_done, 1)

        @block.scalar
        def _(act):
            for i, (c, rows, n, m, t, dst) in enumerate(units):
                if i % 2 == 0:
                    act.wait_ge(mm_done, i + 1)
                    nc.scalar.copy(dst, source(i, c, rows, n)).then_inc(act_copied, 1)

        @block.vector
        def _(dve):
            for i, (c, rows, n, m, t, dst) in enumerate(units):
                if i % 2 == 1:
                    dve.wait_ge(mm_done, i + 1)
                    nc.vector.tensor_copy(dst, source(i, c, rows, n)).then_inc(dve_copied, 1)


class Steps:

    def __init__(self, engine, semaphore):
        self.engine, self.semaphore, self.n = engine, semaphore, 0

    def __call__(self, ins):
        self.n += 1
        ins.then_inc(self.semaphore, 1)
        self.engine.wait_ge(self.semaphore, self.n)


def block_conv(nc, L, PS, C, state_conv, conv_w, dnT, convT, out_conv_p, out_conv_s):
    NC = 12
    NR = 4 + 3 * TS
    ctx = ExitStack()
    with ctx:
        sem = L.signals.named("")
        rows_loaded, rows_tp, rows_copied, tail_tp, tail_copied, stored, conv_done, silu_done, sq_done, sum_done, sum_copied, root_done, diag_done, bcast_done, unit_done, dve_step = map(
            sem, ("c_rows_loaded", "c_rows_tp", "c_rows_copied", "c_tail_tp", "c_tail_copied", "c_stored", "c_conv_done",
                  "c_silu_done", "c_sq_done", "c_sum_done", "c_sum_copied", "c_root_done", "c_diag_done", "c_bcast_done", "c_unit_done", "c_dve_step"))
        rows = L.at("conv_rows", A_OB, [NR, NC * P])
        tail = L.at("conv_tail", A_OB + 6144, [3 + TS, NC * P])
        samp = L.at("conv_samp", A_OB + 12288, [P, 2, NC, TS])
        acc = L.at("conv_acc", A_OA, [P, 2, TT])
        rn = L.at("conv_rn", A_OA + 2 * TT * 4, [P, 72])
        diag = L.at("conv_diag", A_OA + 2 * TT * 4 + 288, [P, 2, 4, P])
        w = convT
        units = [(c, j, t0, n) for c in range(8) for j, (t0, n) in enumerate(((0, 512), (512, 512), (TP, TS)))]
        block = ctx.enter_context(nc.Block())

        @block.sync
        def _(sp):
            sp.dma_start(rows[0:4, :], conv_w).then_inc(rows_loaded, 16)
            sp.dma_start(rows[4:NR, :], state_conv.rearrange("b j c -> (b j) c")).then_inc(rows_loaded, 16)
            sp.wait_ge(tail_copied, 3)
            sp.dma_start(out_conv_p, tail[0:3, :]).then_inc(stored, 16)
            sp.dma_start(out_conv_s[:, 2, :], tail[3:3 + TS, :]).then_inc(stored, 16)
            sp.dma_start(out_conv_s[:, 0:2, :], state_conv[:, 1:3, :]).then_inc(stored, 16)
            sp.wait_ge(stored, 48)

        @block.tensor
        def _(pe):
            pe.wait_ge(rows_loaded, 32)
            for c in range(NC):
                ins = nc.tensor.transpose(PS[0][:, c * NR:(c + 1) * NR], rows[0:NR, c * P:(c + 1) * P], C["ident"][0:NR, 0:NR])
            ins.then_inc(rows_tp, 1)
            for c in range(NC):
                ins = nc.tensor.transpose(PS[1 + c // 4][0:3 + TS, (c % 4) * P:(c % 4 + 1) * P], dnT[:, c, TP - 3:TT], C["ident"][:, :])
            ins.then_inc(tail_tp, 1)
            for c in range(8):
                pe.wait_ge(sq_done, c + 1)
                for t in range(NT + 1):
                    n = P if t < NT else TS
                    ins = nc.tensor.matmul(PS[4][0:n, 8 * t + c:8 * t + c + 1], acc[:, c % 2, t * P:t * P + n], C["ones"][:, 0:1], start=True, stop=True)
                ins.then_inc(sum_done, 1)
            for u, (c, j, t0, n) in enumerate(units):
                m = min(n, P)
                pe.wait_ge(diag_done, u + 1)
                if u >= 2:
                    pe.wait_ge(unit_done, u - 1)
                nc.tensor.matmul(PS[5 + u % 2][:, 0:n], C["ones"][0:m, :],
                                 diag[0:m, u % 2].rearrange("p t n -> p (t n)")[:, 0:n], start=True, stop=True).then_inc(bcast_done, 1)

        @block.vector
        def _(dve):
            step = Steps(dve, dve_step)
            dve.wait_ge(rows_tp, 1)
            nc.vector.tensor_copy(w[:, :, :], PS[0][:, 0:NC * NR].rearrange("p (c r) -> p c r", r=NR)).then_inc(rows_copied, 1)
            dve.wait_ge(rows_copied, 1)
            dve.wait_ge(tail_tp, 1)
            for b in range(3):
                nc.vector.tensor_copy(tail[:, 512 * b:512 * b + 512], PS[1 + b][0:3 + TS, :]).then_inc(tail_copied, 1)
            st = w[:, :, 4:NR].rearrange("p c (b j) -> p c b j", j=3)
            tap = lambda j: w[:, :, j:j + 1].to_broadcast([P, NC, TS])
            step(nc.vector.tensor_tensor(samp[:, 0], dnT[:, :, TP:TT], tap(3), ALU.mult))
            for j in range(3):
                step(nc.vector.tensor_tensor(samp[:, 1], st[:, :, :, j], tap(j), ALU.mult))
                step(nc.vector.tensor_tensor(samp[:, 0], samp[:, 0], samp[:, 1], ALU.add))
            for c in range(NC):
                if c >= 2:
                    dve.wait_ge(silu_done, c - 1)
                    if c - 2 < 8:
                        dve.wait_ge(sum_done, c - 1)
                a, x = acc[:, c % 2, :], dnT[:, c, :]
                nc.vector.tensor_copy(a[:, TP:TT], samp[:, 0, c, :])
                step(nc.vector.tensor_scalar(a[:, 0:TP], x[:, 0:TP], w[:, c, 3:4], None, ALU.mult))
                for j in (2, 1, 0):
                    d = 3 - j
                    ins = nc.vector.scalar_tensor_tensor(a[:, d:TP], x[:, 0:TP - d], w[:, c, j:j + 1], a[:, d:TP], ALU.mult, ALU.add)
                    if j:
                        step(ins)
                    else:
                        ins.then_inc(conv_done, 1)
            dve.wait_ge(sum_done, 8)
            nc.vector.tensor_scalar(rn[:, 0:64], PS[4][:, 0:64], EPS, None, ALU.add).then_inc(sum_copied, 1)
            nc.vector.tensor_scalar(rn[0:TS, 64:72], PS[4][0:TS, 64:72], EPS, None, ALU.add).then_inc(sum_copied, 1)
            dve.wait_ge(silu_done, 12)
            for u, (c, j, t0, n) in enumerate(units):
                dve.wait_ge(bcast_done, u + 1)
                nc.vector.scalar_tensor_tensor(dnT[:, c, t0:t0 + n], PS[5 + u % 2][:, 0:n], DD ** -0.5 if c < 4 else 1.0,
                                               dnT[:, c, t0:t0 + n], ALU.mult, ALU.mult).then_inc(unit_done, 1)

        @block.gpsimd
        def _(pool):
            for c in range(8):
                pool.wait_ge(silu_done, c + 1)
                nc.gpsimd.tensor_tensor(acc[:, c % 2, :], dnT[:, c, :], dnT[:, c, :], ALU.mult).then_inc(sq_done, 1)
            pool.wait_ge(sum_copied, 2)
            nc.gpsimd.tensor_tensor(rn[:, 0:64], rn[:, 0:64], C["mhalf"][:, 0:1].to_broadcast([P, 64]), ALU.pow).then_inc(root_done, 1)
            nc.gpsimd.tensor_tensor(rn[0:TS, 64:72], rn[0:TS, 64:72], C["mhalf"][0:TS, 0:8], ALU.pow).then_inc(root_done, 1)
            pool.wait_ge(root_done, 2)
            for u, (c, j, t0, n) in enumerate(units):
                if u >= 2:
                    pool.wait_ge(bcast_done, u - 1)
                if j < 2:
                    ins = nc.gpsimd.tensor_tensor(diag[:, u % 2], C["ident"].unsqueeze(1).to_broadcast([P, 4, P]),
                                                  rn[:, 32 * j + c:32 * j + 32:8].unsqueeze(2).to_broadcast([P, 4, P]), ALU.mult)
                else:
                    ins = nc.gpsimd.tensor_tensor(diag[0:TS, u % 2, 0, 0:TS], C["ident"][0:TS, 0:TS],
                                                  rn[0:TS, 64 + c:65 + c].to_broadcast([TS, TS]), ALU.mult)
                ins.then_inc(diag_done, 1)

        @block.scalar
        def _(act):
            act.wait_ge(tail_tp, 1)
            for c in range(NC):
                act.wait_ge(conv_done, c + 1)
                nc.scalar.activation(dnT[:, c, :], acc[:, c % 2, :], ACT.Silu).then_inc(silu_done, 1)


def block_decays(nc, L, PS, C, A_log, dt_bias, R, Rs, ab_p, ab_s):
    ctx = ExitStack()
    with ctx:
        sem = L.signals.named("")
        loaded, dve_step, act_step = map(sem, ("d_loaded", "d_dve_step", "d_act_step"))
        par = L.at("decay_par", A_FREE, [P, 8])
        y = L.at("decay_y", A_FREE + 32, [P, NT, 4])
        z = L.at("decay_z", A_FREE + 160, [P, NT, 4])
        block = ctx.enter_context(nc.Block())
        cases = ((P, NT, R[:, :, RAB:RAB + 4], R[:, :, RAB + 4:RZ], ab_p), (TS, 1, Rs[:, RAB:RAB + 4].unsqueeze(1), Rs[:, RAB + 4:RZ].unsqueeze(1), ab_s))

        @block.sync
        def _(sp):
            sp.dma_start(par[:, 0:4], A_log.unsqueeze(0).to_broadcast([P, 4])).then_inc(loaded, 16)
            sp.dma_start(par[:, 4:8], dt_bias.unsqueeze(0).to_broadcast([P, 4])).then_inc(loaded, 16)

        @block.vector
        def _(dve):
            step = Steps(dve, dve_step)
            dve.wait_ge(loaded, 32)
            for i, (n, t, a, b, out) in enumerate(cases):
                yy, zz = y[0:n, 0:t], z[0:n, 0:t]
                step(nc.vector.tensor_tensor(yy, a, par[0:n, 4:8].unsqueeze(1).to_broadcast([n, t, 4]), ALU.add))
                step(nc.vector.tensor_scalar(zz, yy, -1.0, None, ALU.mult))
                step(nc.vector.tensor_tensor(zz, zz, yy, ALU.min))
                dve.wait_ge(act_step, 2 * i + 3)
                step(nc.vector.scalar_tensor_tensor(yy, yy, 0.0, zz, ALU.max, ALU.add))
                step(nc.vector.tensor_tensor(yy, yy, par[0:n, 0:4].unsqueeze(1).to_broadcast([n, t, 4]), ALU.mult))
                step(nc.vector.tensor_scalar(out[0:n, :, 0:4], yy, -1.0, None, ALU.mult))

        @block.scalar
        def _(act):
            step = Steps(act, act_step)
            act.wait_ge(loaded, 32)
            step(nc.scalar.activation(par[:, 0:4], par[:, 0:4], ACT.Exp))
            for i, (n, t, a, b, out) in enumerate(cases):
                zz = z[0:n, 0:t]
                act.wait_ge(dve_step, 6 * i + 3)
                step(nc.scalar.activation(zz, zz, ACT.Exp))
                step(nc.scalar.activation(zz, zz, ACT.Ln, bias=1.0))
            for n, t, a, b, out in cases:
                nc.scalar.activation(out[0:n, :, 4:8], b, ACT.Sigmoid)


def block_delta(nc, L, PS, C, dnT, ab, S_out):
    ctx = ExitStack()
    with ctx:
        sem = L.signals.named("g_")
        gates_done, rows_tp, grow_done, kk_done, qk_done = map(sem, ("gates", "rows_tp", "grow", "kk", "qk"))
        w_done, w_copied, z_done, tu_done, mask_done, first_mask, t_init = map(sem, ("w", "w_copied", "z", "tu", "mask", "first_mask", "t_init"))
        first_tp, wT_done, wT_copied, vnew_done, vnew_copied, o_done, qs_scaled, s_done, s_ready = map(
            sem, ("first_tp", "wT", "wT_copied", "vnew", "vnew_copied", "o", "qs_scaled", "s", "s_ready"))
        d_in, d_exp, a_ready, qkd_ready, kv_ready, o_ready, dve_step, col_done, s_stored, small_ready = map(
            sem, ("d_in", "d_exp", "a_ready", "qkd_ready", "kv_ready", "o_ready", "dve_step", "col", "s_stored", "small"))
        t, u = Region(L, A_OA, A_END - 512), Region(L, A_OB, A_R)
        H4 = [P, DH, P]
        tg, D1, D2, Tm, Wb, wT, vnew, S, o, Bf = (t(n, H4) for n in ("tg", "D1", "D2", "T", "W", "wT", "vnew", "S", "o", "B_first"))
        B = [t("B0", H4), t("B1", H4)]
        A, Um = ([t(f"{n}{i}", H4) for i in range(2)] for n in ("A", "U"))
        QKD, kd, vb, kbg = ([u(f"{n}{i}", H4) for i in range(2)] for n in ("QKD", "kd", "vb", "kbg"))
        sm = t("small", [P, 12, 4])
        gcol, ngcol, egc, egl, kds, nbg = ([sm[:, 2 * i + j, :] for j in range(2)] for i in range(6))
        v4 = lambda ps: ps[:, :].rearrange("p (h n) -> p h n", h=DH)
        heads = range(DH)
        hs = [slice(h * P, (h + 1) * P) for h in heads]
        tok = lambda c: slice(c * P, (c + 1) * P)
        LV = (2, 4, 8, 16, 32, 64)
        NL = len(LV)
        block = ctx.enter_context(nc.Block())
        bc = lambda m: m.unsqueeze(1).to_broadcast(H4)
        col = lambda m: m.unsqueeze(2).to_broadcast(H4)

        @block.tensor
        def _(pe):
            def gate_sums(c):
                pe.wait_ge(gates_done, c + 1)
                if c >= 2:
                    pe.wait_ge(o_ready, c - 1)
                    pe.wait_ge(wT_copied, c - 1)
                nc.tensor.matmul(PS[2][:, :], C["ones"], tg[:, :, :].rearrange("p h n -> p (h n)"), start=True, stop=True)
                nc.tensor.matmul(PS[3][:, 0:4], C["tri"], ab[:, c, 0:4], start=True, stop=True).then_inc(grow_done, 1)

            def rows(c):
                if c >= 2:
                    pe.wait_ge(vnew_copied, c - 1)
                    pe.wait_ge(qs_scaled, c - 1)
                for h in heads:
                    nc.tensor.transpose(PS[0][:, hs[h]], dnT[:, 4 + h, tok(c)], C["ident"])
                for h in heads:
                    ins = nc.tensor.transpose(PS[1][:, hs[h]], dnT[:, 8 + h, tok(c)], C["ident"])
                ins.then_inc(rows_tp, 1)

            def keys(c):
                if c >= 2:
                    pe.wait_ge(s_ready, c)
                for h in heads:
                    ins = nc.tensor.matmul(PS[5][:, hs[h]], dnT[:, 4 + h, tok(c)], dnT[:, 4 + h, tok(c)], start=True, stop=True)
                ins.then_inc(kk_done, 1)

            def queries_and_first(c):
                pe.wait_ge(a_ready, c + 1)
                for h in heads:
                    ins = nc.tensor.matmul(PS[5][:, hs[h]], dnT[:, 4 + h, tok(c)], dnT[:, h, tok(c)], start=True, stop=True)
                ins.then_inc(qk_done, 1)
                pe.wait_ge(first_mask, c + 1)
                for h in heads:
                    ins = nc.tensor.transpose(PS[3][:, hs[h]], Bf[:, h, :], C["ident"])
                ins.then_inc(first_tp, 1)

            def wT_product(c):
                pe.wait_ge(tu_done, (NL + 1) * (c + 1))
                for h in heads:
                    ins = nc.tensor.matmul(PS[3][:, hs[h]], kbg[c % 2][:, h, :], Um[c % 2][:, h, :], start=True, stop=True)
                ins.then_inc(wT_done, 1)

            def new_values(c):
                pe.wait_ge(wT_copied, c + 1)
                pe.wait_ge(s_ready, c + 1)
                for h in heads:
                    nc.tensor.matmul(PS[0][:, hs[h]], Um[c % 2][:, h, :], vb[c % 2][:, h, :], start=True, stop=False)
                    ins = nc.tensor.matmul(PS[0][:, hs[h]], wT[:, h, :], S[:, h, :], start=False, stop=True)
                ins.then_inc(vnew_done, 1)

            def query_state(c):
                for h in heads:
                    ins = nc.tensor.matmul(PS[1][:, hs[h]], dnT[:, h, tok(c)], S[:, h, :], start=True, stop=True)
                ins.then_inc(o_done, 1)

            def output_and_state(c):
                pe.wait_ge(vnew_copied, c + 1)
                pe.wait_ge(qkd_ready, c + 1)
                for h in heads:
                    nc.tensor.matmul(PS[2][:, hs[h]], QKD[c % 2][:, h, :], vnew[:, h, :], start=True, stop=True)
                for h in heads:
                    ins = nc.tensor.matmul(PS[5][:, hs[h]], kd[c % 2][:, h, :], vnew[:, h, :], start=True, stop=True)
                ins.then_inc(s_done, 1)

            gate_sums(0)
            rows(0)
            keys(0)
            queries_and_first(0)
            before = {(0, 1): wT_product, (1, 1): new_values, (2, 0): query_state, (2, 1): output_and_state}
            nxt = {(3, 0): gate_sums, (3, 1): rows, (4, 0): keys, (5, 1): queries_and_first}

            def gap(c, where):
                if where in before and c >= 1:
                    before[where](c - 1)
                if where in nxt and c + 1 < NT:
                    nxt[where](c + 1)

            for c in range(NT):
                U = Um[c % 2]
                for l in range(NL):
                    pe.wait_ge(mask_done, NL * c + l + 1)
                    pe.wait_ge(tu_done, (NL + 1) * c + l + 1)
                    for h in heads:
                        ins = nc.tensor.matmul(PS[7][:, hs[h]], B[l % 2][:, h, :], U[:, h, :], start=True, stop=True)
                    ins.then_inc(w_done, 1)
                    gap(c, (l, 0))
                    pe.wait_ge(w_copied, NL * c + l + 1)
                    if l == 0:
                        pe.wait_ge(t_init, c + 1)
                    if l < NL - 1:
                        for h in heads:
                            nc.tensor.matmul(PS[4][:, hs[h]], Wb[:, h, :], Tm[:, h, :], start=True, stop=True)
                    for h in heads:
                        ins = nc.tensor.matmul(PS[6][:, hs[h]], Tm[:, h, :], Wb[:, h, :], start=True, stop=True)
                    ins.then_inc(z_done, 1)
                    gap(c, (l, 1))
            for f in (wT_product, new_values, query_state, output_and_state):
                f(NT - 1)

        @block.gpsimd
        def _(pool):
            def gates(c):
                if c:
                    pool.wait_ge(grow_done, c)
                nc.gpsimd.tensor_tensor(tg[:, :, :], bc(C["tri"]), col(ab[:, c, 0:4]), ALU.mult).then_inc(gates_done, 1)

            def mask(c, l):
                if NL * c + l >= 2:
                    pool.wait_ge(w_done, NL * c + l - 1)
                nc.gpsimd.tensor_tensor(B[l % 2][:, :, :], bc(C[f"level{LV[l]}"]), A[c % 2][:, :, :], ALU.mult).then_inc(mask_done, 1)

            def start(c):
                pool.wait_ge(a_ready, c + 1)
                if c:
                    pool.wait_ge(first_tp, c)
                nc.gpsimd.tensor_tensor(Bf[:, :, :], bc(C["level1"]), A[c % 2][:, :, :], ALU.mult).then_inc(first_mask, 1)
                mask(c, 0)
                mask(c, 1)
                pool.wait_ge(first_mask, c + 1)
                if c:
                    pool.wait_ge(z_done, NL * c)
                nc.gpsimd.tensor_tensor(Tm[:, :, :], bc(C["ident"]), Bf[:, :, :], ALU.subtract).then_inc(t_init, 1)

            nc.gpsimd.memset(S[:, :, :], 0.0).then_inc(s_ready, 1)
            gates(0)
            start(0)
            for c in range(NT):
                if c + 1 < NT:
                    gates(c + 1)
                for l in range(2, NL):
                    mask(c, l)
                if c + 1 < NT:
                    start(c + 1)

        @block.vector
        def _(dve):
            step = Steps(dve, dve_step)

            def decays(c):
                i = c % 2
                dve.wait_ge(grow_done, c + 1)
                step(nc.vector.tensor_copy(gcol[i], PS[3][:, 0:4]))
                nc.vector.tensor_scalar(ngcol[i], PS[3][:, 0:4], -1.0, None, ALU.mult)
                last = v4(PS[2])[:, :, P - 1]
                nc.vector.tensor_copy(egl[i], last)
                nc.vector.tensor_tensor(kds[i], last, gcol[i], ALU.subtract).then_inc(small_ready, 1)
                nc.vector.tensor_tensor(D1[:, :, :], v4(PS[2]), bc(C["upper"]), ALU.add).then_inc(d_in, 1)
                if c:
                    dve.wait_ge(qkd_ready, c)
                nc.vector.tensor_tensor(D2[:, :, :], v4(PS[2]), bc(C["lower"]), ALU.add).then_inc(d_in, 1)

            def coefficients(c):
                i = c % 2
                dve.wait_ge(d_exp, 2 * c + 1)
                dve.wait_ge(kk_done, c + 1)
                step(nc.vector.tensor_tensor(D1[:, :, :], v4(PS[5]), D1[:, :, :], ALU.mult))
                nc.vector.tensor_tensor(A[i][:, :, :], D1[:, :, :], col(ab[:, c, 4:8]), ALU.mult).then_inc(a_ready, 1)

            def scaled_rows(c):
                i = c % 2
                dve.wait_ge(col_done, c + 1)
                dve.wait_ge(rows_tp, c + 1)
                step(nc.vector.scalar_tensor_tensor(nbg[i], egc[i], -1.0, ab[:, c, 4:8], ALU.mult, ALU.mult))
                nc.vector.tensor_tensor(kbg[i][:, :, :], v4(PS[0]), col(nbg[i]), ALU.mult)
                nc.vector.tensor_tensor(vb[i][:, :, :], v4(PS[1]), col(ab[:, c, 4:8]), ALU.mult)
                nc.vector.tensor_tensor(kd[i][:, :, :], v4(PS[0]), col(kds[i]), ALU.mult).then_inc(kv_ready, 1)

            def first_and_queries(c):
                i = c % 2
                dve.wait_ge(first_tp, c + 1)
                nc.vector.scalar_tensor_tensor(Um[i][:, :, :], v4(PS[3]), -1.0, bc(C["ident"]), ALU.mult, ALU.add).then_inc(tu_done, 1)
                dve.wait_ge(d_exp, 2 * c + 2)
                dve.wait_ge(qk_done, c + 1)
                nc.vector.tensor_tensor(QKD[i][:, :, :], v4(PS[5]), D2[:, :, :], ALU.mult).then_inc(qkd_ready, 1)

            def follow(c):
                i = c % 2
                dve.wait_ge(qs_scaled, c + 1)
                dve.wait_ge(s_done, c + 1)
                ov = dnT[:, 8:12, tok(c)]
                nc.vector.tensor_tensor(ov, o[:, :, :], v4(PS[2]), ALU.add).then_inc(o_ready, 1)
                step(nc.vector.tensor_tensor(S[:, :, :], S[:, :, :], col(egl[i]), ALU.mult))
                nc.vector.tensor_tensor(S[:, :, :], S[:, :, :], v4(PS[5]), ALU.add).then_inc(s_ready, 1)

            decays(0)
            coefficients(0)
            scaled_rows(0)
            first_and_queries(0)
            for c in range(NT):
                U = Um[c % 2]
                for l in range(NL):
                    dve.wait_ge(z_done, NL * c + l + 1)
                    if l == 0:
                        dve.wait_ge(tu_done, (NL + 1) * c + 1)
                    if l < NL - 1:
                        step(nc.vector.tensor_tensor(Tm[:, :, :], Tm[:, :, :], v4(PS[4]), ALU.subtract))
                    nc.vector.tensor_tensor(U[:, :, :], U[:, :, :], v4(PS[6]), ALU.subtract).then_inc(tu_done, 1)
                    dve.wait_ge(tu_done, (NL + 1) * c + l + 2)
                    if l == 2 and c >= 1:
                        follow(c - 1)
                    if c + 1 < NT:
                        if l == 3:
                            decays(c + 1)
                        if l == 4:
                            coefficients(c + 1)
                        if l == 5:
                            first_and_queries(c + 1)
                            scaled_rows(c + 1)
            follow(NT - 1)

        @block.scalar
        def _(act):
            def exps(c, d):
                i = c % 2
                if d == 0:
                    act.wait_ge(small_ready, c + 1)
                    nc.scalar.activation(egc[i], gcol[i], ACT.Exp)
                    nc.scalar.activation(kds[i], kds[i], ACT.Exp)
                    nc.scalar.activation(egl[i], egl[i], ACT.Exp).then_inc(col_done, 1)
                Dm, bias, scale = ((D1, gcol[i], -1.0), (D2, ngcol[i], 1.0))[d]
                act.wait_ge(d_in, 2 * c + d + 1)
                for h in heads:
                    ins = nc.scalar.activation(Dm[:, h, :], Dm[:, h, :], ACT.Exp, bias=bias[:, h:h + 1], scale=scale)
                ins.then_inc(d_exp, 1)

            def copy_wT(c):
                act.wait_ge(wT_done, c + 1)
                nc.scalar.copy(wT[:, :, :], v4(PS[3])).then_inc(wT_copied, 1)

            def copy_values(c):
                act.wait_ge(vnew_done, c + 1)
                nc.scalar.copy(vnew[:, :, :], v4(PS[0])).then_inc(vnew_copied, 1)

            def scale_queries(c):
                act.wait_ge(o_done, c + 1)
                act.wait_ge(col_done, c + 1)
                if c:
                    act.wait_ge(o_ready, c)
                for h in heads:
                    ins = nc.scalar.mul(o[:, h, :], v4(PS[1])[:, h, :], egc[c % 2][:, h:h + 1])
                ins.then_inc(qs_scaled, 1)

            exps(0, 0)
            exps(0, 1)
            for c in range(NT):
                for l in range(NL):
                    act.wait_ge(w_done, NL * c + l + 1)
                    nc.scalar.copy(Wb[:, :, :], v4(PS[7])).then_inc(w_copied, 1)
                    if c >= 1 and l < 3:
                        (copy_wT, copy_values, scale_queries)[l](c - 1)
                    if c + 1 < NT and l in (4, 5):
                        exps(c + 1, l - 4)
            for f in (copy_wT, copy_values, scale_queries):
                f(NT - 1)

        @block.sync
        def _(sp):
            sp.wait_ge(s_ready, NT + 1)
            sp.dma_start(S_out.rearrange("h d e -> d h e"), S[:, :, :]).then_inc(s_stored, 16)
            sp.wait_ge(s_stored, 16)


def block_delta_sample(nc, L, PS, C, state_S, dnT, ab_s, Os, S_out):
    ctx = ExitStack()
    with ctx:
        sem = L.signals.named("e_")
        S_loaded = sem("S_loaded")
        S_stored = [sem("S_stored0"), sem("S_stored1")]
        diag_done, row_done, row_ready, kS_done, v_ready, vdiag_done, vb_done, T1_done, S_ready, o_done, o_copied, otp_done, dve_step = map(
            sem, ("diag", "row", "row_ready", "kS", "v_ready", "vdiag", "vb", "T1", "S_ready", "o", "o_copied", "otp", "dve_step"))
        t = Region(L, A_OA, A_FREE + 14336)
        S0 = t("S0", [P, TS, DH, P])
        S1 = t("S1", [P, 2, DH, P])
        diag = t("diag", [P, 2, DH, P])
        T1 = t("T1", [P, DH, P])
        rdiag = t("rdiag", [TS, 2, DH, TS])
        row = t("row", [P, 2, DH, TS])
        bg = t("bg", [P, DH, TS])
        bv = t("bv", [P, DH, TS])
        kx = t("kx", [P, DH, TS])
        vn = t("vn", [P, DH, TS])
        oT = t("oT", [P, DH, TS])
        q, k, v = (dnT[:, 4 * i:4 * i + 4, TP:TT] for i in range(3))
        block = ctx.enter_context(nc.Block())

        @block.sync
        def _(sp):
            sp.dma_start(S0[:, 0:4], state_S[0:4].rearrange("b h d e -> d b h e")).then_inc(S_loaded, 16)
            sp.dma_start(S0[:, 4:8], state_S[4:8].rearrange("b h d e -> d b h e")).then_inc(S_loaded, 16)
            for b in range(TS):
                sp.wait_ge(S_ready, b + 1)
                sp.dma_start(S_out[b].rearrange("h d e -> d h e"), S1[:, b % 2]).then_inc(S_stored[b % 2], 16)
            for s in S_stored:
                sp.wait_ge(s, 16 * (TS // 2))

        @block.gpsimd
        def _(pool):
            for i in range(2):
                nc.gpsimd.tensor_tensor(rdiag[:, i], C["ident"][0:TS, 0:TS].unsqueeze(1).to_broadcast([TS, DH, TS]),
                                        ab_s[0:TS, 0, 4 * i:4 * i + 4].unsqueeze(2).to_broadcast([TS, DH, TS]), ALU.mult).then_inc(diag_done, 1)
            pool.wait_ge(v_ready, 1)
            for b in range(TS):
                if b >= 2:
                    pool.wait_ge(vb_done, b - 1)
                nc.gpsimd.tensor_tensor(diag[:, b % 2], C["ident"].unsqueeze(1).to_broadcast([P, DH, P]),
                                        vn[:, :, b].unsqueeze(2).to_broadcast([P, DH, P]), ALU.mult).then_inc(vdiag_done, 1)

        @block.tensor
        def _(pe):
            def read_state(b):
                pe.wait_ge(S_ready, b + 1)
                for h in range(DH):
                    ins = nc.tensor.matmul(PS[2][:, h * TS + b:h * TS + b + 1], S1[:, b % 2, h, :], q[:, h, b:b + 1], start=True, stop=True)
                ins.then_inc(o_done, 1)

            pe.wait_ge(diag_done, 2)
            nc.tensor.matmul(PS[3][:, 0:64], C["ones"][0:TS, :], rdiag[:, :, :, :].rearrange("p i h b -> p (i h b)"), start=True, stop=True).then_inc(row_done, 1)
            pe.wait_ge(S_loaded, 32)
            for b in range(TS):
                for h in range(DH):
                    ins = nc.tensor.matmul(PS[0][:, h * TS + b:h * TS + b + 1], S0[:, b, h, :], k[:, h, b:b + 1], start=True, stop=True)
            ins.then_inc(kS_done, 1)
            for b in range(TS):
                pe.wait_ge(vdiag_done, b + 1)
                if b >= 2:
                    pe.wait_ge(T1_done, b - 1)
                nc.tensor.matmul(PS[(1, 5)[b % 2]][:, :], C["ones"], diag[:, b % 2].rearrange("p h n -> p (h n)"), start=True, stop=True).then_inc(vb_done, 1)
                if b >= 1:
                    read_state(b - 1)
            read_state(TS - 1)
            pe.wait_ge(o_copied, 1)
            for h in range(DH):
                ins = nc.tensor.transpose(PS[4][0:TS, h * P:(h + 1) * P], oT[:, h, :], C["ident"])
            ins.then_inc(otp_done, 1)

        @block.scalar
        def _(act):
            act.wait_ge(row_done, 1)
            nc.scalar.activation(row[:, 0], PS[3][:, 0:32].rearrange("p (h b) -> p h b", h=DH), ACT.Exp).then_inc(row_ready, 1)
            nc.scalar.copy(row[:, 1], PS[3][:, 32:64].rearrange("p (h b) -> p h b", h=DH)).then_inc(row_ready, 1)

        @block.vector
        def _(dve):
            step = Steps(dve, dve_step)
            dve.wait_ge(row_ready, 2)
            nc.vector.tensor_tensor(bg[:, :, :], row[:, 0], row[:, 1], ALU.mult)
            step(nc.vector.tensor_tensor(bv[:, :, :], v, row[:, 1], ALU.mult))
            dve.wait_ge(kS_done, 1)
            step(nc.vector.tensor_tensor(kx[:, :, :], PS[0][:, 0:DH * TS].rearrange("p (h b) -> p h b", h=DH), bg[:, :, :], ALU.mult))
            nc.vector.tensor_tensor(vn[:, :, :], bv[:, :, :], kx[:, :, :], ALU.subtract).then_inc(v_ready, 1)
            for b in range(TS):
                if b >= 2:
                    dve.wait_ge(S_stored[b % 2], 16 * (b // 2))
                    dve.wait_ge(o_done, b - 1)
                nc.vector.tensor_tensor(S1[:, b % 2], S0[:, b], row[:, 0, :, b].unsqueeze(2).to_broadcast([P, DH, P]), ALU.mult)
                dve.wait_ge(vb_done, b + 1)
                if b:
                    dve.wait_ge(S_ready, b)
                nc.vector.tensor_tensor(T1[:, :, :], PS[(1, 5)[b % 2]][:, :].rearrange("p (h n) -> p h n", h=DH), k[:, :, b].unsqueeze(2).to_broadcast([P, DH, P]), ALU.mult).then_inc(T1_done, 1)
                dve.wait_ge(T1_done, b + 1)
                nc.vector.tensor_tensor(S1[:, b % 2], S1[:, b % 2], T1[:, :, :], ALU.add).then_inc(S_ready, 1)
            dve.wait_ge(o_done, TS)
            nc.vector.tensor_copy(oT[:, :, :], PS[2][:, 0:32].rearrange("p (h b) -> p h b", h=DH)).then_inc(o_copied, 1)
            dve.wait_ge(otp_done, 1)
            nc.vector.tensor_copy(Os[:, :], PS[4][0:TS, :])


def block_delta_gate(nc, L, PS, C, dnT, Os, R, Rs, dn_norm, obT):
    ctx = ExitStack()
    with ctx:
        sem = L.signals.named("h_")
        loaded, silu_done, zg_done, sq_done, ss_done, mean_done, r_done, y_done, tp_done, copied, dve_step = map(
            sem, ("loaded", "silu", "zg", "sq", "ss", "mean", "r", "y", "tp", "copied", "dve_step"))
        sq = L.at("h_sq", A_OA, [P, 2, DH, P])
        y = L.at("h_y", A_OA + 4096, [P, 2, DH, P])
        gain = L.at("h_gain", A_OA + 8192, [P, P])
        ss = L.at("h_ss", A_OA + 8704, [P, NT + 1, DH])
        mean = L.at("h_mean", A_OA + 8704 + 160, [P, NT + 1, DH])
        r = L.at("h_r", A_OA + 8704 + 320, [P, NT + 1, DH])
        tiles = [(c, P, dnT[:, 8:12, c * P:(c + 1) * P], R[:, c, RZ:RW].rearrange("p (h n) -> p h n", h=DH)) for c in range(NT)]
        tiles.append((NT, TS, Os[:, :].rearrange("p (h n) -> p h n", h=DH), Rs[:, RZ:RW].rearrange("p (h n) -> p h n", h=DH)))
        block = ctx.enter_context(nc.Block())

        @block.sync
        def _(sp):
            sp.dma_start(gain[:, :], dn_norm.unsqueeze(0).to_broadcast([P, P])).then_inc(loaded, 16)

        @block.scalar
        def _(act):
            for c, n, o, z in tiles:
                nc.scalar.activation(z, z, ACT.Silu).then_inc(silu_done, 1)
            for c, n, o, z in tiles:
                act.wait_ge(tp_done, c + 1)
                nc.scalar.copy(obT[:, :, c * P:c * P + n], PS[c % 2][:, :].rearrange("p (h n) -> p h n", h=DH)[:, :, 0:n]).then_inc(copied, 1)

        @block.gpsimd
        def _(pool):
            for c, n, o, z in tiles:
                if c >= 2:
                    pool.wait_ge(ss_done, c - 1)
                nc.gpsimd.tensor_tensor(sq[0:n, c % 2], o, o, ALU.mult).then_inc(sq_done, 1)
            pool.wait_ge(mean_done, 2)
            for i, (n, a, b) in enumerate(((P, 0, NT), (TS, NT, NT + 1))):
                nc.gpsimd.tensor_tensor(r[0:n, a:b, :], mean[0:n, a:b, :], C["mhalf"][0:n, 0:1].unsqueeze(2).to_broadcast([n, b - a, DH]), ALU.pow).then_inc(r_done, 1)
            pool.wait_ge(loaded, 16)
            for c, n, o, z in tiles:
                pool.wait_ge(silu_done, c + 1)
                nc.gpsimd.tensor_tensor(z, z, gain[0:n, :].unsqueeze(1).to_broadcast([n, DH, P]), ALU.mult).then_inc(zg_done, 1)

        @block.vector
        def _(dve):
            step = Steps(dve, dve_step)
            for c, n, o, z in tiles:
                dve.wait_ge(sq_done, c + 1)
                nc.vector.tensor_reduce(ss[0:n, c, :], sq[0:n, c % 2], AX.X, ALU.add).then_inc(ss_done, 1)
            dve.wait_ge(ss_done, NT + 1)
            for n, a, b in ((P, 0, NT), (TS, NT, NT + 1)):
                nc.vector.tensor_scalar(mean[0:n, a:b, :], ss[0:n, a:b, :], 1.0 / DD, EPS, ALU.mult, ALU.add).then_inc(mean_done, 1)
            dve.wait_ge(r_done, 2)
            for c, n, o, z in tiles:
                if c >= 2:
                    dve.wait_ge(tp_done, c - 1)
                step(nc.vector.tensor_tensor(y[0:n, c % 2], o, r[0:n, c, :].unsqueeze(2).to_broadcast([n, DH, P]), ALU.mult))
                dve.wait_ge(zg_done, c + 1)
                nc.vector.tensor_tensor(y[0:n, c % 2], y[0:n, c % 2], z, ALU.mult).then_inc(y_done, 1)

        @block.tensor
        def _(pe):
            for c, n, o, z in tiles:
                pe.wait_ge(y_done, c + 1)
                if c >= 2:
                    pe.wait_ge(copied, c - 1)
                for h in range(DH):
                    ins = nc.tensor.transpose(PS[c % 2][:, h * P:h * P + n], y[0:n, c % 2, h, :], C["ident"][0:n, 0:n])
                ins.then_inc(tp_done, 1)


GROUPS = ((Q0, 8, 0), (KS0, 2, 8), (KW0, 2, 10))


def block_qk(nc, L, PS, C, q_norm, k_norm, state_win, R, Rs, gates_p, gates_s, qT, kT, kv_p, kv_s, win_p, win_s):
    ctx = ExitStack()
    with ctx:
        sem = L.signals.named("q_")
        loaded, sq_done, ss_done, mean_done, r_done, gain_ready, x_done, xg_done, rope_done, tp_done, act_copied, dve_copied, stored, passed, dve_step = map(
            sem, ("loaded", "sq", "ss", "mean", "r", "gain", "x", "xg", "rope", "tp", "act_copied", "dve_copied", "stored", "passed", "dve_step"))
        T = Region(L, A_MID, A_OA)
        gain = T("q_gain", [P, 3, HD])
        ss, mean, r = (T("q_" + n, [P, NT + 1, 12]) for n in ("ss", "mean", "r"))
        sq = T("q_sq", [P, 2, 12, HD])
        T = Region(L, A_FREE, A_SMALL)
        rot = [T(f"q_rot{i}", [P, NT, 8, ROT]) for i in range(4)]
        cases = [(c, P, R[:, c, :]) for c in range(NT)] + [(NT, TS, Rs[:, :])]
        spans = ((P, 0, NT), (TS, NT, NT + 1))
        heads = lambda x, at, n: x[:, at:at + n * HD].rearrange("p (h d) -> p h d", d=HD)
        block = ctx.enter_context(nc.Block())

        @block.sync
        def _(sp):
            sp.dma_start(gain[:, 0, :], q_norm.unsqueeze(0).to_broadcast([P, HD])).then_inc(loaded, 16)
            sp.dma_start(gain[:, 1, :], k_norm[0].unsqueeze(0).to_broadcast([P, HD])).then_inc(loaded, 16)
            sp.dma_start(gain[:, 2, :], k_norm[1].unsqueeze(0).to_broadcast([P, HD])).then_inc(loaded, 16)
            sp.dma_start(win_s[:, 0:WIN - 1], state_win[:, 1:WIN]).then_inc(passed, 16)
            sp.wait_ge(rope_done, 6)
            sp.dma_start(kv_p.rearrange("(t p) c -> p t c", p=P), R[:, :, KC0:KW0]).then_inc(stored, 16)
            sp.dma_start(kv_s, Rs[:, KC0:KW0]).then_inc(stored, 16)
            sp.dma_start(win_p.rearrange("(t p) c -> p t c", p=P), R[:, NT - WIN // P:NT, KW0:NG0]).then_inc(stored, 16)
            sp.dma_start(win_s[:, WIN - 1], Rs[:, KW0:NG0]).then_inc(stored, 16)
            sp.wait_ge(stored, 64)
            sp.wait_ge(passed, 16)

        @block.gpsimd
        def _(pool):
            for c, n, x in cases:
                if c >= 2:
                    pool.wait_ge(ss_done, c - 1)
                for at, h, slot in GROUPS:
                    ins = nc.gpsimd.tensor_tensor(sq[0:n, c % 2, slot:slot + h, :], heads(x, at, h), heads(x, at, h), ALU.mult)
                ins.then_inc(sq_done, 1)
            pool.wait_ge(mean_done, 2)
            for n, a, b in spans:
                nc.gpsimd.tensor_tensor(r[0:n, a:b, :], mean[0:n, a:b, :], C["mhalf"][0:n, 0:1].unsqueeze(2).to_broadcast([n, b - a, 12]), ALU.pow).then_inc(r_done, 1)
            pool.wait_ge(gain_ready, 1)
            for c, n, x in cases:
                pool.wait_ge(x_done, c + 1)
                for i, (at, h, slot) in enumerate(GROUPS):
                    ins = nc.gpsimd.tensor_tensor(heads(x, at, h), heads(x, at, h), gain[0:n, i:i + 1, :].to_broadcast([n, h, HD]), ALU.mult)
                ins.then_inc(xg_done, 1)

        @block.vector
        def _(dve):
            step = Steps(dve, dve_step)
            dve.wait_ge(loaded, 48)
            nc.vector.tensor_scalar(gain[:, 0, :], gain[:, 0, :], HD ** -0.5, None, ALU.mult).then_inc(gain_ready, 1)
            for c, n, x in cases:
                dve.wait_ge(sq_done, c + 1)
                nc.vector.tensor_reduce(ss[0:n, c, :], sq[0:n, c % 2], AX.X, ALU.add).then_inc(ss_done, 1)
            dve.wait_ge(ss_done, NT + 1)
            for n, a, b in spans:
                nc.vector.tensor_scalar(mean[0:n, a:b, :], ss[0:n, a:b, :], 1.0 / HD, EPS, ALU.mult, ALU.add).then_inc(mean_done, 1)
            dve.wait_ge(r_done, 2)
            for c, n, x in cases:
                for at, h, slot in GROUPS:
                    ins = nc.vector.tensor_tensor(heads(x, at, h), heads(x, at, h), r[0:n, c, slot:slot + h].unsqueeze(2).to_broadcast([n, h, HD]), ALU.mult)
                ins.then_inc(x_done, 1)
            dve.wait_ge(xg_done, NT + 1)
            for i, (at, h, slot) in enumerate(GROUPS):
                for n, t0, t1, x in ((P, 0, NT, R[:, :, at:at + h * HD]), (TS, NT, NT + 1, Rs[:, at:at + h * HD].unsqueeze(1))):
                    x = x.rearrange("p t (h d) -> p t h d", d=HD)
                    nt = t1 - t0
                    cos, sin = (C[k][0:n, ROT * t0:ROT * t1].rearrange("p (t d) -> p t d", d=ROT).unsqueeze(2).to_broadcast([n, nt, h, ROT]) for k in ("cos", "sin"))
                    a, b = x[:, :, :, 0:ROT], x[:, :, :, ROT:2 * ROT]
                    ra, rb, rc, rd = (t[0:n, 0:nt, 0:h, :] for t in rot)
                    nc.vector.tensor_tensor(ra, a, cos, ALU.mult)
                    nc.vector.tensor_tensor(rb, b, sin, ALU.mult)
                    nc.vector.tensor_tensor(rc, b, cos, ALU.mult)
                    step(nc.vector.tensor_tensor(rd, a, sin, ALU.mult))
                    nc.vector.tensor_tensor(a, ra, rb, ALU.subtract)
                    ins = nc.vector.tensor_tensor(b, rc, rd, ALU.add)
                    ins.then_inc(rope_done, 1)
                    dve.wait_ge(rope_done, 2 * i + (1 if t0 == 0 else 2))
            for c, n, x in cases:
                dve.wait_ge(tp_done, 2 * c + 2)
                nc.vector.tensor_copy(kT[:, :, c * P:c * P + n], PS[2 * (c % 2) + 1][:, :].rearrange("p (j n) -> p j n", j=4)[:, :, 0:n]).then_inc(dve_copied, 1)

        @block.tensor
        def _(pe):
            pe.wait_ge(rope_done, 6)
            for c, n, x in cases:
                if c >= 2:
                    pe.wait_ge(act_copied, c - 1)
                for j in range(4):
                    pair = x[:, j * P:(j + 1) * P]
                    ins = nc.tensor.transpose(PS[2 * (c % 2)][:, j * P:j * P + n], pair, C["ident"][0:n, 0:n])
                ins.then_inc(tp_done, 1)
                if c >= 2:
                    pe.wait_ge(dve_copied, c - 1)
                for j, at in enumerate((KS0, KW0, KC0, VC0)):
                    ins = nc.tensor.transpose(PS[2 * (c % 2) + 1][:, j * P:j * P + n], x[:, at:at + P], C["ident"][0:n, 0:n])
                ins.then_inc(tp_done, 1)

        @block.scalar
        def _(act):
            nc.scalar.activation(gates_p[:, :, :], R[:, :, NG0:RAB], ACT.Sigmoid)
            nc.scalar.activation(gates_s[:, :], Rs[:, NG0:RAB], ACT.Sigmoid)
            for c, n, x in cases:
                act.wait_ge(tp_done, 2 * c + 1)
                nc.scalar.copy(qT[:, :, c * P:c * P + n], PS[2 * (c % 2)][:, :].rearrange("p (j n) -> p j n", j=4)[:, :, 0:n]).then_inc(act_copied, 1)


def load_cmp_weights(nc, engine, i, w_cmp, wbd, zeroed, loaded):
    engine.wait_ge(zeroed, 1)
    for g in range(2):
        engine.dma_start(wbd[64 * g:64 * g + 64, :, 64 * g:64 * g + 64], w_cmp[i].rearrange("l d e -> d l e")).then_inc(loaded, 16)


def block_compress_prompt(nc, L, PS, C, cmp_pos, w_cmp, kT, cpos, kv_cmp):
    ctx = ExitStack()
    with ctx:
        sem = L.signals.named("m_")
        pos_loaded, pos_tp, pos_copied, zeroed0, zeroed1, w_loaded0, w_loaded1, mm_done, c_done, c_copied = map(
            sem, ("pos_loaded", "pos_tp", "pos_copied", "zeroed0", "zeroed1", "w_loaded0", "w_loaded1", "mm", "c", "c_copied"))
        wbd = [L.at("m_wk", A_MID, [P, 32, P]), L.at("m_wv", A_OA, [P, 32, P])]
        T = Region(L, A_FREE, A_SMALL)
        pos = T("m_pos", [64, P])
        posT = T("m_posT", [P, 64])
        block = ctx.enter_context(nc.Block())

        @block.gpsimd
        def _(pool):
            nc.gpsimd.memset(wbd[0][:, :, :], 0.0).then_inc(zeroed0, 1)

        @block.sync
        def _(sp):
            for g in range(2):
                sp.dma_start(pos[:, 64 * g:64 * g + 64], cmp_pos.rearrange("i l d -> (i l) d")).then_inc(pos_loaded, 16)
            load_cmp_weights(nc, sp, 0, w_cmp, wbd[0], zeroed0, w_loaded0)
            load_cmp_weights(nc, sp, 1, w_cmp, wbd[1], zeroed1, w_loaded1)

        @block.tensor
        def _(pe):
            pe.wait_ge(pos_loaded, 32)
            nc.tensor.transpose(PS[0][:, 0:64], pos[:, :], C["ident"][0:64, 0:64]).then_inc(pos_tp, 1)
            pe.wait_ge(pos_copied, 1)
            for i in range(2):
                pe.wait_ge((w_loaded0, w_loaded1)[i], 32)
                for l in range(32):
                    nc.tensor.matmul(PS[1 + i][:, 0:P], posT[:, 32 * i + l:32 * i + l + 1].to_broadcast([P, P]), wbd[i][:, l, :], start=(l == 0), stop=(l == 31))
                for l in range(32):
                    ins = nc.tensor.matmul(PS[3 + i][0:NCP, 0:P], kT[:, 2 + i, l:l + 16 * (NCP - 1) + 1:16], wbd[i][:, l, :], start=(l == 0), stop=(l == 31))
                ins.then_inc(mm_done, 1)

        @block.vector
        def _(dve):
            nc.vector.memset(wbd[1][:, :, :], 0.0).then_inc(zeroed1, 1)
            dve.wait_ge(pos_tp, 1)
            nc.vector.tensor_copy(posT[:, :], PS[0][:, 0:64]).then_inc(pos_copied, 1)
            for i in range(2):
                dve.wait_ge(mm_done, i + 1)
                nc.vector.tensor_copy(cpos[:, i, :], PS[1 + i][:, 0:P]).then_inc(c_copied, 1)
                dve.wait_ge(c_copied, i + 1)
                nc.vector.tensor_tensor(kv_cmp[0:NCP, i, :], PS[3 + i][0:NCP, 0:P], cpos[0:NCP, i, :], ALU.add)


def block_cmp_norm(nc, L, PS, C, k_gain, n, B, kc, kcT, base, end, bank=0):
    ctx = ExitStack()
    with ctx:
        sem = L.signals.named(f"r{B}_")
        loaded, mean_done, r_done, k_ready, tp_done, copied, dve_step = map(sem, ("loaded", "mean", "r", "k_ready", "tp", "copied", "dve_step"))
        T = Region(L, base, end)
        gain = T("r_gain", [P, HD])
        sq = T("r_sq", [P, 2 * B, HD])
        mean, r = T("r_mean", [P, 2 * B]), T("r_r", [P, 2 * B])
        rot = [T(f"r_rot{i}", [P, 2 * B, ROT]) for i in range(4)]
        x = kc.rearrange("p b (g d) -> p (b g) d", d=HD)
        block = ctx.enter_context(nc.Block())

        @block.sync
        def _(sp):
            sp.dma_start(gain[:, :], k_gain.unsqueeze(0).to_broadcast([P, HD])).then_inc(loaded, 16)

        @block.gpsimd
        def _(pool):
            pool.wait_ge(mean_done, 1)
            nc.gpsimd.tensor_tensor(r[0:n, :], mean[0:n, :], C["mhalf"][0:n, 0:1].to_broadcast([n, 2 * B]), ALU.pow).then_inc(r_done, 1)

        @block.vector
        def _(dve):
            step = Steps(dve, dve_step)
            step(nc.vector.tensor_tensor(sq[0:n], x, x, ALU.mult))
            step(nc.vector.tensor_reduce(mean[0:n, :], sq[0:n], AX.X, ALU.add))
            nc.vector.tensor_scalar(mean[0:n, :], mean[0:n, :], 1.0 / HD, EPS, ALU.mult, ALU.add).then_inc(mean_done, 1)
            dve.wait_ge(r_done, 1)
            dve.wait_ge(loaded, 16)
            step(nc.vector.tensor_tensor(x, x, r[0:n, :].unsqueeze(2).to_broadcast([n, 2 * B, HD]), ALU.mult))
            step(nc.vector.tensor_tensor(x, x, gain[0:n, :].unsqueeze(1).to_broadcast([n, 2 * B, HD]), ALU.mult))
            cos, sin = (C[k][0:n, :].unsqueeze(1).to_broadcast([n, 2 * B, ROT]) for k in ("ccos", "csin"))
            a, b = x[:, :, 0:ROT], x[:, :, ROT:2 * ROT]
            ra, rb, rc, rd = (t[0:n] for t in rot)
            nc.vector.tensor_tensor(ra, a, cos, ALU.mult)
            nc.vector.tensor_tensor(rb, b, sin, ALU.mult)
            nc.vector.tensor_tensor(rc, b, cos, ALU.mult)
            step(nc.vector.tensor_tensor(rd, a, sin, ALU.mult))
            nc.vector.tensor_tensor(a, ra, rb, ALU.subtract)
            nc.vector.tensor_tensor(b, rc, rd, ALU.add).then_inc(k_ready, 1)
            for s in range(B):
                dve.wait_ge(tp_done, s + 1)
                nc.vector.tensor_copy(kcT[:, s, 0:n], PS[bank + s % 2][:, 0:n]).then_inc(copied, 1)

        @block.tensor
        def _(pe):
            pe.wait_ge(k_ready, 1)
            for s in range(B):
                if s >= 2:
                    pe.wait_ge(copied, s - 1)
                nc.tensor.transpose(PS[bank + s % 2][:, 0:n], kc[:, s, :], C["ident"][0:n, 0:n]).then_inc(tp_done, 1)


def block_attend_prompt(nc, L, PS, C, qT, kT, kcT, kv_cmp, R, gates, oaT):
    NWT = WIN // P
    SEL, WINB, CMP, PW = 0, TP, TP + (NWT + 1) * P, TP + (NWT + 1) * P + 64
    ctx = ExitStack()
    with ctx:
        sem = L.signals.named("a_")
        s_done, max_done, exp_done, scaled, tp_done, act_pt, dve_pt, pv_done, o_copied, dve_step = map(
            sem, ("s", "max", "exp", "scaled", "tp", "act_pt", "dve_pt", "pv", "o_copied", "dve_step"))
        T = Region(L, A_MID - 2 * TT * 4, A_OA)
        Pb = [T(f"a_P{i}", [P, PW]) for i in range(2)]
        small = T("a_small", [P, 2, 16])
        T = Region(L, A_FREE, A_SMALL)
        PT = [T(f"a_PT{i}", [P, 14 * P]) for i in range(2)]
        SLOT = (1, 2, 0)
        units = [(i, g, j) for i in range(NT) for g in range(2) for j in range(4)]

        def parts(i):
            lo = max(0, i - NWT)
            return lo, ((SEL, (i + 1) * P), (WINB, (i + 1 - lo) * P), (CMP, NCP))

        def blocks(i):
            lo, _ = parts(i)
            return ([(SEL + k * P, P, 0, k) for k in range(i + 1)] + [(WINB + (k - lo) * P, P, 1, k) for k in range(lo, i + 1)]
                    + [(CMP, NCP, 2, 0)])

        def quads(i):
            b = blocks(i)
            return [b[k:k + 4] for k in range(0, len(b), 4)]

        S = PS[8]
        sview = {0: lambda n: S[:, 0:n], 1: lambda n: S[:, 1024:1024 + n], 2: lambda n: S[:, 1024 + 640:1024 + 640 + n]}
        first_quad = []
        n = 0
        for i, g, j in units:
            first_quad.append(n)
            n += len(quads(i))
        block = ctx.enter_context(nc.Block())

        @block.tensor
        def _(pe):
            def scores(u):
                i, g, j = units[u]
                if u:
                    pe.wait_ge(exp_done, u)
                rows = slice(64 * g, 64 * g + 64)
                q = qT[rows, j, i * P:(i + 1) * P]
                lo, _ = parts(i)
                for branch, first, last in ((0, 0, i), (1, lo, i)):
                    width = (last + 1 - first) * P
                    for c0 in range(0, width, 512):
                        w = min(512, width - c0)
                        out = sview[branch](width)[:, c0:c0 + w]
                        masks = []
                        if c0 + w == width:
                            masks.append((w - P, "causal"))
                        if branch == 1 and i - first == NWT and c0 == 0:
                            masks.append((0, "edge"))
                        nc.tensor.matmul(out, q, kT[rows, branch, first * P + c0:first * P + c0 + w], start=True, stop=not masks)
                        for m, (at, name) in enumerate(masks):
                            nc.tensor.matmul(out[:, at:at + P], C["ident"], C[name], start=False, stop=(m == len(masks) - 1))
                nc.tensor.matmul(sview[2](NCP), q, kcT[rows, 0, 0:NCP], start=True, stop=False)
                nc.tensor.matmul(sview[2](NCP), C["ident"], C["cmpmask"][:, 64 * i:64 * i + NCP], start=False, stop=True).then_inc(s_done, 1)

            def values(u):
                i, g, j = units[u]
                pe.wait_ge(scaled, u + 1)
                f = first_quad[u]
                for n, quad in enumerate(quads(i)):
                    if f + n >= 2:
                        m = f + n - 2
                        pe.wait_ge((act_pt, dve_pt)[m % 2], m // 2 + 1)
                    for k, (at, keys, _, _) in enumerate(quad):
                        ins = nc.tensor.transpose(PS[4 + (f + n) % 2][0:keys, k * P:(k + 1) * P], Pb[u % 2][:, at:at + keys], C["ident"])
                    ins.then_inc(tp_done, 1)
                out = PS[6 + (u // 4) % 2]
                if j == 0 and u >= 8:
                    pe.wait_ge(o_copied, u // 4 - 1)
                b = blocks(i)
                for n, quad in enumerate(quads(i)):
                    pe.wait_ge((act_pt, dve_pt)[(f + n) % 2], (f + n) // 2 + 1)
                    for k, (at, keys, branch, kt) in enumerate(quad):
                        v = kv_cmp[0:NCP, 1, :] if branch == 2 else R[:, kt, (VS0, VW0)[branch]:(VS0, VW0)[branch] + P]
                        x = 4 * n + k
                        ins = nc.tensor.matmul(out[:, j * P:(j + 1) * P], v, PT[u % 2][0:keys, x * P:(x + 1) * P], start=(x == 0), stop=(x == len(b) - 1))
                ins.then_inc(pv_done, 1)

            scores(0)
            for u in range(len(units)):
                if u + 1 < len(units):
                    scores(u + 1)
                values(u)

        def copy_quad(engine, u, n, quad, done):
            engine.wait_ge(tp_done, first_quad[u] + n + 1)
            if n <= 1 and u >= 2:
                engine.wait_ge(pv_done, u - 1)
            src = PS[4 + (first_quad[u] + n) % 2]
            full = len([b for b in quad if b[1] == P])
            ins = None
            pieces = []
            if full:
                pieces.append((P, 0, full))
            if full < len(quad):
                pieces.append((NCP, full, full + 1))
            for rows, a, b in pieces:
                dst, s = PT[u % 2][0:rows, (4 * n + a) * P:(4 * n + b) * P], src[0:rows, a * P:b * P]
                ins = nc.scalar.copy(dst, s) if done is act_pt else nc.vector.tensor_copy(dst, s)
            ins.then_inc(done, 1)

        @block.vector
        def _(dve):
            def maxima(u):
                i, g, j = units[u]
                dve.wait_ge(s_done, u + 1)
                if u >= 2:
                    dve.wait_ge(exp_done, u - 1)
                for b, (at, n) in enumerate(parts(i)[1]):
                    ins = nc.vector.tensor_reduce(small[:, u % 2, SLOT[b]:SLOT[b] + 1], sview[b](n), AX.X, ALU.max, negate=True)
                ins.then_inc(max_done, 1)

            def scale(u):
                i, g, j = units[u]
                dve.wait_ge(exp_done, u + 1)
                s = small[:, u % 2, :]
                step(nc.vector.reciprocal(s[:, 8:11], s[:, 4:7]))
                if i == 0:
                    step(nc.vector.tensor_scalar(s[:, 8:9], s[:, 8:9], C["cmpvalid"], None, ALU.mult))
                step(nc.vector.tensor_tensor(s[:, 12:15], s[:, 8:11], gates[:, i, 3 * (4 * g + j):3 * (4 * g + j) + 3], ALU.mult))
                for b, (at, n) in enumerate(parts(i)[1]):
                    p = Pb[u % 2][:, at:at + n]
                    ins = nc.vector.tensor_scalar(p, p, s[:, 12 + SLOT[b]:13 + SLOT[b]], None, ALU.mult)
                ins.then_inc(scaled, 1)

            def output(u):
                i, g, j = units[u]
                dve.wait_ge(pv_done, u + 1)
                rows = slice(64 * g, 64 * g + 64)
                nc.vector.tensor_copy(oaT[rows, :, i * P:(i + 1) * P], PS[6 + (u // 4) % 2][rows, :].rearrange("p (j n) -> p j n", j=4)).then_inc(o_copied, 1)

            step = Steps(dve, dve_step)
            maxima(0)
            scale(0)
            for u in range(len(units)):
                for n, quad in enumerate(quads(units[u][0])):
                    if (first_quad[u] + n) % 2:
                        copy_quad(dve, u, n, quad, dve_pt)
                if u + 1 < len(units):
                    maxima(u + 1)
                    scale(u + 1)
                if u % 4 == 3:
                    output(u)

        @block.scalar
        def _(act):
            def exps(u):
                i, g, j = units[u]
                act.wait_ge(max_done, u + 1)
                if u >= 2:
                    act.wait_ge(scaled, u - 1)
                    act.wait_ge(tp_done, first_quad[u - 1])
                s = small[:, u % 2, :]
                for b, (at, n) in enumerate(parts(i)[1]):
                    ins = nc.scalar.activation(Pb[u % 2][:, at:at + n], sview[b](n), ACT.Exp, bias=s[:, SLOT[b]:SLOT[b] + 1], accum_out=s[:, 4 + SLOT[b]:5 + SLOT[b]])
                ins.then_inc(exp_done, 1)

            exps(0)
            for u in range(len(units)):
                for n, quad in enumerate(quads(units[u][0])):
                    if (first_quad[u] + n) % 2 == 0:
                        copy_quad(act, u, n, quad, act_pt)
                if u + 1 < len(units):
                    exps(u + 1)


def block_window_keys(nc, L, PS, C, state_win, page_table, qT, kT, gates_s, qbd, snew, g64, pages, sw):
    ctx = ExitStack()
    with ctx:
        sem = L.signals.named("w_")
        zeroed, qbd_ready, loaded, other_loaded, tp_done, act_copied, dve_copied, s_done, new_done = map(
            sem, ("zeroed", "qbd", "loaded", "other_loaded", "tp", "act_copied", "dve_copied", "s", "new"))
        kw = L.at("w_k", A_R, [P, TS, WIN // P, P])
        kwT = L.at("w_kT", A_R + 16384, [P, TS, WIN])
        block = ctx.enter_context(nc.Block())

        @block.sync
        def _(sp):
            for b in range(TS):
                sp.dma_start(kw[:, b], state_win[b, :, 0:P].rearrange("(t p) c -> p t c", p=P)).then_inc(loaded, 16)
            sp.dma_start(pages[:, :], page_table.rearrange("(a b) n -> a (b n)", a=1)).then_inc(other_loaded, 16)
            sp.dma_start(g64[:, :], gates_s[:, :].rearrange("b (h i) -> b h i", i=3)).then_inc(other_loaded, 16)
            sp.wait_ge(other_loaded, 32)

        @block.gpsimd
        def _(pool):
            nc.gpsimd.memset(qbd[:, :, :], 0.0).then_inc(zeroed, 1)
            pool.wait_ge(zeroed, 1)
            for b in range(TS):
                nc.gpsimd.tensor_copy(qbd[0:64, b, 8 * b:8 * b + 4], qT[0:64, :, TP + b])
                ins = nc.gpsimd.tensor_copy(qbd[64:P, b, 8 * b + 4:8 * b + 8], qT[64:P, :, TP + b])
            ins.then_inc(qbd_ready, 1)

        @block.tensor
        def _(pe):
            pe.wait_ge(loaded, 16 * TS)
            for b in range(TS):
                if b >= 4:
                    pe.wait_ge((act_copied, dve_copied)[b % 2], (b - 4) // 2 + 1)
                for t in range(WIN // P):
                    ins = nc.tensor.transpose(PS[b % 4][:, t * P:(t + 1) * P], kw[:, b, t, :], C["ident"])
                ins.then_inc(tp_done, 1)
            pe.wait_ge(qbd_ready, 1)
            for b in range(TS):
                nc.tensor.matmul(PS[5][0:64, 0:2], qbd[:, b, :], kT[:, 0:2, TP + b], start=(b == 0), stop=(b == TS - 1))
            for b in range(TS):
                pe.wait_ge((act_copied, dve_copied)[b % 2], b // 2 + 1)
                ins = nc.tensor.matmul(PS[4][0:64, :], qbd[:, b, :], kwT[:, b, :], start=(b == 0), stop=(b == TS - 1))
            ins.then_inc(s_done, 1)

        @block.scalar
        def _(act):
            for b in range(0, TS, 2):
                act.wait_ge(tp_done, b + 1)
                nc.scalar.copy(kwT[:, b, :], PS[b % 4]).then_inc(act_copied, 1)

        @block.vector
        def _(dve):
            for b in range(1, TS, 2):
                dve.wait_ge(tp_done, b + 1)
                nc.vector.tensor_copy(kwT[:, b, :], PS[b % 4]).then_inc(dve_copied, 1)
            dve.wait_ge(s_done, 1)
            nc.vector.tensor_copy(snew[:, :], PS[5][0:64, 0:2]).then_inc(new_done, 1)
            dve.wait_ge(new_done, 1)
            nc.vector.tensor_copy(sw[:, 0:WIN], PS[4][0:64, :])
            nc.vector.tensor_copy(sw[:, WIN:WIN + 1], snew[:, 1:2])


def block_cache_keys(nc, L, PS, C, cache, pages, w_cmp, cpos, qbd, kcs, vcs):
    HP = NPAGE // 2
    ctx = ExitStack()
    with ctx:
        sem = L.signals.named("k_")
        loaded = [sem(f"loaded{i}") for i in range(3)]
        zeroed, w_loaded, tp_done, act_copied, dve_copied, cmp_done, s_done, c_copied = map(
            sem, ("zeroed", "w_loaded", "tp", "act_copied", "dve_copied", "cmp", "s", "c_copied"))
        X = Region(L, A_R, A_RS)
        wbd = [X(f"k_wbd{i}", [P, 32, P]) for i in range(2)]
        T3 = X("k_T3", [P, 3, PAST])
        stage = [L.at(f"k_stage{i}", A_DN + 12288 * i, [P, HP, 3, P]) for i in range(3)]
        steps = [(b, half) for b in range(TS) for half in range(2)]
        def copies(engine, parity, done):
            n = 0
            for s, (b, half) in enumerate(steps):
                for i in range(3):
                    for quad in range(2):
                        if n % 2 == parity:
                            engine.wait_ge(tp_done, n + 1)
                            if half == 0 and b and i == 0:
                                engine.wait_ge(s_done, b)
                            dst, src = T3[:, i, 1024 * half + 512 * quad:1024 * half + 512 * quad + 512], PS[4 + n % 2]
                            ins = nc.scalar.copy(dst, src) if parity == 0 else nc.vector.tensor_copy(dst, src)
                            ins.then_inc(done, 1)
                        n += 1
                if half and parity:
                    engine.wait_ge(cmp_done, b + 1)
                    nc.vector.tensor_tensor(kcs[0:NCS, b, :], PS[6][0:NCS, 0:P], cpos[0:NCS, 0, :], ALU.add).then_inc(c_copied, 1)
                    nc.vector.tensor_tensor(vcs[0:NCS, b, :], PS[7][0:NCS, 0:P], cpos[0:NCS, 1, :], ALU.add).then_inc(c_copied, 1)

        block = ctx.enter_context(nc.Block())

        @block.gpsimd
        def _(pool):
            for i in range(2):
                nc.gpsimd.memset(wbd[i][:, :, :], 0.0).then_inc(zeroed, 1)

        @block.scalar
        def _(act):
            act.wait_ge(zeroed, 2)
            for i in range(2):
                load_cmp_weights(nc, act, i, w_cmp, wbd[i], zeroed, w_loaded)
            copies(act, 0, act_copied)

        @block.sync
        def _(sp):
            for s, (b, half) in enumerate(steps):
                if s >= 3:
                    sp.wait_ge(tp_done, 6 * (s - 2))
                for p in range(HP):
                    page = sp.value_load(pages[0:1, NPAGE * b + HP * half + p:NPAGE * b + HP * half + p + 1], min_val=0, max_val=cache.shape[0] - 1)
                    sp.dma_start(stage[s % 3][:, p], cache[bass.ds(page, 1), :, 0:3 * P].rearrange("a t (i c) -> (a t) i c", c=P)).then_inc(loaded[s % 3], 16)

        @block.tensor
        def _(pe):
            n = 0
            for s, (b, half) in enumerate(steps):
                pe.wait_ge(loaded[s % 3], 16 * HP * (s // 3 + 1))
                for i in range(3):
                    for quad in range(2):
                        if n >= 2:
                            pe.wait_ge((act_copied, dve_copied)[n % 2], (n - 2) // 2 + 1)
                        for p in range(4):
                            ins = nc.tensor.transpose(PS[4 + n % 2][:, p * P:(p + 1) * P], stage[s % 3][:, 4 * quad + p, i, :], C["ident"])
                        ins.then_inc(tp_done, 1)
                        n += 1
                if half:
                    pe.wait_ge(act_copied, n // 2)
                    pe.wait_ge(dve_copied, n // 2)
                    if b == 0:
                        pe.wait_ge(w_loaded, 64)
                    else:
                        pe.wait_ge(c_copied, 2 * b)
                    for i in range(2):
                        for l in range(32):
                            ins = nc.tensor.matmul(PS[6 + i][0:NCS, 0:P], T3[:, i, l:l + 16 * (NCS - 1) + 1:16], wbd[i][:, l, :], start=(l == 0), stop=(l == 31))
                    ins.then_inc(cmp_done, 1)
                    for c in range(4):
                        ins = nc.tensor.matmul(PS[c][0:64, :], qbd[:, b, :], T3[:, 2, 512 * c:512 * c + 512], start=(b == 0), stop=(b == TS - 1))
                    ins.then_inc(s_done, 1)

        @block.vector
        def _(dve):
            copies(dve, 1, dve_copied)


def block_attend_sample(nc, L, PS, C, cache, pages, state_win, kcsT, vcs, qbd, snew, g64, sw, Rs, oaT):
    ctx = ExitStack()
    with ctx:
        sem = L.signals.named("b_")
        v_loaded, pool_v_loaded, vw_loaded = sem("v_loaded"), sem("pool_v_loaded"), sem("vw_loaded")
        c_done, grouped, g_copied, imp_done, ct_done, ct_copied, pd_done, pd_copied, pt_done, act_pt, dve_pt, o_done = map(
            sem, ("c", "grouped", "g_copied", "imp", "ct", "ct_copied", "pd", "pd_copied", "pt", "act_pt", "dve_pt", "o"))
        max_done, exp_done, p_ready, pg_ready, dve_step, pd_ready, o_copied, otp_done = map(
            sem, ("max", "exp", "p_ready", "pg_ready", "dve_step", "pd_ready", "o_copied", "otp"))
        X = Region(L, A_R, A_RS)
        v_lo = X("b_vlo", [P, 4, NPAGE, P])
        ss = X("b_ss", [64, PAST + 1])
        PT = X("b_PT", [P, NPAGE, 64])
        wT = X("b_wT", [P, WIN // P, 64])
        pc, pcg, pgT, pcT = X("b_pc", [64, P]), X("b_pcg", [64, P]), X("b_pgT", [P, 64]), X("b_pcT", [P, 64])
        score, top, msk = X("b_score", [64, 3, 40]), X("b_top", [64, 2, 8]), X("b_msk", [64, 40])
        st, pdd, pd = X("b_st", [64, 16]), X("b_pdd", [64, 2, 64]), X("b_pd", [TS, 2, 64])
        v_hi = L.at("b_vhi", A_DN, [P, 4, NPAGE, P])
        vw_lo = L.at("b_vwlo", A_DN + 32768, [P, TS - 1, WIN // P, P])
        vw_hi = X("b_vwhi", [P, 1, WIN // P, P])
        osb = X("b_o", [NH, TS, P])
        NW = WIN // P
        block = ctx.enter_context(nc.Block())

        def load_values(queue, b, loaded):
            v = v_lo[:, b] if b < 4 else v_hi[:, b - 4]
            for p in range(NPAGE):
                page = queue.value_load(pages[0:1, NPAGE * b + p:NPAGE * b + p + 1], min_val=0, max_val=cache.shape[0] - 1)
                queue.dma_start(v[:, p, :], cache[bass.ds(page, 1), :, 3 * P:4 * P].rearrange("a t c -> (a t) c")).then_inc(loaded, 16)

        @block.sync
        def _(sp):
            for b in range(4):
                load_values(sp, b, v_loaded)
            for b in range(TS):
                dst = vw_lo[:, b] if b < TS - 1 else vw_hi[:, 0]
                sp.dma_start(dst, state_win[b, :, P:2 * P].rearrange("(t p) c -> p t c", p=P)).then_inc(vw_loaded, 16)

        @block.gpsimd
        def _(pool):
            for b in (4, 5):
                load_values(pool, b, pool_v_loaded)

        @block.tensor
        def _(pe):
            for b in range(TS):
                ins = nc.tensor.matmul(PS[6][0:64, 0:NCS], qbd[:, b, :], kcsT[:, b, 0:NCS], start=(b == 0), stop=(b == TS - 1))
            ins.then_inc(c_done, 1)
            pe.wait_ge(p_ready, 1)
            nc.tensor.matmul(PS[5][0:NCS, 0:64], pc[:, 0:NCS], C["group"][0:64, :], start=True, stop=True).then_inc(grouped, 1)
            pe.wait_ge(pg_ready, 1)
            nc.tensor.transpose(PS[7][0:NCS, 0:64], pcg[:, 0:NCS], C["ident"][0:64, 0:64]).then_inc(ct_done, 1)
            pe.wait_ge(g_copied, 1)
            nc.tensor.matmul(PS[6][0:64, 0:NSEL], pgT[0:NCS, :], C["ovl"][0:NCS, :], start=True, stop=True).then_inc(imp_done, 1)
            pe.wait_ge(pd_ready, 2)
            for h in range(2):
                for t in range(8):
                    k = 8 * h + t
                    ins = nc.tensor.transpose(PS[4 + h][:, t * 64:(t + 1) * 64], ss[:, k * P:(k + 1) * P], C["ident"][0:64, 0:64])
                ins.then_inc(pt_done, 1)
            for t in range(NW):
                ins = nc.tensor.transpose(PS[0][:, t * 64:(t + 1) * 64], sw[:, t * P:(t + 1) * P], C["ident"][0:64, 0:64])
            ins.then_inc(pt_done, 1)
            nc.tensor.matmul(PS[6][0:TS, 0:P], C["seq"][0:64, :], pdd[:, :, :].rearrange("r i c -> r (i c)"), start=True, stop=True).then_inc(pd_done, 1)
            pe.wait_ge(pd_copied, 1)
            pe.wait_ge(ct_copied, 1)
            pe.wait_ge(act_pt, 1)
            pe.wait_ge(dve_pt, 2)
            pe.wait_ge(vw_loaded, 16 * TS)
            pe.wait_ge(v_loaded, 16 * 6 * NPAGE)
            pe.wait_ge(pool_v_loaded, 16 * 2 * NPAGE)
            for b in range(TS):
                cols = slice(8 * b, 8 * b + 8)
                o = PS[1 + b // 4][0:NH, P * (b % 4):P * (b % 4) + P]
                v = v_lo[:, b] if b < 4 else v_hi[:, b - 4]
                w = vw_lo[:, b] if b < TS - 1 else vw_hi[:, 0]
                nc.tensor.matmul(o, pd[:, 0, cols], Rs[:, VS0:VS0 + P], start=True, stop=False)
                nc.tensor.matmul(o, pd[:, 1, cols], Rs[:, VW0:VW0 + P], start=False, stop=False)
                for t in range(NPAGE):
                    nc.tensor.matmul(o, PT[:, t, cols], v[:, t, :], start=False, stop=False)
                for t in range(NW):
                    nc.tensor.matmul(o, wT[:, t, cols], w[:, t, :], start=False, stop=False)
                ins = nc.tensor.matmul(o, pcT[0:NCS, cols], vcs[0:NCS, b, :], start=False, stop=True)
                if b % 4 == 3:
                    ins.then_inc(o_done, 1)
            pe.wait_ge(o_copied, 2)
            for b in range(TS):
                ins = nc.tensor.transpose(PS[3][:, 8 * b:8 * b + 8], osb[:, b, :], C["ident"][0:NH, 0:NH])
            ins.then_inc(otp_done, 1)

        @block.scalar
        def _(act):
            for b in (6, 7):
                load_values(act, b, v_loaded)
            act.wait_ge(max_done, 1)
            nc.scalar.activation(pc[:, 0:NCS], PS[6][0:64, 0:NCS], ACT.Exp, bias=st[:, 0:1], accum_out=st[:, 1:2]).then_inc(exp_done, 1)
            act.wait_ge(grouped, 1)
            nc.scalar.copy(pgT[0:NCS, :], PS[5][0:NCS, 0:64]).then_inc(g_copied, 1)
            act.wait_ge(ct_done, 1)
            nc.scalar.copy(pcT[0:NCS, :], PS[7][0:NCS, 0:64]).then_inc(ct_copied, 1)
            act.wait_ge(max_done, 2)
            nc.scalar.activation(sw[:, 1:WIN + 1], sw[:, 1:WIN + 1], ACT.Exp, bias=st[:, 4:5], accum_out=st[:, 6:7]).then_inc(exp_done, 1)
            act.wait_ge(max_done, 3)
            nc.scalar.activation(ss[:, :], ss[:, :], ACT.Exp, bias=st[:, 3:4], accum_out=st[:, 5:6]).then_inc(exp_done, 1)
            act.wait_ge(pt_done, 1)
            nc.scalar.copy(PT[:, 0:8, :], PS[4][:, :].rearrange("p (t r) -> p t r", r=64)).then_inc(act_pt, 1)

        @block.vector
        def _(dve):
            step = Steps(dve, dve_step)
            dve.wait_ge(c_done, 1)
            nc.vector.tensor_reduce(st[:, 0:1], PS[6][0:64, 0:NCS], AX.X, ALU.max, negate=True).then_inc(max_done, 1)
            nc.vector.tensor_reduce(st[:, 4:5], sw[:, 1:WIN + 1], AX.X, ALU.max, negate=True).then_inc(max_done, 1)
            dve.wait_ge(exp_done, 1)
            step(nc.vector.reciprocal(st[:, 2:3], st[:, 1:2]))
            nc.vector.tensor_scalar(pc[:, 0:NCS], pc[:, 0:NCS], st[:, 2:3], None, ALU.mult).then_inc(p_ready, 1)
            dve.wait_ge(p_ready, 1)
            nc.vector.tensor_scalar(pcg[:, 0:NCS], pc[:, 0:NCS], g64[:, 0:1], None, ALU.mult).then_inc(pg_ready, 1)
            dve.wait_ge(imp_done, 1)
            step(nc.vector.tensor_tensor(score[:, 0, 0:NSEL], PS[6][0:64, 0:NSEL], C["bonus"][0:64, :], ALU.add))
            for r in range(2):
                step(nc.vector.max(top[:, r, :], score[:, r, 0:NSEL]))
                step(nc.vector.match_replace(score[:, r + 1, 0:NSEL], top[:, r, :], score[:, r, 0:NSEL], -BIG))
            step(nc.vector.tensor_scalar(msk[:, 0:NSEL], score[:, 2, 0:NSEL], -BIG, None, ALU.is_equal))
            step(nc.vector.tensor_scalar(msk[:, 0:NSEL], msk[:, 0:NSEL], -1.0, BIG, ALU.add, ALU.mult))
            nc.vector.tensor_tensor(ss[:, 0:PAST].rearrange("r (s k) -> r s k", k=64), PS[8][0:64, 0:PAST].rearrange("r (s k) -> r s k", k=64),
                                    msk[:, 0:NSEL - 1].unsqueeze(2).to_broadcast([64, NSEL - 1, 64]), ALU.add)
            step(nc.vector.tensor_tensor(ss[:, PAST:PAST + 1], snew[:, 0:1], msk[:, NSEL - 1:NSEL], ALU.add))
            nc.vector.tensor_reduce(st[:, 3:4], ss[:, :], AX.X, ALU.max, negate=True).then_inc(max_done, 1)
            dve.wait_ge(exp_done, 3)
            step(nc.vector.reciprocal(st[:, 8:10], st[:, 5:7]))
            step(nc.vector.tensor_tensor(st[:, 10:12], st[:, 8:10], g64[:, 1:3], ALU.mult))
            nc.vector.memset(sw[:, 0:1], 0.0)
            step(nc.vector.tensor_scalar(ss[:, :], ss[:, :], st[:, 10:11], None, ALU.mult))
            step(nc.vector.tensor_scalar(sw[:, 1:WIN + 1], sw[:, 1:WIN + 1], st[:, 11:12], None, ALU.mult))
            nc.vector.tensor_scalar(pdd[:, 0, :], C["ident"][0:64, 0:64], ss[:, PAST:PAST + 1], None, ALU.mult).then_inc(pd_ready, 1)
            nc.vector.tensor_scalar(pdd[:, 1, :], C["ident"][0:64, 0:64], sw[:, WIN:WIN + 1], None, ALU.mult).then_inc(pd_ready, 1)
            dve.wait_ge(pt_done, 2)
            nc.vector.tensor_copy(PT[:, 8:16, :], PS[5][:, :].rearrange("p (t r) -> p t r", r=64)).then_inc(dve_pt, 1)
            dve.wait_ge(pt_done, 3)
            nc.vector.tensor_copy(wT[:, :, :], PS[0][:, 0:64 * NW].rearrange("p (t r) -> p t r", r=64)).then_inc(dve_pt, 1)
            dve.wait_ge(pd_done, 1)
            nc.vector.tensor_copy(pd[:, :, :], PS[6][0:TS, 0:P].rearrange("b (i r) -> b i r", r=64)).then_inc(pd_copied, 1)
            for i in range(2):
                dve.wait_ge(o_done, i + 1)
                nc.vector.tensor_copy(osb[:, 4 * i:4 * i + 4, :], PS[1 + i][0:NH, :].rearrange("h (b c) -> h b c", c=P)).then_inc(o_copied, 1)
            dve.wait_ge(otp_done, 1)
            o = PS[3][:, 0:64].rearrange("p (b h) -> p h b", h=NH)
            for g in range(2):
                nc.vector.tensor_copy(oaT[64 * g:64 * g + 64, :, TP:TT], o[64 * g:64 * g + 64, 4 * g:4 * g + 4, :])


def block_merge(nc, L, PS, C, w_in, w_a, w_b, hT, oaT, obT, mixed):
    ctx = ExitStack()
    with ctx:
        sem = L.signals.named("x_")
        wab_loaded, mm_done, sig_done, t_done, m_done = map(sem, ("wab_loaded", "mm", "sig", "t", "m"))
        g_loaded = [sem(f"g_loaded{i}") for i in range(3)]
        wa = L.at("x_wa", A_R, [P, 4, D])
        wb = L.at("x_wb", A_R + 16384, [P, 4, D])
        T = Region(L, A_R + 32768, A_R + 41856)
        sg = [T(f"x_sig{i}", [P, 2, 512]) for i in range(2)]
        wg = [L.at(f"x_wg{i}", A_DN + 16384 * i, [P, KD, 2, 256]) for i in range(3)]
        wv = w_in.rearrange("(k p) n -> p k n", p=P)
        units = [(m, t0, n) for m in range(KD) for t0, n in THIRDS]
        block = ctx.enter_context(nc.Block())

        @block.sync
        def _(sp):
            for g in range(2):
                sp.dma_start(wa[64 * g:64 * g + 64, :, :], w_a[256 * g:256 * g + 256].rearrange("(j d) n -> d j n", d=HD)).then_inc(wab_loaded, 16)
            for q in range(4):
                if q == 1:
                    sp.dma_start(wb[:, :, :], w_b.rearrange("(j p) n -> p j n", p=P)).then_inc(wab_loaded, 16)
                if q >= 3:
                    sp.wait_ge(mm_done, 6 * (q - 2))
                for i, at in enumerate((MA0, MB0)):
                    sp.dma_start(wg[q % 3][:, :, i, :], wv[:, :, at + 256 * q:at + 256 * q + 256]).then_inc(g_loaded[q % 3], 16)

        @block.tensor
        def _(pe):
            for u, (m, t0, n) in enumerate(units):
                q, c = m // 2, 128 * (m % 2)
                if m % 2 == 0 and t0 == 0:
                    pe.wait_ge(g_loaded[q % 3], 32 * (q // 3 + 1))
                b = 4 * (u % 2)
                if u >= 2:
                    pe.wait_ge(t_done, 2 * (u - 1))
                for i in range(2):
                    for k in range(KD):
                        ins = nc.tensor.matmul(PS[b + i][:, 0:n], wg[q % 3][:, k, i, c:c + P], hT[:, k, t0:t0 + n], start=(k == 0), stop=(k == KD - 1))
                if u == 0:
                    pe.wait_ge(wab_loaded, 48)
                for i, (w, o) in enumerate(((wa, oaT), (wb, obT))):
                    for k in range(4):
                        ins = nc.tensor.matmul(PS[b + 2 + i][:, 0:n], w[:, k, m * P:(m + 1) * P], o[:, k, t0:t0 + n], start=(k == 0), stop=(k == 3))
                ins.then_inc(mm_done, 1)

        @block.scalar
        def _(act):
            for u, (m, t0, n) in enumerate(units):
                act.wait_ge(mm_done, u + 1)
                if u >= 2:
                    act.wait_ge(m_done, u - 1)
                for i in range(2):
                    nc.scalar.activation(sg[u % 2][:, i, 0:n], PS[4 * (u % 2) + i][:, 0:n], ACT.Sigmoid).then_inc(sig_done, 1)

        @block.vector
        def _(dve):
            for u, (m, t0, n) in enumerate(units):
                for i in range(2):
                    dve.wait_ge(sig_done, 2 * u + i + 1)
                    nc.vector.tensor_tensor(sg[u % 2][:, i, 0:n], sg[u % 2][:, i, 0:n], PS[4 * (u % 2) + 2 + i][:, 0:n], ALU.mult).then_inc(t_done, 1)

        @block.gpsimd
        def _(pool):
            for u, (m, t0, n) in enumerate(units):
                pool.wait_ge(t_done, 2 * u + 2)
                nc.gpsimd.tensor_tensor(mixed[m][:, t0:t0 + n], sg[u % 2][:, 0, 0:n], sg[u % 2][:, 1, 0:n], ALU.add).then_inc(m_done, 1)


def block_out(nc, L, PS, C, x_p, x_s, w_out, norm_ffn, w_rg, w_re, b_rg, b_re, mixed, x1, h2_rows, logits):
    ctx = ExitStack()
    with ctx:
        sem = L.signals.named("o_")
        w_loaded, small_loaded, zeroed, zero_stored, mm_done, x1_done, sq_done, mean_done, r_done, xn_done, h2_done, tp_done, h2T_done, lg_done, lg_copied, bias_done = map(
            sem, ("w_loaded", "small", "zeroed", "zero_stored", "mm", "x1", "sq", "mean", "r", "xn", "h2", "tp", "h2T", "lg", "lg_copied", "bias"))
        x_loaded = [sem("x_loaded0"), sem("x_loaded1")]
        h2_stored = [sem("h2_stored0"), sem("h2_stored1")]
        wo = L.at("o_w", A_HT, [P, KD, D])
        Y = Region(L, A_DN, A_OA)
        x = Y("o_x", [P, 2, D])
        junk = Y("o_junk", [P, D])
        h2 = Y("o_h2", [P, 2, D])
        h2T = Y("o_h2T", [P, 2, KD, P])
        gain = Y("o_gain", [P, D])
        wr = Y("o_wr", [P, KD, NG + NE])
        bias = Y("o_bias", [P, NG + NE])
        zrow = Y("o_zero", [1, D])
        ss, mean, r = Y("o_ss", [P, 16]), Y("o_mean", [P, 16]), Y("o_r", [P, 16])
        tiles = [(t, P) for t in range(NT)] + [(NT, TS)]
        block = ctx.enter_context(nc.Block())

        def store(sp, t):
            n = tiles[t][1]
            sp.wait_ge(h2_done, t + 1)
            sp.dma_start(h2_rows[t * P:t * P + n, :], h2[0:n, t % 2, :]).then_inc(h2_stored[t % 2], 16)

        @block.sync
        def _(sp):
            for t, n in tiles:
                if t >= 2:
                    sp.wait_ge(x1_done, t - 1)
                src = x_p[0, t * P:(t + 1) * P, :] if t < NT else x_s[:, 0, :]
                sp.dma_start(x[0:n, t % 2, :], src).then_inc(x_loaded[t % 2], 16)
                if t == 0:
                    sp.dma_start(wo[:, :, :], w_out.rearrange("(k p) n -> p k n", p=P)).then_inc(w_loaded, 16)
                    sp.dma_start(gain[:, :], norm_ffn.unsqueeze(0).to_broadcast([P, D])).then_inc(small_loaded, 16)
                    sp.dma_start(wr[:, :, 0:NG], w_rg.rearrange("(k p) n -> p k n", p=P)).then_inc(small_loaded, 16)
                    sp.dma_start(wr[:, :, NG:NG + NE], w_re.rearrange("(k p) n -> p k n", p=P)).then_inc(small_loaded, 16)
                    sp.dma_start(bias[:, 0:NG], b_rg.unsqueeze(0).to_broadcast([P, NG])).then_inc(small_loaded, 16)
                    sp.dma_start(bias[:, NG:NG + NE], b_re.unsqueeze(0).to_broadcast([P, NE])).then_inc(small_loaded, 16)
                if t >= 1:
                    store(sp, t - 1)
            store(sp, NT)
            sp.wait_ge(h2_stored[0], 16 * 5)
            sp.wait_ge(h2_stored[1], 16 * 4)
            sp.wait_ge(zeroed, 1)
            sp.dma_start(h2_rows[TT:TT + 1, :], zrow[:, :]).then_inc(zero_stored, 16)
            sp.wait_ge(zero_stored, 16)

        @block.tensor
        def _(pe):
            def project(t, n):
                if t >= 2:
                    pe.wait_ge(x1_done, t - 1)
                for half in range(2):
                    for k in range(KD):
                        ins = nc.tensor.matmul(PS[2 * (t % 2) + half][0:n, :], mixed[k][:, t * P:t * P + n], wo[:, k, 512 * half:512 * half + 512], start=(k == 0), stop=(k == KD - 1))
                ins.then_inc(mm_done, 1)

            pe.wait_ge(w_loaded, 16)
            project(0, P)
            for t, n in tiles:
                if t + 1 < len(tiles):
                    project(*tiles[t + 1])
                pe.wait_ge(h2_done, t + 1)
                if t >= 1:
                    pe.wait_ge(h2T_done, t)
                for k in range(KD):
                    ins = nc.tensor.transpose(PS[4 + k // 4][:, (k % 4) * P:(k % 4) * P + n], h2[0:n, t % 2, k * P:(k + 1) * P], C["ident"][0:n, 0:n])
                ins.then_inc(tp_done, 1)
                pe.wait_ge(h2T_done, t + 1)
                if t == 0:
                    pe.wait_ge(small_loaded, 80)
                if t >= 2:
                    pe.wait_ge(lg_copied, t - 1)
                for k in range(KD):
                    ins = nc.tensor.matmul(PS[6 + t % 2][0:n, 0:NG + NE], h2T[:, t % 2, k, 0:n], wr[:, k, :], start=(k == 0), stop=(k == KD - 1))
                ins.then_inc(lg_done, 1)

        @block.vector
        def _(dve):
            nc.vector.memset(zrow[:, :], 0.0).then_inc(zeroed, 1)
            nc.vector.memset(logits[:, NT, :], 0.0).then_inc(zeroed, 1)
            dve.wait_ge(zeroed, 2)

            def copy_logits(t, n):
                dve.wait_ge(lg_done, t + 1)
                nc.vector.tensor_tensor(logits[0:n, t, :], PS[6 + t % 2][0:n, 0:NG + NE], bias[0:n, :], ALU.add).then_inc(lg_copied, 1)

            dve.wait_ge(small_loaded, 80)
            for t, n in tiles:
                dve.wait_ge(mm_done, t + 1)
                dve.wait_ge(x_loaded[t % 2], 16 * (t // 2 + 1))
                for half in range(2):
                    s = slice(512 * half, 512 * half + 512)
                    ins = nc.vector.tensor_tensor(x1[0:n, t, s], PS[2 * (t % 2) + half][0:n, :], x[0:n, t % 2, s], ALU.add)
                ins.then_inc(x1_done, 1)
                dve.wait_ge(r_done, t + 1)
                if t >= 2:
                    dve.wait_ge(h2_stored[t % 2], 16 * (t // 2))
                    dve.wait_ge(tp_done, t - 1)
                nc.vector.tensor_scalar(h2[0:n, t % 2, :], x1[0:n, t, :], r[0:n, t:t + 1], None, ALU.mult).then_inc(xn_done, 1)
                if t >= 1:
                    copy_logits(*tiles[t - 1])
            copy_logits(*tiles[NT])

        @block.scalar
        def _(act):
            for t, n in tiles:
                act.wait_ge(x1_done, t + 1)
                if t >= 1:
                    act.wait_ge(sq_done, t)
                nc.scalar.activation(junk[0:n, :], x1[0:n, t, :], ACT.Square, accum_out=ss[0:n, t:t + 1]).then_inc(sq_done, 1)
                act.wait_ge(tp_done, t + 1)
                if t >= 2:
                    act.wait_ge(lg_done, t - 1)
                for half in range(2):
                    ins = nc.scalar.copy(h2T[:, t % 2, 4 * half:4 * half + 4, 0:n], PS[4 + half][:, :].rearrange("p (k n) -> p k n", k=4)[:, :, 0:n])
                ins.then_inc(h2T_done, 1)

        @block.gpsimd
        def _(pool):
            pool.wait_ge(small_loaded, 80)
            for t, n in tiles:
                pool.wait_ge(sq_done, t + 1)
                nc.gpsimd.tensor_scalar(mean[0:n, t:t + 1], ss[0:n, t:t + 1], 1.0 / D, EPS, ALU.mult, ALU.add).then_inc(mean_done, 1)
                pool.wait_ge(mean_done, t + 1)
                nc.gpsimd.tensor_tensor(r[0:n, t:t + 1], mean[0:n, t:t + 1], C["mhalf"][0:n, 0:1], ALU.pow).then_inc(r_done, 1)
                pool.wait_ge(xn_done, t + 1)
                nc.gpsimd.tensor_tensor(h2[0:n, t % 2, :], h2[0:n, t % 2, :], gain[0:n, :], ALU.mult).then_inc(h2_done, 1)


def expert_weights(L, w_gate, w_up, w_down):
    sem = L.signals.named("f_")
    gu_loaded, d_loaded = ([sem(n + str(i)) for i in range(2)] for n in ("gu_loaded", "d_loaded"))
    W = [L.at(f"f_W{i}", A_W + 49152 * i, [P, 3 * 4096]) for i in range(2)]
    wg, wu = ([w[:, o:o + 4096].rearrange("p (k n) -> p k n", k=KD) for w in W] for o in (0, 4096))
    wd = [w[:, 8192:12288].rearrange("p (k n) -> p k n", k=4) for w in W]
    source = lambda w, e: w.rearrange("e (k p) n -> e p k n", p=P)[bass.ds(e, 1)].rearrange("a p k n -> (a p) k n")

    def load_gate_and_up(queue, par, e):
        for dst, w in ((wg[par], w_gate), (wu[par], w_up)):
            queue.dma_start(dst, source(w, e)).then_inc(gu_loaded[par], 16)

    def load_down(queue, par, e):
        queue.dma_start(wd[par], source(w_down, e)).then_inc(d_loaded[par], 16)

    return wg, wu, wd, gu_loaded, d_loaded, load_gate_and_up, load_down


def block_route(nc, L, PS, C, logits, slot, weight, blocks, table, weights):
    NT1 = NT + 1
    TILES = [(t, P) for t in range(NT)] + [(NT, TS)]
    ctx = ExitStack()
    with ctx:
        sem = L.signals.named("t_")
        step_sem, exp_in, exp_done, a_ready, rank_done, filled, fill_ready, slot_ready, scattered, blocks_ready = map(
            sem, ("step", "exp_in", "exp", "a_ready", "rank", "filled", "fill_ready", "slot_ready", "scattered", "blocks_ready"))
        load_gate_and_up, load_down = weights[5:]
        Y = Region(L, A_W + 49152, A_OA)
        g, e = logits[:, :, 0:NG], logits[:, :, NG:NG + NE]
        N = lambda name, n: Y("t_" + name, [P, NT1, n])
        mx, gi, den = N("mx", 1), N("gi", 1), N("den", 1)
        ga, gb = N("ga", NG), N("gb", NG)
        le, tmp, tmp2 = N("le", NE), N("tmp", NE), N("tmp2", NE)
        oh = [N("oh1", NE), N("oh2", NE)]
        m1, m2, ei = N("m1", 1), N("m2", 1), N("ei", 1)
        A = N("A", NE)
        before = Y("t_before", [P, NT1 + 1, NE])
        ex, w1 = N("ex", 1), N("w1", 1)
        count, nb, end, end2, start = (Y("t_" + s, [P, NE]) for s in ("count", "nb", "end", "end2", "start"))
        cmpb = Y("t_cmp", [P, NE, NT1])
        eb = Y("t_eb", [P, MAXBLK, NE])
        ebs = Y("t_ebs", [P, MAXBLK])
        slotf = Y("t_slotf", [P, NT1, 2])
        fill = Y("t_fill", [P, MAXBLK + 2, 2], I32)
        tok = Y("t_tok", [P, NT1, 2, 2], I32)
        b3 = lambda x, n: x.to_broadcast([P, NT1, n])
        block = ctx.enter_context(nc.Block())

        @block.vector
        def _(dve):
            step = Steps(dve, step_sem)
            V = nc.vector
            ids = C["eid"].unsqueeze(1)

            def first_max(x, n, idx, onehot, scratch, m):
                step(V.tensor_reduce(m[:, :, 0], x, AX.X, ALU.max))
                step(V.tensor_tensor(scratch, x, b3(m[:, :, :], n), ALU.not_equal))
                step(V.scalar_tensor_tensor(scratch, scratch, 100.0, ids[:, :, 0:n].to_broadcast([P, NT1, n]), ALU.mult, ALU.add))
                step(V.tensor_reduce(idx[:, :, 0], scratch, AX.X, ALU.min))
                step(V.tensor_tensor(onehot, ids[:, :, 0:n].to_broadcast([P, NT1, n]), b3(idx[:, :, :], n), ALU.is_equal))

            V.memset(fill[:, :, 0], TT).then_inc(fill_ready, 1)
            V.memset(fill[:, :, 1], 2 * TT).then_inc(fill_ready, 1)
            V.tensor_copy(tok[:, :, :, :], C["tok"].rearrange("p (t k c) -> p t k c", k=2, c=2)).then_inc(fill_ready, 1)
            first_max(g, NG, gi, gb[:, :, :], ga[:, :, :], mx)
            V.tensor_tensor(ga[:, :, :], g, b3(mx[:, :, :], NG), ALU.subtract).then_inc(exp_in, 1)
            step(V.tensor_scalar(gb[:, :, :], gb[:, :, :], -1.0, BIG, ALU.add, ALU.mult))
            for t in range(NT1):
                ins = V.tensor_tensor(le[:, t, :].rearrange("p (g e) -> p g e", g=NG), e[:, t, :].rearrange("p (g e) -> p g e", g=NG),
                                      gb[:, t, :].unsqueeze(2).to_broadcast([P, NG, EPG]), ALU.add)
                if t == NT1 - 1:
                    step(ins)
            first_max(le[:, :, :], NE, ei, oh[0][:, :, :], tmp[:, :, :], m1)
            step(V.scalar_tensor_tensor(tmp2[:, :, :], oh[0][:, :, :], -3.0 * BIG, le[:, :, :], ALU.mult, ALU.add))
            first_max(tmp2[:, :, :], NE, ei, oh[1][:, :, :], tmp[:, :, :], m2)
            V.tensor_tensor(ex[:, :, :], m2[:, :, :], m1[:, :, :], ALU.subtract).then_inc(exp_in, 1)
            step(V.tensor_tensor(A[:, :, :], oh[0][:, :, :], oh[1][:, :, :], ALU.add))
            step(V.tensor_tensor(A[:, NT, :], A[:, NT, :], C["tokvalid"].to_broadcast([P, NE]), ALU.mult))
            step(V.memset(before[:, 0, :], 0.0))
            for t in range(NT1):
                ins = V.tensor_tensor(before[:, t + 1, :], before[:, t, :], A[:, t, :], ALU.add)
                if t < NT:
                    step(ins)
            ins.then_inc(a_ready, 1)
            dve.wait_ge(exp_done, 2)
            step(V.tensor_reduce(den[:, :, 0], ga[:, :, :], AX.X, ALU.add))
            step(V.tensor_scalar(w1[:, :, :], ex[:, :, :], 1.0, None, ALU.add))
            step(V.tensor_tensor(w1[:, :, :], w1[:, :, :], den[:, :, :], ALU.mult))
            step(V.reciprocal(weight[:, :, 0], w1[:, :, 0]))
            step(V.tensor_tensor(weight[:, :, 1], weight[:, :, 0], ex[:, :, 0], ALU.mult))
            dve.wait_ge(rank_done, 1)
            step(V.tensor_copy(count[:, :], PS[1][:, 0:NE]))
            step(V.tensor_tensor(cmpb[:, :, :], count[:, :].unsqueeze(2).to_broadcast([P, NE, NT1]), C["blk"][:, 0:NT1].unsqueeze(1).to_broadcast([P, NE, NT1]), ALU.is_gt))
            step(V.tensor_reduce(nb[:, :], cmpb[:, :, :], AX.X, ALU.add))
            cur, nxt = nb, end
            for s in (1, 2, 4, 8, 16):
                V.tensor_copy(nxt[:, 0:s], cur[:, 0:s])
                step(V.tensor_tensor(nxt[:, s:NE], cur[:, s:NE], cur[:, 0:NE - s], ALU.add))
                cur, nxt = nxt, (end2 if nxt is end else end)
            step(V.tensor_tensor(start[:, :], cur[:, :], nb[:, :], ALU.subtract))
            step(V.tensor_scalar(start[:, :], start[:, :], float(P), None, ALU.mult))
            step(V.tensor_tensor(tmp[:, :, :], PS[0][:, 0:NT1 * NE].rearrange("p (t e) -> p t e", e=NE), start[:, :].unsqueeze(1).to_broadcast([P, NT1, NE]), ALU.add))
            for k in range(2):
                step(V.tensor_tensor(tmp2[:, :, :], tmp[:, :, :], oh[k][:, :, :], ALU.mult))
                step(V.tensor_reduce(slotf[:, :, k], tmp2[:, :, :], AX.X, ALU.add))
            V.tensor_copy(slot[:, :, :], slotf[:, :, :]).then_inc(slot_ready, 1)
            step(V.tensor_tensor(eb[:, :, :], cur[:, :].unsqueeze(1).to_broadcast([P, MAXBLK, NE]), C["blkid"].unsqueeze(2).to_broadcast([P, MAXBLK, NE]), ALU.is_le))
            step(V.tensor_reduce(ebs[:, :], eb[:, :, :], AX.X, ALU.add))
            step(V.tensor_scalar(ebs[:, :], ebs[:, :], float(NE - 1), None, ALU.min))
            V.tensor_copy(blocks[0:1, 0:MAXBLK], ebs[0:1, :])
            V.tensor_copy(blocks[0:1, MAXBLK:MAXBLK + 1], cur[0:1, NE - 1:NE]).then_inc(blocks_ready, 1)

        @block.sync
        def _(sp):
            sp.wait_ge(blocks_ready, 1)
            e = sp.value_load(blocks[0:1, 0:1], min_val=0, max_val=NE - 1)
            load_gate_and_up(sp, 0, e)
            load_down(sp, 0, e)

        @block.scalar
        def _(act):
            act.wait_ge(exp_in, 1)
            nc.scalar.activation(ga[:, :, :], ga[:, :, :], ACT.Exp).then_inc(exp_done, 1)
            act.wait_ge(exp_in, 2)
            nc.scalar.activation(ex[:, :, :], ex[:, :, :], ACT.Exp).then_inc(exp_done, 1)

        @block.tensor
        def _(pe):
            pe.wait_ge(a_ready, 1)
            cols = lambda x: x.rearrange("p t e -> p (t e)")
            nc.tensor.matmul(PS[0][:, 0:NE * NT1], C["strictT"], cols(A[:, :, :]), start=True, stop=False)
            nc.tensor.matmul(PS[0][:, 0:NE * NT1], C["ones"], cols(before[:, 0:NT1, :]), start=False, stop=True)
            nc.tensor.matmul(PS[1][:, 0:NE], C["ones"], before[:, NT1, :], start=True, stop=True).then_inc(rank_done, 1)

        @block.gpsimd
        def _(pool):
            pool.wait_ge(fill_ready, 3)
            pool.dma_start(table.rearrange("(p b) c -> p b c", p=P), fill[:, :, :]).then_inc(filled, 16)
            pool.wait_ge(filled, 16)
            pool.wait_ge(slot_ready, 1)
            for t, n in TILES:
                for k in range(2):
                    pool.indirect_dma_start(out=table, out_offset=bass.IndirectOffsetOnAxis(ap=slot[0:n, t, k:k + 1], axis=0),
                                            in_=tok[0:n, t, k, :], in_offset=None).then_inc(scattered, 16)
            pool.wait_ge(scattered, 16 * 2 * NT1)


def block_experts(nc, L, PS, C, weights, h2_rows, table, blocks, expert_out):
    ctx = ExitStack()
    with ctx:
        sem = L.signals.named("f_")
        slots_loaded, slots_float, slots_tp, slots_ready = map(sem, ("slots", "slots_float", "slots_tp", "slots_ready"))
        wg, wu, wd, gu_loaded, d_loaded, load_gate_and_up, load_down = weights
        (x_loaded, stored, gidx_ready, sidx_ready, tp_done, xT_act, xT_dve, gu_done, silu_done, a_done, atp_done,
         aT_done, down_done, out_act, out_dve, out_free) = ([sem(n + str(i)) for i in range(2)] for n in (
             "x_loaded", "stored", "gidx", "sidx", "tp", "xT_act", "xT_dve", "gu", "silu", "a", "atp",
             "aT", "down", "out_act", "out_dve", "out_free"))
        T = Region(L, A_HT, A_CONST)
        x = [T(f"f_x{i}", [P, D]) for i in range(2)]
        xT = [T(f"f_xT{i}", [P, KD, P]) for i in range(2)]
        sg, a = T("f_sg", [P, FE]), T("f_a", [P, FE])
        aT = T("f_aT", [P, 4, P])
        out = [T(f"f_out{i}", [P, D]) for i in range(2)]
        tokens = L.at("f_tokens", A_W + 98304, [P, MAXBLK + 2, 2], I32)
        gidx, sidx = (L.at(f"f_idx{i}", A_W + 98304 + 416 + 32 * i, [P, 2, 2], I32) for i in range(2))
        NB = MAXBLK + 2
        raw, rawf = T("f_raw", [NB, P, 2], I32), T("f_rawf", [NB, 2, P])
        block = ctx.enter_context(nc.Block())

        def each_block(engine, first=None, tail=None, rest=None):
            nothing = lambda *a: None
            first, tail, rest = first or nothing, tail or nothing, rest or nothing
            n = engine.value_load(blocks[0:1, MAXBLK:MAXBLK + 1], min_val=MINBLK, max_val=MAXBLK)
            first(0, 1, 1, 0)
            rest(0, 1, 1)
            with engine.Fori(0, MAXBLK // 2) as i:
                for par, b, number in ((1, 2 * i + 1, i + 1), (0, 2 * i + 2, i + 2)):
                    with engine.If(b < n):
                        first(par, number, i + 2, b)
                    if tail is not nothing:
                        with engine.If(b < n + 1):
                            tail(1 - par, i + 1)
                    if rest is not nothing:
                        with engine.If(b < n):
                            rest(par, number, i + 2)
            return n

        @block.sync
        def _(sp):
            for pair in (gu_done, down_done, tp_done, out_act, out_dve, out_free):
                for s in pair:
                    sp.sem_inc(s, 1)

            sp.dma_start(raw[:, :, :], table.rearrange("(b p) c -> b p c", p=P)).then_inc(slots_loaded, 16)

            def load(par, u, u_next, b):
                if isinstance(b, int):
                    return
                e = sp.value_load(blocks[0:1, bass.ds(b, 1)], min_val=0, max_val=NE - 1)
                sp.wait_ge(gu_done[par], u)
                load_gate_and_up(sp, par, e)
                sp.wait_ge(down_done[par], u)
                load_down(sp, par, e)

            each_block(sp, load)

        @block.gpsimd
        def _(pool):
            pool.wait_ge(slots_ready, 2)
            turn = pool.alloc_register("turn")

            def gather(par, count, b):
                nc.gpsimd.tensor_copy(gidx[:, par, :], tokens[:, bass.ds(b, 1), :].rearrange("p b c -> p (b c)")).then_inc(gidx_ready[par], 1)
                pool.wait_ge(slots_ready, 2)
                pool.wait_ge(gidx_ready[par], count)
                pool.indirect_dma_start(out=x[par][:, :], out_offset=None, in_=h2_rows,
                                        in_offset=bass.IndirectOffsetOnAxis(ap=gidx[:, par, 0:1], axis=0)).then_inc(x_loaded[par], 16)

            def gather_next(par, u, u_next, b):
                pool.wait_ge(tp_done[1 - par], u_next)
                pool.reg_mov(turn, u_next)
                count = pool.snap(turn)
                gather(1 - par, count, b + 1)

            def scatter(par, u):
                nc.gpsimd.tensor_copy(sidx[:, par, :], tokens[:, bass.ds(2 * u - 2 + par, 1), :].rearrange("p b c -> p (b c)")).then_inc(sidx_ready[par], 1)
                pool.wait_ge(sidx_ready[par], u)
                pool.wait_ge(out_act[par], u + 1)
                pool.reg_mov(turn, u + 1)
                count = pool.snap(turn)
                pool.wait_ge(slots_ready, 2)
                pool.wait_ge(out_dve[par], count)
                pool.indirect_dma_start(out=expert_out, out_offset=bass.IndirectOffsetOnAxis(ap=sidx[:, par, 1:2], axis=0),
                                        in_=out[par][:, :], in_offset=None).then_inc(stored[par], 16)
                pool.wait_ge(stored[par], 16 * u)
                pool.sem_inc(out_free[par], 1)

            gather(0, 1, 0)
            n = each_block(pool, gather_next, scatter)
            pool.wait_ge(x_loaded[0], n // 2 * 16 + 16)
            pool.wait_ge(x_loaded[1], (n + 1) // 2 * 16)

        @block.tensor
        def _(pe):
            def transpose_rows(par, u):
                pe.wait_ge(x_loaded[par], 16 * u)
                for k in range(KD):
                    ins = nc.tensor.transpose(PS[k // 4][:, (k % 4) * P:(k % 4 + 1) * P], x[par][:, k * P:(k + 1) * P], C["ident"])
                ins.then_inc(tp_done[par], 1)

            def gate_and_up(par, u, u_next, b):
                pe.wait_ge(xT_act[par], u)
                pe.wait_ge(xT_dve[par], u)
                pe.wait_ge(gu_loaded[par], 32 * u)
                for w, bank in ((wg, 2), (wu, 3)):
                    for k in range(KD):
                        ins = nc.tensor.matmul(PS[bank][:, :], xT[par][:, k, :], w[par][:, k, :], start=(k == 0), stop=(k == KD - 1))
                ins.then_inc(gu_done[par], 1)

            def down(par, u):
                pe.wait_ge(aT_done[par], u)
                pe.wait_ge(d_loaded[par], 16 * u)
                pe.wait_ge(out_act[1 - par], u + par)
                pe.wait_ge(out_dve[1 - par], u + par)
                for half in range(2):
                    for k in range(4):
                        ins = nc.tensor.matmul(PS[5 + half][:, :], aT[:, k, :], wd[par][:, k, 512 * half:512 * half + 512], start=(k == 0), stop=(k == 3))
                ins.then_inc(down_done[par], 1)

            def transposes(par, u, u_next):
                transpose_rows(1 - par, u_next)
                pe.wait_ge(a_done[par], u)
                for k in range(4):
                    ins = nc.tensor.transpose(PS[4][:, k * P:(k + 1) * P], a[:, k * P:(k + 1) * P], C["ident"])
                ins.then_inc(atp_done[par], 1)

            pe.wait_ge(slots_float, 1)
            for c in range(2):
                ins = nc.tensor.transpose(PS[7][:, 64 * c:64 * c + NB], rawf[:, c, :], C["ident"][0:NB, 0:NB])
            ins.then_inc(slots_tp, 1)
            transpose_rows(0, 1)
            each_block(pe, gate_and_up, down, transposes)

        @block.scalar
        def _(act):
            def copy_rows(par, u):
                act.wait_ge(tp_done[par], u + 1)
                nc.scalar.copy(xT[par][:, 0:4, :], PS[0][:, :].rearrange("p (k n) -> p k n", k=4)).then_inc(xT_act[par], 1)

            def silu(par, u, u_next, b):
                act.wait_ge(gu_done[par], u + 1)
                nc.scalar.activation(sg[:, :], PS[2][:, :], ACT.Silu).then_inc(silu_done[par], 1)

            def copy_out(par, u):
                act.wait_ge(out_free[par], u)
                act.wait_ge(down_done[par], u + 1)
                nc.scalar.copy(out[par][:, 0:512], PS[5][:, :]).then_inc(out_act[par], 1)

            copy_rows(0, 1)
            each_block(act, silu, copy_out, lambda par, u, u_next: copy_rows(1 - par, u_next))

        @block.vector
        def _(dve):
            def copy_rows(par, u):
                dve.wait_ge(tp_done[par], u + 1)
                nc.vector.tensor_copy(xT[par][:, 4:8, :], PS[1][:, :].rearrange("p (k n) -> p k n", k=4)).then_inc(xT_dve[par], 1)

            def times_up(par, u, u_next, b):
                dve.wait_ge(silu_done[par], u)
                nc.vector.tensor_tensor(a[:, :], sg[:, :], PS[3][:, :], ALU.mult).then_inc(a_done[par], 1)

            def copy_out(par, u):
                dve.wait_ge(out_free[par], u)
                dve.wait_ge(down_done[par], u + 1)
                nc.vector.tensor_copy(out[par][:, 512:1024], PS[6][:, :]).then_inc(out_dve[par], 1)

            def copies(par, u, u_next):
                copy_rows(1 - par, u_next)
                dve.wait_ge(atp_done[par], u)
                nc.vector.tensor_copy(aT[:, :, :], PS[4][:, :].rearrange("p (k n) -> p k n", k=4)).then_inc(aT_done[par], 1)

            dve.wait_ge(slots_loaded, 16)
            nc.vector.tensor_copy(rawf[:, :, :], raw[:, :, :].rearrange("b p c -> b c p")).then_inc(slots_float, 1)
            dve.wait_ge(slots_tp, 1)
            for c in range(2):
                nc.vector.tensor_copy(tokens[:, :, c], PS[7][:, 64 * c:64 * c + NB]).then_inc(slots_ready, 1)
            copy_rows(0, 1)
            each_block(dve, times_up, copy_out, copies)


def block_combine(nc, L, C, weight, x1, expert_out, y_p, y_s):
    ctx = ExitStack()
    with ctx:
        sem = L.signals.named("z_")
        got = [sem(f"got{i}") for i in range(3)]
        stored = [sem("stored0"), sem("stored1")]
        y_done, step_sem = sem("y_done"), sem("step")
        T = Region(L, A_HT, A_CONST)
        r = [T(f"z_r{i}", [P, 2, D]) for i in range(3)]
        tiles = [(t, P) for t in range(NT)] + [(NT, TS)]
        rows = expert_out[0:2 * TT].rearrange("(k t) n -> t k n", k=2)
        block = ctx.enter_context(nc.Block())

        @block.scalar
        def _(act):
            for t, n in tiles:
                if t >= 3:
                    act.wait_ge(y_done, t - 2)
                act.dma_start(r[t % 3][0:n, :, :], rows[t * P:t * P + n]).then_inc(got[t % 3], 16)

        @block.vector
        def _(dve):
            step = Steps(dve, step_sem)
            for t, n in tiles:
                dve.wait_ge(got[t % 3], 16 * (t // 3 + 1))
                x = x1[0:n, t, :]
                step(nc.vector.scalar_tensor_tensor(x, r[t % 3][0:n, 0, :], weight[0:n, t, 0:1], x, ALU.mult, ALU.add))
                nc.vector.scalar_tensor_tensor(x, r[t % 3][0:n, 1, :], weight[0:n, t, 1:2], x, ALU.mult, ALU.add).then_inc(y_done, 1)

        @block.sync
        def _(sp):
            for t, n in tiles:
                sp.wait_ge(y_done, t + 1)
                dst = y_p[0, t * P:(t + 1) * P, :] if t < NT else y_s[:, 0, :]
                sp.dma_start(dst, x1[0:n, t, :]).then_inc(stored[t % 2], 16)
            sp.wait_ge(stored[0], 16 * 5)
            sp.wait_ge(stored[1], 16 * 4)


def load_constants(nc, L, table):
    t = L.at("constants", A_CONST, [P, CONST.shape[1]])
    with nc.semaphore("constants_loaded") as loaded, nc.Block() as block:
        @block.sync
        def _(sp):
            sp.dma_start(t[:, :], table).then_inc(loaded, 16)
            sp.wait_ge(loaded, 16)
    return {name: t[:, a:a + n] for name, (a, n) in WHERE.items()}


def build(nc, I, O):
    L = Layout(nc)
    whole = nc.alloc_psum_tensor("psum", [P, 4096], F32)
    PS = [whole[:, 512 * i:512 * i + 512] for i in range(8)] + [whole[:, :]]
    C = load_constants(nc, L, I["shape_constants"])
    hT = L.at("hT", A_HT, [P, KD, TT])
    R = L.at("R", A_R, [P, NT, RW])
    Rs = L.at("Rs", A_RS, [TS, RW])
    block_norm(nc, L, PS, C, I["x_prompt"], I["x_sample"], I["norm_mix"][0], hT)
    dnT = L.at("dnT", A_DN, [P, 12, TT])
    block_project(nc, L, PS, C, I["w_in"][0], hT, R, Rs, dnT)
    obT = L.at("obT", A_OB, [P, DH, TT])
    convT = L.at("convT", A_FREE + 18432, [P, 12, 4 + 3 * TS])
    ab_p = L.at("ab_p", A_END - 512, [P, NT, 8])
    ab_s = L.at("ab_s", A_END - 256, [TS, 1, 8])
    Os = L.at("Os", A_FREE + 14336, [TS, DW])
    block_conv(nc, L, PS, C, I["state_dn_conv"][0], I["dn_conv_w"][0], dnT, convT, O["conv_prompt"][0, 0], O["conv_sample"][0])
    block_decays(nc, L, PS, C, I["dn_A_log"][0], I["dn_dt_bias"][0], R, Rs, ab_p, ab_s)
    block_delta(nc, L, PS, C, dnT, ab_p, O["S_prompt"][0, 0])
    block_delta_sample(nc, L, PS, C, I["state_dn_S"][0], dnT, ab_s, Os, O["S_sample"][0])
    block_delta_gate(nc, L, PS, C, dnT, Os, R, Rs, I["dn_norm"][0], obT)
    L.signals.renew()
    S = Region(L, A_SMALL, A_END)
    gates_p, gates_s = S("gates_p", [P, NT, 24]), S("gates_s", [TS, 24])
    cpos, kv_cmp, kcT = S("cpos", [P, 2, P]), S("kv_cmp", [64, 2, P]), S("kcT", [P, 1, 64])
    qT, kT = L.at("qT", A_QT, [P, 4, TT]), L.at("kT", A_KT, [P, 4, TT])
    oaT = L.at("oaT", A_OA, [P, 4, TT])
    rows = lambda ap: ap.rearrange("b t i g d -> b t (i g d)")
    block_qk(nc, L, PS, C, I["q_norm"][0], I["k_norm"][0], rows(I["state_win"][0]), R, Rs, gates_p, gates_s, qT, kT,
             rows(O["kv_prompt"][0])[0], rows(O["kv_sample"][0])[:, 0], rows(O["win_prompt"][0])[0], rows(O["win_sample"][0]))
    block_compress_prompt(nc, L, PS, C, I["cmp_pos"][0], I["w_cmp"][0], kT, cpos, kv_cmp)
    block_cmp_norm(nc, L, PS, C, I["k_norm"][0, 2], NCP, 1, kv_cmp[0:NCP, 0:1, :], kcT, A_FREE, A_SMALL)
    block_attend_prompt(nc, L, PS, C, qT, kT, kcT, kv_cmp, R, gates_p, oaT)
    L.signals.renew()
    Z = Region(L, A_FREE, A_SMALL)
    kcs, vcs, kcsT, qbd = Z("kcs", [P, TS, P]), Z("vcs", [P, TS, P]), Z("kcsT", [P, TS, P]), Z("qbd", [P, TS, 64])
    snew, g64 = Z("snew", [64, 2]), Z("g64", [64, 3])
    pages = Z("pages", [1, TS * NPAGE], I32)
    sw = L.at("sw", A_OA - 2080, [64, WIN + 1])
    block_window_keys(nc, L, PS, C, rows(I["state_win"][0]), I["page_table"], qT, kT, gates_s, qbd, snew, g64, pages, sw)
    cache = I["cache_nsa"][0].rearrange("n t i g d -> n t (i g d)")
    block_cache_keys(nc, L, PS, C, cache, pages, I["w_cmp"][0], cpos, qbd, kcs, vcs)
    block_cmp_norm(nc, L, PS, C, I["k_norm"][0, 2], NCS, TS, kcs[0:NCS, :, :], kcsT, A_R, A_RS, 4)
    block_attend_sample(nc, L, PS, C, cache, pages, rows(I["state_win"][0]), kcsT, vcs, qbd, snew, g64, sw, Rs, oaT)
    L.signals.renew()
    lo, hi = L.at("mixed_lo", A_R + 41856, [P, 4, TT]), L.at("mixed_hi", A_FREE, [P, 4, TT])
    mixed = [(lo, hi)[m // 4][:, m % 4, :] for m in range(KD)]
    block_merge(nc, L, PS, C, I["w_in"][0], I["w_proj_a"][0], I["w_proj_b"][0], hT, oaT, obT, mixed)
    K = Region(L, A_OB, A_R)
    logits, slot, weight, blocks = K("logits", [P, NT + 1, NG + NE]), K("slot", [P, NT + 1, 2], I32), K("weight", [P, NT + 1, 2]), K("blocks", [1, 64], I32)
    x1 = L.at("x1", A_R, [P, NT + 1, D])
    h2_rows = nc.dram_tensor("h2_rows", [TT + 1, D], F32, kind="Internal").ap()
    table = nc.dram_tensor("slot_tokens", [(MAXBLK + 2) * P, 2], I32, kind="Internal").ap()
    expert_out = nc.dram_tensor("expert_out", [2 * TT + 1, D], F32, kind="Internal").ap()
    block_out(nc, L, PS, C, I["x_prompt"], I["x_sample"], I["w_out"][0], I["norm_ffn"][0], I["w_router_g"][0], I["w_router_e"][0],
              I["b_router_g"][0], I["b_router_e"][0], mixed, x1, h2_rows, logits)
    weights = expert_weights(L, I["w_gate"][0], I["w_up"][0], I["w_down"][0])
    block_route(nc, L, PS, C, logits, slot, weight, blocks, table, weights)
    block_experts(nc, L, PS, C, weights, h2_rows, table, blocks, expert_out)
    block_combine(nc, L, C, weight, x1, expert_out, O["y_prompt"], O["y_sample"])

_INS = ["x_prompt", "x_sample", "cache_nsa", "page_table", "state_win", "state_dn_conv", "state_dn_S",
        "norm_mix", "w_in", "q_norm", "k_norm", "cmp_pos", "w_cmp", "dn_conv_w", "dn_A_log", "dn_dt_bias", "dn_norm",
        "w_proj_a", "w_proj_b", "w_out", "norm_ffn", "w_router_g", "b_router_g", "w_router_e", "b_router_e",
        "w_gate", "w_up", "w_down"]
_OUTS = [("y_prompt", (1, TP, D)), ("y_sample", (TS, 1, D)), ("kv_prompt", (1, 1, TP, 4, NKV, HD)), ("kv_sample", (1, TS, 1, 4, NKV, HD)),
         ("win_prompt", (1, 1, WIN, 2, NKV, HD)), ("win_sample", (1, TS, WIN, 2, NKV, HD)),
         ("conv_prompt", (1, 1, 3, 3 * DW)), ("conv_sample", (1, TS, 3, 3 * DW)),
         ("S_prompt", (1, 1, DH, DD, DD)), ("S_sample", (1, TS, DH, DD, DD))]


def kernel(**inputs):
    import concourse.bacc as bacc
    from concourse.bass_utils import run_bass_kernel_spmd

    nc = bacc.Bacc("TRN2", target_bir_lowering=False, num_devices=1)
    arrays = {name: np.ascontiguousarray(inputs[name]) for name in _INS}
    arrays["shape_constants"] = CONST
    ins = {n: nc.dram_tensor(n, a.shape, mybir.dt.from_np(a.dtype), kind="ExternalInput").ap() for n, a in arrays.items()}
    outs = {n: nc.dram_tensor("out_" + n, shape, F32, kind="ExternalOutput").ap() for n, shape in _OUTS}
    build(nc, ins, outs)
    r = run_bass_kernel_spmd(nc, [arrays], core_ids=[0])
    return tuple(r.results[0]["out_" + n] for n, _ in _OUTS)
```
